# Optimizing a Trainium2 kernel written in Bass

```python
import math
import jax, jax.numpy as jnp
from jax import lax
import numpy as np

D_MODEL = 1024
BATCH = 1
SEQ = 1024
DEPTH = 1

D_FF = 2816
RMS_EPS = 1e-6
SUBLN_EPS = 1e-5
CONV_WIDTH = 4
DN_HEADS = 8
DN_HEAD_DIM = 64
DN_WIDTH = DN_HEADS * DN_HEAD_DIM
DN_CHUNK = 64
DIFF_HEADS = 4
DIFF_HEAD_DIM = 64
DIFF_V_DIM = 2 * DIFF_HEAD_DIM
DIFF_QK_WIDTH = DIFF_HEADS * 2 * DIFF_HEAD_DIM
DIFF_V_WIDTH = DIFF_HEADS * DIFF_V_DIM
Q_BLOCK = 128
N_BRANCHES = 2
IN_SPLIT_SIZES = (3 * DN_WIDTH, DN_WIDTH, DN_HEADS, DN_HEADS, DIFF_QK_WIDTH, DIFF_QK_WIDTH, DIFF_V_WIDTH, N_BRANCHES * D_MODEL)
W_IN_COLS = sum(IN_SPLIT_SIZES)

kernel_name = "hybrid_gdn_diffattn_macaron"

def lambda_init(layer_idx):
    return 0.8 - 0.6 * math.exp(-0.3 * layer_idx)

def rms_norm(x, g, eps=RMS_EPS):
    xf = x.astype(jnp.float32)
    y = xf * lax.rsqrt(jnp.mean(xf * xf, axis=-1, keepdims=True) + eps)
    return (y * g.astype(jnp.float32)).astype(x.dtype)

def l2_normalize(x, eps=1e-6):
    xf = x.astype(jnp.float32)
    return xf * lax.rsqrt(jnp.sum(xf * xf, axis=-1, keepdims=True) + eps)

def swiglu_ffn(x, w_gate, w_up, w_down):
    return (jax.nn.silu(x @ w_gate) * (x @ w_up)) @ w_down

def causal_depthwise_conv(x, w):
    width = w.shape[0]
    return lax.conv_general_dilated(
        x, w[:, None, :], window_strides=(1,), padding=[(width - 1, 0)],
        dimension_numbers=('NWC', 'WIO', 'NWC'), feature_group_count=x.shape[-1])

def gated_delta_rule_chunked(q, k, v, g, beta):
    B, H, T, dk = q.shape
    dv = v.shape[-1]
    C = DN_CHUNK
    N = T // C
    f32 = jnp.float32
    q = (q.astype(f32) * dk ** -0.5).reshape(B, H, N, C, dk)
    k = k.astype(f32).reshape(B, H, N, C, dk)
    v = v.astype(f32).reshape(B, H, N, C, dv)
    g = g.astype(f32).reshape(B, H, N, C)
    beta = beta.astype(f32).reshape(B, H, N, C)
    gc = jnp.cumsum(g, axis=-1)
    incl = jnp.tril(jnp.ones((C, C), dtype=bool))
    strict = jnp.tril(jnp.ones((C, C), dtype=bool), k=-1)
    rel = gc[..., :, None] - gc[..., None, :]
    decay = jnp.where(incl, jnp.exp(jnp.where(incl, rel, 0.0)), 0.0)
    kb = k * beta[..., None]
    a_strict = jnp.where(strict, jnp.einsum('bhncd,bhnsd->bhncs', kb, k) * decay, 0.0)
    eye = jnp.eye(C, dtype=f32)
    t_inv = lax.linalg.triangular_solve(eye + a_strict, jnp.broadcast_to(eye, a_strict.shape),
                                        left_side=True, lower=True, unit_diagonal=True)
    u = jnp.einsum('bhncs,bhnse->bhnce', t_inv, v * beta[..., None])
    w = jnp.einsum('bhncs,bhnsd->bhncd', t_inv, kb * jnp.exp(gc)[..., None])
    attn = jnp.einsum('bhncd,bhnsd->bhncs', q, k) * decay
    q_dec = q * jnp.exp(gc)[..., None]
    k_dec = k * jnp.exp(gc[..., -1:] - gc)[..., None]
    chunk_decay = jnp.exp(gc[..., -1])

    def step(state, xs):
        u_n, w_n, q_n, k_n, attn_n, cd_n = xs
        v_new = u_n - jnp.einsum('bhcd,bhde->bhce', w_n, state)
        o_n = jnp.einsum('bhcd,bhde->bhce', q_n, state) + jnp.einsum('bhcs,bhse->bhce', attn_n, v_new)
        state = state * cd_n[..., None, None] + jnp.einsum('bhcd,bhce->bhde', k_n, v_new)
        return state, o_n

    def to_front(t):
        return jnp.moveaxis(t, 2, 0)

    s0 = jnp.zeros((B, H, dk, dv), f32)
    _, o = lax.scan(step, s0, (to_front(u), to_front(w), to_front(q_dec), to_front(k_dec),
                               to_front(attn), to_front(chunk_decay)))
    return jnp.moveaxis(o, 0, 2).reshape(B, H, T, dv)

def differential_attention(q1, q2, k1, k2, v, lam, slopes):
    B, H, T, d = q1.shape
    nb = T // Q_BLOCK
    f32 = jnp.float32
    scale = d ** -0.5
    k1f, k2f, vf = k1.astype(f32), k2.astype(f32), v.astype(f32)
    kpos = jnp.arange(T, dtype=jnp.int32)

    def probs(qb, kf, bias, causal):
        s = jnp.einsum('bhqd,bhkd->bhqk', qb, kf) * scale + bias
        s = jnp.where(causal, s, -jnp.inf)
        return jax.nn.softmax(s, axis=-1)

    def block(args):
        q1b, q2b, start = args
        qpos = start + jnp.arange(Q_BLOCK, dtype=jnp.int32)
        dist = qpos[:, None] - kpos[None, :]
        causal = dist >= 0
        bias = -slopes[:, None, None] * dist.astype(f32)[None]
        p = probs(q1b.astype(f32), k1f, bias, causal) - lam * probs(q2b.astype(f32), k2f, bias, causal)
        return jnp.einsum('bhqk,bhke->bhqe', p, vf)

    def to_blocks(t):
        return t.reshape(B, H, nb, Q_BLOCK, d).transpose(2, 0, 1, 3, 4)

    starts = jnp.arange(nb, dtype=jnp.int32) * Q_BLOCK
    out = lax.map(block, (to_blocks(q1), to_blocks(q2), starts))
    return out.transpose(1, 2, 0, 3, 4).reshape(B, H, T, v.shape[-1])

def setup_inputs(seed: int = 0) -> dict:
    key = jax.random.key(seed)
    ks = jax.random.split(key, 24)
    f32 = jnp.float32
    L = DEPTH

    def normal(k, shape, fan_in):
        return jax.random.normal(k, shape, f32) * fan_in ** -0.5

    def gain(k, shape):
        return 1.0 + 0.02 * jax.random.normal(k, shape, f32)

    x = jax.random.normal(ks[0], (BATCH, SEQ, D_MODEL), f32)
    ffn1_norm = gain(ks[1], (L, D_MODEL))
    ffn1_w_gate = normal(ks[2], (L, D_MODEL, D_FF), D_MODEL)
    ffn1_w_up = normal(ks[3], (L, D_MODEL, D_FF), D_MODEL)
    ffn1_w_down = normal(ks[4], (L, D_FF, D_MODEL), D_FF)
    mix_norm = gain(ks[5], (L, D_MODEL))
    w_in = normal(ks[6], (L, D_MODEL, W_IN_COLS), D_MODEL)
    conv_qkv = normal(ks[7], (L, CONV_WIDTH, 3 * DN_WIDTH), CONV_WIDTH)
    dn_a_log = jnp.log(jax.random.uniform(ks[8], (L, DN_HEADS), f32, 1.0, 16.0))
    dt = jnp.exp(jax.random.uniform(ks[9], (L, DN_HEADS), f32, math.log(1e-3), math.log(1e-1)))
    dn_dt_bias = dt + jnp.log(-jnp.expm1(-dt))
    dn_out_norm = gain(ks[10], (L, DN_HEAD_DIM))
    diff_lambda_q1 = 0.1 * jax.random.normal(ks[11], (L, DIFF_HEAD_DIM), f32)
    diff_lambda_k1 = 0.1 * jax.random.normal(ks[12], (L, DIFF_HEAD_DIM), f32)
    diff_lambda_q2 = 0.1 * jax.random.normal(ks[13], (L, DIFF_HEAD_DIM), f32)
    diff_lambda_k2 = 0.1 * jax.random.normal(ks[14], (L, DIFF_HEAD_DIM), f32)
    diff_subln = gain(ks[15], (L, DIFF_V_DIM))
    w_branch_a = normal(ks[16], (L, DN_WIDTH, D_MODEL), DN_WIDTH)
    w_branch_b = normal(ks[17], (L, DIFF_V_WIDTH, D_MODEL), DIFF_V_WIDTH)
    w_out = normal(ks[18], (L, D_MODEL, D_MODEL), D_MODEL)
    ffn2_norm = gain(ks[19], (L, D_MODEL))
    ffn2_w_gate = normal(ks[20], (L, D_MODEL, D_FF), D_MODEL)
    ffn2_w_up = normal(ks[21], (L, D_MODEL, D_FF), D_MODEL)
    ffn2_w_down = normal(ks[22], (L, D_FF, D_MODEL), D_FF)
    final_norm = gain(ks[23], (D_MODEL,))
    return {"x": x, "ffn1_norm": ffn1_norm, "ffn1_w_gate": ffn1_w_gate, "ffn1_w_up": ffn1_w_up,
            "ffn1_w_down": ffn1_w_down, "mix_norm": mix_norm, "w_in": w_in, "conv_qkv": conv_qkv,
            "dn_a_log": dn_a_log, "dn_dt_bias": dn_dt_bias, "dn_out_norm": dn_out_norm,
            "diff_lambda_q1": diff_lambda_q1, "diff_lambda_k1": diff_lambda_k1,
            "diff_lambda_q2": diff_lambda_q2, "diff_lambda_k2": diff_lambda_k2, "diff_subln": diff_subln,
            "w_branch_a": w_branch_a, "w_branch_b": w_branch_b, "w_out": w_out,
            "ffn2_norm": ffn2_norm, "ffn2_w_gate": ffn2_w_gate, "ffn2_w_up": ffn2_w_up,
            "ffn2_w_down": ffn2_w_down, "final_norm": final_norm}

def reference(x, ffn1_norm, ffn1_w_gate, ffn1_w_up, ffn1_w_down, mix_norm, w_in, conv_qkv,
              dn_a_log, dn_dt_bias, dn_out_norm, diff_lambda_q1, diff_lambda_k1, diff_lambda_q2,
              diff_lambda_k2, diff_subln, w_branch_a, w_branch_b, w_out, ffn2_norm, ffn2_w_gate,
              ffn2_w_up, ffn2_w_down, final_norm):
    B, T, _ = x.shape
    f32 = jnp.float32
    split_points = [int(s) for s in np.cumsum(IN_SPLIT_SIZES)[:-1]]
    slopes = jnp.asarray([2.0 ** (-8.0 * (i + 1) / DIFF_HEADS) for i in range(DIFF_HEADS)], f32)

    for l in range(DEPTH):
        x = x + 0.5 * swiglu_ffn(rms_norm(x, ffn1_norm[l]), ffn1_w_gate[l], ffn1_w_up[l], ffn1_w_down[l])

        h = rms_norm(x, mix_norm[l])
        proj = h @ w_in[l]
        qkv_dn, z_dn, a_dn, b_dn, q_df, k_df, v_df, gate_logits = jnp.split(proj, split_points, axis=-1)

        qkv_dn = jax.nn.silu(causal_depthwise_conv(qkv_dn, conv_qkv[l]))
        q_dn, k_dn, v_dn = jnp.split(qkv_dn, 3, axis=-1)

        def dn_heads(t):
            return t.reshape(B, T, DN_HEADS, DN_HEAD_DIM).transpose(0, 2, 1, 3)

        q_dn = l2_normalize(dn_heads(q_dn))
        k_dn = l2_normalize(dn_heads(k_dn))
        v_dn = dn_heads(v_dn)
        g_dn = -jnp.exp(dn_a_log[l].astype(f32)) * jax.nn.softplus(a_dn.astype(f32) + dn_dt_bias[l].astype(f32))
        beta_dn = jax.nn.sigmoid(b_dn.astype(f32))
        o_dn = gated_delta_rule_chunked(q_dn, k_dn, v_dn, g_dn.transpose(0, 2, 1), beta_dn.transpose(0, 2, 1))
        o_dn = o_dn.transpose(0, 2, 1, 3).astype(x.dtype)
        o_dn = rms_norm(o_dn, dn_out_norm[l]) * jax.nn.silu(z_dn.reshape(B, T, DN_HEADS, DN_HEAD_DIM))
        y_a = o_dn.reshape(B, T, DN_WIDTH) @ w_branch_a[l]

        q_df = q_df.reshape(B, T, DIFF_HEADS, 2, DIFF_HEAD_DIM).transpose(3, 0, 2, 1, 4)
        k_df = k_df.reshape(B, T, DIFF_HEADS, 2, DIFF_HEAD_DIM).transpose(3, 0, 2, 1, 4)
        v_df = v_df.reshape(B, T, DIFF_HEADS, DIFF_V_DIM).transpose(0, 2, 1, 3)
        lam_init = lambda_init(l)
        lam = (jnp.exp(jnp.sum(diff_lambda_q1[l].astype(f32) * diff_lambda_k1[l].astype(f32)))
               - jnp.exp(jnp.sum(diff_lambda_q2[l].astype(f32) * diff_lambda_k2[l].astype(f32)))
               + lam_init)
        o_df = differential_attention(q_df[0], q_df[1], k_df[0], k_df[1], v_df, lam, slopes)
        o_df = o_df.transpose(0, 2, 1, 3).astype(x.dtype)
        o_df = rms_norm(o_df, diff_subln[l], eps=SUBLN_EPS) * (1.0 - lam_init)
        y_b = o_df.reshape(B, T, DIFF_V_WIDTH) @ w_branch_b[l]

        gate_a, gate_b = jnp.split(jax.nn.sigmoid(gate_logits), 2, axis=-1)
        x = x + (gate_a * y_a + gate_b * y_b) @ w_out[l]

        x = x + 0.5 * swiglu_ffn(rms_norm(x, ffn2_norm[l]), ffn2_w_gate[l], ffn2_w_up[l], ffn2_w_down[l])

    return rms_norm(x, final_norm)


_drawn_inputs = setup_inputs


def setup_inputs(seed=0):
    import zlib

    import numpy as np

    out = dict(_drawn_inputs(seed))
    spreads = {}
    factors = {'ffn1_norm': 5.104,
     'mix_norm': 3.079,
     'dn_out_norm': 76.267,
     'diff_lambda_k2': 3.922,
     'diff_subln': 200.0,
     'ffn2_norm': 33.674,
     'final_norm': 24.497,
     'diff_lambda_k1': 3.711}
    for name, (base, spread) in spreads.items():
        noise = np.random.default_rng([zlib.crc32(name.encode()), seed]).standard_normal(out[name].shape)
        drawn = base * np.exp(spread * noise) if base else spread * noise
        out[name] = __import__('jax').numpy.asarray(drawn.astype(out[name].dtype))
    for name, factor in factors.items():
        out[name] = (out[name] * factor).astype(out[name].dtype)
    return out
```

```python
from contextlib import ExitStack

import concourse.bass as bass
from concourse import mybir

F32 = mybir.dt.float32
F32R = mybir.dt.float32r
ACT = mybir.ActivationFunctionType
ALU = mybir.AluOpType
AX_X = mybir.AxisListType.X

P = 128
D_MODEL = 1024
T = 1024
DC = D_MODEL // P
HALF = 512
NH = T // HALF
D_FF = 2816
FC = D_FF // P
HD = 64
DN_HEADS = 8
HP = DN_HEADS // 2
DN_W = DN_HEADS * HD
CH = 64
NCH = T // CH
DF_HEADS = 4
CONV = 4
RMS_EPS = 1e-6
SUBLN_EPS = 1e-5
L2_EPS = 1e-6
LAM_INIT = 0.8 - 0.6
OFF_Z = 3 * DN_W
OFF_AB = OFF_Z + DN_W
OFF_Q = OFF_AB + 2 * DN_HEADS
OFF_K = OFF_Q + DF_HEADS * P
OFF_V = OFF_K + DF_HEADS * P
OFF_G = OFF_V + DF_HEADS * P
NEG = -3.0e38
BETA_ROW = 32


class Core:

    def __init__(self, nc, ctx):
        self.nc = nc
        self.ctx = ctx
        self.n = 0
        self.sems = []

    def sb(self, ctx, name, shape, dt=F32):
        self.n += 1
        return ctx.enter_context(self.nc.sbuf_tensor(f"{name}_{self.n}", shape, dt))

    def sb_shared(self, ctx, name, shape):
        split = self.sb(ctx, f"{name}_hi", shape, F32R)
        size = 4
        for s in shape[1:]:
            size *= s
        return split, self.nc.alloc_sbuf_tensor_at(f"{name}_raw_{self.n}", shape, F32,
                                                   offset=self.nc.sbuf_base - size)

    def ps(self, ctx, name, shape):
        self.n += 1
        return ctx.enter_context(self.nc.psum_tensor(f"{name}_{self.n}", shape, F32))

    def sem(self, name):
        self.n += 1
        self.sems.append(self.nc.alloc_semaphore(name=f"{name}_{self.n}"))
        return self.sems[-1]

    def end_phase(self):
        self.nc.clear_and_free_semaphores(self.sems)
        self.nc.all_engine_barrier()
        self.sems = []


def three_pass(pe, banks, w_hi, w_lo, x_hi, x_lo, start, stop):
    for h, bank in enumerate(banks):
        pe.matmul(bank, w_hi, x_hi[:, h * HALF:(h + 1) * HALF], start=start, stop=False)
    for h, bank in enumerate(banks):
        pe.matmul(bank, w_hi, x_lo[:, h * HALF:(h + 1) * HALF], start=False, stop=False)
    for h, bank in enumerate(banks):
        last = pe.matmul(bank, w_lo, x_hi[:, h * HALF:(h + 1) * HALF], start=False, stop=stop)
    return last


class Ring:

    def __init__(self, core, ctx, depth):
        self.depth = depth
        self.raw = core.sb(ctx, "w_raw", [P, depth, DC, P])
        self.hi = core.sb(ctx, "w_hi", [P, depth, DC, P], F32R)
        self.lo = core.sb(ctx, "w_lo", [P, depth, DC, P], F32R)
        self.landed = [core.sem(f"w_landed{s}") for s in range(depth)]
        self.hi_made = core.sem("w_hi_made")
        self.lo_made = core.sem("w_lo_made")


def setup_phase(core, a):
    nc = core.nc
    c = core
    per = core.ctx
    c.xT = c.sb(per, "xT", [P, DC, T])
    c.n_hi = c.sb(per, "n_hi", [P, DC, T], F32R)
    c.n_lo = c.sb(per, "n_lo", [P, DC, T], F32R)
    c.ident = c.sb(per, "ident", [P, P])
    c.ones = c.sb(per, "ones", [P, P])
    c.head_ones = c.sb(per, "head_ones", [P, P])
    c.ident2 = c.sb(per, "ident2", [P, CH])
    c.gains = c.sb(per, "gains", [P, 4, DC])
    c.eps = c.sb(per, "eps", [P, 2])

    gains_in = c.sem("gains_loaded")
    zeroed = c.sem("consts_zeroed")
    made = c.sem("consts_made")
    turned = c.sem("x_turned")
    taken = c.sem("x_taken")
    with ExitStack() as ctx:
        xin = c.sb(ctx, "x_in", [P, 2, D_MODEL])
        xps = c.ps(ctx, "x_ps", [P, 4, HALF])
        slot_in = [c.sem("x_in_slot0"), c.sem("x_in_slot1")]
        block = ctx.enter_context(nc.Block())
        xrows = a["x"].rearrange("b (t p) d -> (b t) p d", p=P)

        @block.sync
        def _(sp):
            for i, name in enumerate(("ffn1_norm", "mix_norm", "ffn2_norm")):
                sp.dma_start(c.gains[:, i, :], a[name].rearrange("l (c p) -> p (l c)", p=P),
                             allow_slow_non_contiguous=True).then_inc(gains_in, 16)
            sp.dma_start(c.gains[:, 3, :], a["final_norm"].rearrange("(c p) -> p c", p=P),
                             allow_slow_non_contiguous=True).then_inc(gains_in, 16)
            for t in range(T // P):
                if t >= 2:
                    sp.wait_ge(turned, 2 * (t - 1))
                sp.dma_start(xin[:, t % 2, :], xrows[t]).then_inc(slot_in[t % 2], 16)
            sp.wait_ge(gains_in, 64)

        @block.gpsimd
        def _(pool):
            pool.memset(c.ident[:], 0.0).then_inc(zeroed, 1)
            pool.memset(c.ones[:], 1.0).then_inc(zeroed, 1)
            pool.memset(c.eps[:, 0:1], RMS_EPS).then_inc(zeroed, 1)
            pool.memset(c.eps[:, 1:2], SUBLN_EPS).then_inc(zeroed, 1)
            pool.memset(c.head_ones[:], 0.0).then_inc(zeroed, 1)
            pool.wait_ge(zeroed, 5)
            pool.affine_select(out=c.ident[:], in_=c.ident[:], compare_op=ALU.not_equal, fill=1.0, base=0,
                               pattern=[[-1, P]], channel_multiplier=1).then_inc(made, 1)

        @block.tensor
        def _(pe):
            pe.wait_ge(made, 1)
            for t in range(T // P):
                pe.wait_ge(slot_in[t % 2], 16 * (t // 2 + 1))
                for g in range(2):
                    k = 2 * t + g
                    if k >= 4:
                        pe.wait_ge(taken, k - 3)
                    for j in range(4):
                        d = 4 * g + j
                        last = pe.transpose(xps[:, k % 4, j * P:(j + 1) * P],
                                            xin[:, t % 2, d * P:(d + 1) * P], c.ident[:])
                    last.then_inc(turned, 1)

        @block.vector
        def _(dve):
            dve.wait_ge(zeroed, 5)
            for h in range(2):
                dve.memset(c.head_ones[h * HD:(h + 1) * HD, h * HD:(h + 1) * HD], 1.0)
            dve.wait_ge(made, 1)
            dve.tensor_tensor(c.ident2[:], c.ident[:, 0:CH], c.ident[:, CH:P], ALU.add)
            for t in range(T // P):
                for g in range(2):
                    k = 2 * t + g
                    dve.wait_ge(turned, k + 1)
                    dve.tensor_copy(c.xT[:, 4 * g:4 * g + 4, t * P:(t + 1) * P],
                                    xps[:, k % 4, :].rearrange("p (j q) -> p j q", j=4)).then_inc(taken, 1)


def norm_phase(core, which, out=None):
    nc, c = core.nc, core
    gain = c.gains[:, which, :]
    squared = c.sem("squared")
    summed = c.sem("summed")
    rooted = c.sem("rooted")
    inverted = c.sem("inverted")
    scaled = c.sem("scaled")
    hi_made = c.sem("n_hi_made")
    lo_made = c.sem("n_lo_made")
    turned = c.sem("y_turned")
    copied = c.sem("y_copied")
    with ExitStack() as ctx:
        sq = c.sb(ctx, "sq", [P, 2, T])
        rstd = c.sb(ctx, "rstd", [P, T])
        nrm = c.sb(ctx, "nrm", [P, 2 if out is None else DC, T])
        NB = 2 if out is None else DC
        ss = c.ps(ctx, "ss", [P, NH, HALF])
        if out is not None:
            y = c.sb(ctx, "y", [P, 2, D_MODEL])
            yps = c.ps(ctx, "yps", [P, 4, HALF])
            slot_out = [c.sem("y_out0"), c.sem("y_out1")]
        block = ctx.enter_context(nc.Block())

        @block.scalar
        def _(act):
            for k in range(DC):
                if k >= 2:
                    act.wait_ge(summed, k - 1)
                act.activation(sq[:, k % 2, :], c.xT[:, k, :], ACT.Square).then_inc(squared, 1)
            act.wait_ge(summed, DC)
            act.activation(rstd[:], ss[:].rearrange("p h t -> p (h t)"), ACT.Sqrt, scale=1.0 / D_MODEL,
                           bias=c.eps[:, 0:1]).then_inc(rooted, 1)
            if out is None:
                for k in range(DC):
                    act.wait_ge(scaled, k + 1)
                    act.activation(c.n_hi[:, k, :], nrm[:, k % NB, :], ACT.Copy).then_inc(hi_made, 1)

        @block.tensor
        def _(pe):
            for k in range(DC):
                pe.wait_ge(squared, k + 1)
                for h in range(NH):
                    last = pe.matmul(ss[:, h, :], c.ones[:], sq[:, k % 2, h * HALF:(h + 1) * HALF],
                                     start=(k == 0), stop=(k == DC - 1))
                last.then_inc(summed, 1)
            if out is not None:
                pe.wait_ge(scaled, DC)
                for t in range(T // P):
                    for g in range(2):
                        k = 2 * t + g
                        if k >= 4:
                            pe.wait_ge(copied, k - 3)
                        for j in range(4):
                            last = pe.transpose(yps[:, k % 4, j * P:(j + 1) * P],
                                                nrm[:, 4 * g + j, t * P:(t + 1) * P], c.ident[:])
                        last.then_inc(turned, 1)

        @block.vector
        def _(dve):
            dve.wait_ge(rooted, 1)
            dve.reciprocal(rstd[:], rstd[:]).then_inc(inverted, 1)
            dve.wait_ge(inverted, 1)
            for k in range(DC):
                if k >= NB:
                    dve.wait_ge(lo_made, k - NB + 1)
                dve.scalar_tensor_tensor(out=nrm[:, k % NB, :], in0=c.xT[:, k, :], scalar=gain[:, k:k + 1],
                                         in1=rstd[:], op0=ALU.mult, op1=ALU.mult).then_inc(scaled, 1)
                if out is None and k >= 1:
                    dve.wait_ge(hi_made, k)
                    dve.tensor_tensor(c.n_lo[:, k - 1, :], nrm[:, (k - 1) % NB, :], c.n_hi[:, k - 1, :].bitcast(F32),
                                      ALU.subtract).then_inc(lo_made, 1)
            if out is None:
                dve.wait_ge(hi_made, DC)
                dve.tensor_tensor(c.n_lo[:, DC - 1, :], nrm[:, (DC - 1) % NB, :],
                                  c.n_hi[:, DC - 1, :].bitcast(F32), ALU.subtract).then_inc(lo_made, 1)
            else:
                for t in range(T // P):
                    if t >= 2:
                        dve.wait_ge(slot_out[t % 2], 16 * (t // 2))
                    for g in range(2):
                        k = 2 * t + g
                        dve.wait_ge(turned, k + 1)
                        dve.tensor_copy(y[:, t % 2, g * HALF:(g + 1) * HALF], yps[:, k % 4, :]).then_inc(copied, 1)

        if out is not None:
            orow = out.rearrange("b (t p) d -> (b t) p d", p=P)

            @block.sync
            def _(sp):
                for t in range(T // P):
                    sp.wait_ge(copied, 2 * (t + 1))
                    sp.dma_start(orow[t], y[:, t % 2, :]).then_inc(slot_out[t % 2], 16)
                sp.wait_ge(slot_out[0], 16 * (T // P // 2))
                sp.wait_ge(slot_out[1], 16 * (T // P // 2))


def ffn_phase(core, w_gate, w_up, w_down):
    nc, c = core.nc, core
    PAIRS = FC // 2
    with ExitStack() as ctx:
        ring = Ring(c, ctx, 3)
        sg = c.sb(ctx, "silu_gate", [P, T])
        h_raw = c.sb(ctx, "h_raw", [P, 2, T])
        h_hi = c.sb(ctx, "h_hi", [P, 2, T], F32R)
        h_lo = c.sb(ctx, "h_lo", [P, 2, T], F32R)
        ps_g = c.ps(ctx, "ps_gate", [P, NH, HALF])
        ps_u = c.ps(ctx, "ps_up", [P, NH, HALF])
        ps_d = c.ps(ctx, "ps_down", [P, 2, NH, HALF])
        product_done = c.sem("product_done")
        silu_done = c.sem("silu_done")
        h_made = c.sem("h_made")
        h_hi_made = c.sem("h_hi_made")
        h_lo_made = c.sem("h_lo_made")
        down_done = c.sem("down_done")
        added = c.sem("added")
        block = ctx.enter_context(nc.Block())
        cols = lambda w: w.rearrange("l (k p) (f c) -> (l f) p k c", p=P, c=P)
        gate_t, up_t = cols(w_gate), cols(w_up)
        down_t = w_down.rearrange("l (f p) (k c) -> (l f) p k c", p=P, c=P)
        slot = lambda k: (k - 2) % 3
        rnd = lambda i, k: 2 * i + (k - 2) // 3
        tile = lambda i, k: 6 * i - 2 + k

        @block.sync
        def _(sp):
            def load(i, k, src, first=False):
                if not first:
                    sp.wait_ge(ring.lo_made, tile(i, k) - 2)
                sp.dma_start(ring.raw[:, slot(k)], src).then_inc(ring.landed[slot(k)], 16)

            load(0, 2, gate_t[0], True)
            load(0, 3, up_t[0], True)
            load(0, 4, gate_t[1], True)
            load(0, 5, up_t[1])
            with sp.Fori(1, PAIRS) as i:
                load(i, 0, gate_t[2 * i])
                load(i, 1, down_t[2 * i - 2])
                load(i, 2, down_t[2 * i - 1])
                load(i, 3, up_t[2 * i])
                load(i, 4, gate_t[2 * i + 1])
                load(i, 5, up_t[2 * i + 1])
            load(PAIRS, 0, down_t[FC - 2])
            load(PAIRS, 1, down_t[FC - 1])

        @block.scalar
        def _(act):
            def hi(i, k, first=False):
                act.wait_ge(ring.landed[slot(k)], 16 * (rnd(i, k) + 1))
                if k >= 4 and not first:
                    act.wait_ge(down_done, DC * i)
                elif not first:
                    act.wait_ge(product_done, 4 * i + {0: -2, 1: -1, 2: 0, 3: 1}[k])
                act.activation(ring.hi[:, slot(k)], ring.raw[:, slot(k)], ACT.Copy).then_inc(ring.hi_made, 1)

            def silu(i, j):
                act.wait_ge(product_done, 4 * i + 2 * j + 1)
                if j or not (isinstance(i, int) and i == 0):
                    act.wait_ge(h_made, 2 * i + j)
                act.activation(sg[:], ps_g[:].rearrange("p h t -> p (h t)"), ACT.Silu).then_inc(silu_done, 1)

            def h_split(i, j):
                act.wait_ge(h_made, 2 * i + j + 1)
                act.activation(h_hi[:, j, :], h_raw[:, j, :], ACT.Copy).then_inc(h_hi_made, 1)

            hi(0, 2, True)
            hi(0, 3, True)
            hi(0, 4, True)
            silu(0, 0)
            act.wait_ge(product_done, 1)
            hi(0, 5, True)
            h_split(0, 0)
            hi(1, 0)
            silu(0, 1)
            hi(1, 1)

            def pair(i):
                hi(i, 2)
                h_split(i - 1, 1)
                hi(i, 3)
                silu(i, 0)
                hi(i, 4)
                hi(i, 5)
                h_split(i, 0)
                hi(i + 1, 0)
                silu(i, 1)
                hi(i + 1, 1)

            with act.Fori(1, PAIRS) as i:
                pair(i)
            h_split(PAIRS - 1, 1)

        @block.vector
        def _(dve):
            def lo(i, k):
                dve.wait_ge(ring.hi_made, tile(i, k) + 1)
                dve.tensor_tensor(ring.lo[:, slot(k)], ring.raw[:, slot(k)], ring.hi[:, slot(k)].bitcast(F32),
                                  ALU.subtract).then_inc(ring.lo_made, 1)

            def gated(i, j):
                dve.wait_ge(silu_done, 2 * i + j + 1)
                dve.wait_ge(product_done, 4 * i + 2 * j + 2)
                dve.tensor_tensor(h_raw[:, j, :], sg[:], ps_u[:].rearrange("p h t -> p (h t)"),
                                  ALU.mult).then_inc(h_made, 1)

            def h_rest(i, j):
                dve.wait_ge(h_hi_made, 2 * i + j + 1)
                dve.tensor_tensor(h_lo[:, j, :], h_raw[:, j, :], h_hi[:, j, :].bitcast(F32),
                                  ALU.subtract).then_inc(h_lo_made, 1)

            def add_down(i):
                for d in range(DC):
                    dve.wait_ge(down_done, DC * i + d + 1)
                    dve.scalar_tensor_tensor(out=c.xT[:, d, :], in0=ps_d[:, d % 2].rearrange("p h t -> p (h t)"),
                                             scalar=0.5, in1=c.xT[:, d, :], op0=ALU.mult,
                                             op1=ALU.add).then_inc(added, 1)

            lo(0, 2)
            lo(0, 3)
            lo(0, 4)
            lo(0, 5)
            gated(0, 0)
            h_rest(0, 0)
            lo(1, 0)
            lo(1, 1)

            def pair(i):
                gated(i - 1, 1)
                lo(i, 2)
                h_rest(i - 1, 1)
                lo(i, 3)
                add_down(i - 1)
                lo(i, 4)
                lo(i, 5)
                gated(i, 0)
                h_rest(i, 0)
                lo(i + 1, 0)
                lo(i + 1, 1)

            with dve.Fori(1, PAIRS) as i:
                pair(i)
            gated(PAIRS - 1, 1)
            h_rest(PAIRS - 1, 1)
            add_down(PAIRS - 1)

        @block.tensor
        def _(pe):
            def gate(i, k, j, first=False):
                if not first:
                    pe.wait_ge(silu_done, 2 * i + j)
                pe.wait_ge(ring.lo_made, tile(i, k) + 1)
                for d in range(DC):
                    last = three_pass(pe, [ps_g[:, 0], ps_g[:, 1]], ring.hi[:, slot(k), d], ring.lo[:, slot(k), d],
                                      c.n_hi[:, d], c.n_lo[:, d], d == 0, d == DC - 1)
                last.then_inc(product_done, 1)

            def up(i, k, j, first=False):
                if not first:
                    pe.wait_ge(h_made, 2 * i + j)
                pe.wait_ge(ring.lo_made, tile(i, k) + 1)
                for d in range(DC):
                    last = three_pass(pe, [ps_u[:, 0], ps_u[:, 1]], ring.hi[:, slot(k), d], ring.lo[:, slot(k), d],
                                      c.n_hi[:, d], c.n_lo[:, d], d == 0, d == DC - 1)
                last.then_inc(product_done, 1)

            def down(i, ki, k, first=False):
                pe.wait_ge(ring.lo_made, tile(ki, k + 1) + 1)
                pe.wait_ge(h_lo_made, 2 * i + 2)
                for d in range(DC):
                    if not (first and d < 2):
                        pe.wait_ge(added, DC * i + d - 1)
                    for j in range(2):
                        last = three_pass(pe, [ps_d[:, d % 2, 0], ps_d[:, d % 2, 1]],
                                          ring.hi[:, slot(k + j), d], ring.lo[:, slot(k + j), d],
                                          h_hi[:, j], h_lo[:, j], j == 0, j == 1)
                    last.then_inc(down_done, 1)

            gate(0, 2, 0, True)
            up(0, 3, 0, True)
            gate(0, 4, 1)
            up(0, 5, 1)
            gate(1, 0, 0)
            down(0, 1, 1, True)
            up(1, 3, 0)
            gate(1, 4, 1)
            up(1, 5, 1)
            with pe.Fori(2, PAIRS) as i:
                gate(i, 0, 0)
                down(i - 1, i, 1)
                up(i, 3, 0)
                gate(i, 4, 1)
                up(i, 5, 1)
            down(PAIRS - 1, PAIRS, 0)


def past(engine, sem, value):
    if not (isinstance(value, int) and value <= 0):
        engine.wait_ge(sem, value)


def wait_apart(engine, sem, value):
    engine.wait_ge(sem, value)
    engine.nop(nofuse=True)


def mixer_setup(core, a):
    nc, c, per = core.nc, core, core.ctx
    c.masks = c.sb(per, "masks", [P, 7, CH])
    c.sel = c.sb(per, "sel", [BETA_ROW + 2 * DN_HEADS, HP, P])
    c.conv_w = c.sb(per, "conv_w", [P, 3, HP, CONV])
    c.branch_gain = c.sb(per, "branch_gain", [P, 2])
    c.dt_bias = c.sb(per, "dt_bias", [2 * DN_HEADS, 1])
    c.neg_a = c.sb(per, "neg_a", [2 * DN_HEADS, 1])
    c.slopes = c.sb(per, "slopes", [P, DF_HEADS])
    c.neg_lam = c.sb(per, "neg_lam", [P, 1])
    with ExitStack() as ctx:
        wide = c.sb(ctx, "wide_masks", [P, 7, P])
        lam_in = c.sb(ctx, "lam_in", [1, 4, HD])
        lam_sum = c.sb(ctx, "lam_sum", [1, 4])
        lam_ps = c.ps(ctx, "lam_ps", [P, HALF])
        cleared = c.sem("cleared")
        loaded = c.sem("params_loaded")
        cut = c.sem("masks_cut")
        step = c.sem("lam_step")
        exped = c.sem("lam_exped")
        lam_ready = c.sem("lam_ready")
        block = ctx.enter_context(nc.Block())

        @block.sync
        def _(sp):
            for kind in range(3):
                for hp in range(HP):
                    col = kind * DN_W + hp * P
                    sp.dma_start(c.conv_w[:, kind, hp, :], a["conv_qkv"][0, :, col:col + P].rearrange("w p -> p w"),
                                 allow_slow_non_contiguous=True).then_inc(loaded, 16)
            for h in range(2):
                sp.dma_start(c.branch_gain[h * HD:(h + 1) * HD, 0:1], a["dn_out_norm"].rearrange("l e -> e l"),
                             allow_slow_non_contiguous=True).then_inc(loaded, 16)
            sp.dma_start(c.branch_gain[:, 1:2], a["diff_subln"].rearrange("l e -> e l"),
                         allow_slow_non_contiguous=True).then_inc(loaded, 16)
            for i, name in enumerate(("diff_lambda_q1", "diff_lambda_k1", "diff_lambda_q2", "diff_lambda_k2")):
                sp.dma_start(lam_in[:, i, :], a[name]).then_inc(loaded, 16)
            sp.wait_ge(cleared, 3)
            sp.dma_start(c.dt_bias[0:DN_HEADS, :], a["dn_dt_bias"].rearrange("l h -> h l"),
                         allow_slow_non_contiguous=True).then_inc(loaded, 16)
            sp.dma_start(c.neg_a[0:DN_HEADS, :], a["dn_a_log"].rearrange("l h -> h l"),
                         allow_slow_non_contiguous=True).then_inc(loaded, 16)

        N_LOADS = 3 * HP + 3 + 4 + 2

        @block.gpsimd
        def _(pool):
            made = [0]

            def select(view, op, fill, base, pattern, mult):
                pool.wait_ge(cut, made[0])
                pool.affine_select(out=view, in_=view, compare_op=op, fill=fill, base=base, pattern=pattern,
                                   channel_multiplier=mult).then_inc(cut, 1)
                made[0] += 1

            pool.memset(wide[:], 1.0).then_inc(cut, 1)
            pool.memset(c.sel[:], 0.0).then_inc(cut, 1)
            made[0] = 2
            for lv in range(6):
                s = 1 << lv
                view = wide[:, lv, :].rearrange("p (b r) -> p b r", r=2 * s)
                nb = P // (2 * s)
                select(view, ALU.is_ge, 0.0, 0, [[-2 * s, nb], [0, 2 * s]], 1)
                select(view, ALU.is_ge, 0.0, s - 1, [[2 * s, nb], [0, 2 * s]], -1)
                select(view, ALU.is_ge, 0.0, -s, [[0, nb], [1, 2 * s]], 0)
            view = wide[:, 6, :].rearrange("p (b r) -> p b r", r=CH)
            select(view, ALU.is_ge, 0.0, 0, [[-CH, 2], [0, CH]], 1)
            select(view, ALU.is_ge, 0.0, 0, [[CH, 2], [1, CH]], -1)
            for kind in range(2):
                view = c.sel[BETA_ROW * kind:BETA_ROW * kind + 2 * DN_HEADS].rearrange("r h (b q) -> r h b q", b=2)
                select(view, ALU.not_equal, 1.0, -DN_HEADS * kind, [[-2, HP], [-1, 2], [0, CH]], 1)

        N_CUT = 2 + 18 + 2 + 2

        @block.vector
        def _(dve):
            dve.memset(c.dt_bias[:], 0.0).then_inc(cleared, 1)
            dve.memset(c.neg_a[:], 0.0).then_inc(cleared, 1)
            dve.memset(lam_sum[:], 0.0).then_inc(cleared, 1)
            for h in range(DF_HEADS):
                dve.memset(c.slopes[:, h:h + 1], 2.0 ** (-8.0 * (h + 1) / DF_HEADS))
            dve.wait_ge(loaded, 16 * N_LOADS)
            dve.tensor_scalar(c.branch_gain[:, 1:2], c.branch_gain[:, 1:2], 1.0 - LAM_INIT, None, ALU.mult)
            for m in range(2):
                dve.tensor_tensor(lam_in[:, m, :], lam_in[:, 2 * m, :], lam_in[:, 2 * m + 1, :],
                                  ALU.mult).then_inc(step, 1)
                dve.wait_ge(step, m + 1)
            dve.tensor_reduce(lam_sum[:, 0:2], lam_in[:, 0:2, :], AX_X, ALU.add).then_inc(step, 1)
            dve.wait_ge(exped, 1)
            dve.tensor_tensor(lam_sum[:, 2:3], lam_sum[:, 1:2], lam_sum[:, 0:1], ALU.subtract).then_inc(step, 1)
            dve.wait_ge(step, 4)
            dve.tensor_scalar(lam_sum[:, 3:4], lam_sum[:, 2:3], -LAM_INIT, None, ALU.add).then_inc(step, 1)
            dve.wait_ge(lam_ready, 1)
            dve.tensor_copy(c.neg_lam[:], lam_ps[:, 0:1])
            dve.wait_ge(cut, N_CUT)
            dve.tensor_tensor(c.masks[:], wide[:, :, 0:CH], wide[:, :, CH:P], ALU.add)
            dve.wait_ge(exped, 2)
            dve.tensor_scalar(c.neg_a[:], c.neg_a[:], -1.0, None, ALU.mult)

        @block.scalar
        def _(act):
            act.wait_ge(step, 3)
            act.activation(lam_sum[:, 0:2], lam_sum[:, 0:2], ACT.Exp).then_inc(exped, 1)
            act.wait_ge(loaded, 16 * N_LOADS)
            act.activation(c.neg_a[:], c.neg_a[:], ACT.Exp).then_inc(exped, 1)

        @block.tensor
        def _(pe):
            pe.wait_ge(step, 5)
            pe.matmul(lam_ps[:, 0:1], c.ones[0:1, :], lam_sum[:, 3:4], start=True, stop=True).then_inc(lam_ready, 1)


def column_tiles(w, first, count):
    return w[0, :, first:first + count * P].rearrange("(k p) (f c) -> f p k c", p=P, c=P)


def project(pe, core, ring, slot, banks):
    for d in range(DC):
        last = three_pass(pe, banks, ring.hi[:, slot, d], ring.lo[:, slot, d], core.n_hi[:, d], core.n_lo[:, d],
                          d == 0, d == DC - 1)
    return last


def dn_project_phase(core, a, qkv, gc, beta):
    nc, c = core.nc, core
    with ExitStack() as ctx:
        ring = Ring(c, ctx, 3)
        pad = c.sb(ctx, "padded", [P, CONV - 1 + T])
        acc = c.sb(ctx, "conv_acc", [P, T])
        sq = c.sb(ctx, "squares", [P, T])
        root = c.sb(ctx, "root", [P, T])
        ps_x = c.ps(ctx, "ps_proj", [P, 3, NH, HALF])
        ps_s = c.ps(ctx, "ps_sum", [P, NH, HALF])
        projected = c.sem("projected")
        padded = c.sem("padded")
        pad_zero = c.sem("pad_zero")
        conv_step = c.sem("conv_step")
        silu_done = c.sem("silu_done")
        squared = c.sem("squared")
        head_summed = c.sem("head_summed")
        rooted = c.sem("rooted")
        inverted = c.sem("inverted")
        normed = c.sem("normed")
        gate_step = c.sem("decay_step")
        gate_act = c.sem("decay_act")
        block = ctx.enter_context(nc.Block())
        w_in = a["w_in"]
        kinds = [column_tiles(w_in, kind * DN_W, HP) for kind in range(3)]
        NT = 3 * HP
        flat = lambda x: x.rearrange("p h t -> p (h t)")

        @block.sync
        def _(sp):
            def load(i, kind):
                past(sp, ring.lo_made, 3 * i + kind - 2)
                sp.dma_start(ring.raw[:, kind], kinds[kind][i]).then_inc(ring.landed[kind], 16)

            for kind in range(3):
                load(0, kind)
            with sp.Fori(1, HP) as i:
                for kind in range(3):
                    load(i, kind)
            sp.wait_ge(ring.lo_made, NT - 2)
            sp.dma_start(ring.raw[:, 0], column_tiles(w_in, OFF_AB, 1)[0]).then_inc(ring.landed[0], 16)

        @block.scalar
        def _(act):
            def hi(i, kind):
                act.wait_ge(ring.landed[kind], 16 * i + 16)
                past(act, projected, 3 * i + kind - 2)
                act.activation(ring.hi[:, kind], ring.raw[:, kind], ACT.Copy).then_inc(ring.hi_made, 1)

            def root_of(i, kind):
                act.wait_ge(head_summed, 2 * i + kind + 1)
                past(act, normed, 2 * i + kind)
                act.activation(root[:], flat(ps_s[:]), ACT.Sqrt, bias=c.eps[:, 0:1]).then_inc(rooted, 1)

            def pair(i, last=False):
                for kind in range(3):
                    if not (last and kind == 2):
                        hi(i + (kind + 2) // 3, (kind + 2) % 3)
                    act.wait_ge(projected, 3 * i + kind + 1)
                    past(act, conv_step, 4 * (3 * i + kind))
                    act.activation(pad[:, CONV - 1:], flat(ps_x[:, kind]), ACT.Copy).then_inc(padded, 1)
                    if kind:
                        root_of(i, kind - 1)
                    wait_apart(act, conv_step, 4 * (3 * i + kind) + 4)
                    act.activation(qkv[kind][:, i, :], acc[:], ACT.Silu).then_inc(silu_done, 1)
                    if kind < 2:
                        past(act, head_summed, 2 * i + kind)
                        wait_apart(act, silu_done, 3 * i + kind + 1)
                        act.activation(sq[:], qkv[kind][:, i, :], ACT.Square).then_inc(squared, 1)

            hi(0, 0)
            hi(0, 1)
            pair(0)
            with act.Fori(1, HP - 1) as i:
                pair(i)
            pair(HP - 1, True)
            R = 2 * DN_HEADS
            ab = flat(ps_x[0:R, 0])
            act.wait_ge(projected, NT + 1)
            act.wait_ge(normed, 2 * HP)
            act.activation(pad[0:R, 0:T], ab, ACT.Identity, bias=c.dt_bias[:]).then_inc(gate_act, 1)
            act.activation(beta, ab, ACT.Sigmoid).then_inc(gate_act, 1)
            act.wait_ge(gate_act, 1)
            act.activation(acc[0:R, :], pad[0:R, 0:T], ACT.Abs).then_inc(gate_act, 1)
            act.wait_ge(gate_act, 3)
            act.activation(sq[0:R, :], acc[0:R, :], ACT.Exp, scale=-1.0).then_inc(gate_act, 1)
            act.wait_ge(gate_act, 4)
            act.activation(root[0:R, :], sq[0:R, :], ACT.Ln, bias=1.0).then_inc(gate_act, 1)

        @block.vector
        def _(dve):
            def lo(i, kind):
                dve.wait_ge(ring.hi_made, 3 * i + kind + 1)
                dve.tensor_tensor(ring.lo[:, kind], ring.raw[:, kind], ring.hi[:, kind].bitcast(F32),
                                  ALU.subtract).then_inc(ring.lo_made, 1)

            def normalise(i, kind):
                m = 2 * i + kind
                dve.wait_ge(rooted, m + 1)
                dve.reciprocal(root[:], root[:]).then_inc(inverted, 1)
                dve.wait_ge(inverted, m + 1)
                x = qkv[kind][:, i, :]
                dve.scalar_tensor_tensor(out=x, in0=x, scalar=(HD ** -0.5 if kind == 0 else 1.0), in1=root[:],
                                         op0=ALU.mult, op1=ALU.mult).then_inc(normed, 1)

            def pair(i, last=False):
                for kind in range(3):
                    if not (last and kind == 2):
                        lo(i + (kind + 2) // 3, (kind + 2) % 3)
                    s0 = 4 * (3 * i + kind)
                    w = lambda tap: c.conv_w[:, kind, i, tap:tap + 1]
                    dve.wait_ge(padded, 3 * i + kind + 1)
                    past(dve, silu_done, 3 * i + kind)
                    dve.tensor_scalar(acc[:], pad[:, CONV - 1:], w(CONV - 1), None, ALU.mult).then_inc(conv_step, 1)
                    for tap in range(CONV - 1):
                        dve.wait_ge(conv_step, s0 + tap + 1)
                        dve.scalar_tensor_tensor(out=acc[:], in0=pad[:, tap:tap + T], scalar=w(tap), in1=acc[:],
                                                 op0=ALU.mult, op1=ALU.add).then_inc(conv_step, 1)
                    if kind:
                        normalise(i, kind - 1)

            dve.memset(pad[:, 0:CONV - 1], 0.0).then_inc(pad_zero, 1)
            dve.wait_ge(pad_zero, 1)
            lo(0, 0)
            lo(0, 1)
            pair(0)
            with dve.Fori(1, HP - 1) as i:
                pair(i)
            pair(HP - 1, True)
            R = 2 * DN_HEADS
            dve.wait_ge(gate_act, 5)
            dve.scalar_tensor_tensor(out=root[0:R, :], in0=pad[0:R, 0:T], scalar=0.0, in1=root[0:R, :], op0=ALU.max,
                                     op1=ALU.add).then_inc(gate_step, 1)
            dve.memset(acc[0:R, :], 1.0).then_inc(gate_step, 1)
            dve.wait_ge(gate_step, 2)
            dve.memset(acc[0:R, :].rearrange("r (n s) -> r n s", s=CH)[:, :, 0:1], 0.0).then_inc(gate_step, 1)
            dve.tensor_scalar(root[0:R, :], root[0:R, :], c.neg_a[:], None, ALU.mult).then_inc(gate_step, 1)
            dve.wait_ge(gate_step, 4)
            dve.tensor_tensor_scan(gc, acc[0:R, :], root[0:R, :], 0.0, ALU.mult, ALU.add)

        @block.tensor
        def _(pe):
            def tile(i, kind):
                pe.wait_ge(ring.lo_made, 3 * i + kind + 1)
                past(pe, padded, 3 * i + kind - 2)
                project(pe, c, ring, kind, [ps_x[:, kind, 0], ps_x[:, kind, 1]]).then_inc(projected, 1)

            def head_sum(i, kind):
                pe.wait_ge(squared, 2 * i + kind + 1)
                past(pe, rooted, 2 * i + kind)
                for h in range(NH):
                    last = pe.matmul(ps_s[:, h], c.head_ones[:], sq[:, h * HALF:(h + 1) * HALF], start=True, stop=True)
                last.then_inc(head_summed, 1)

            def pair(i):
                tile(i, 0)
                tile(i, 1)
                head_sum(i, 0)
                tile(i, 2)
                head_sum(i, 1)

            pair(0)
            with pe.Fori(1, HP) as i:
                pair(i)
            tile(HP, 0)


def dn_phase(core, qkv, gc, beta):
    nc, c = core.nc, core
    qT, kT, vT = qkv
    R = 2 * DN_HEADS
    SM = [P, HP, CH]
    with ExitStack() as ctx:
        sb = lambda name, shape=SM: c.sb(ctx, name, shape)
        kc, qc, vc = sb("kc"), sb("qc"), sb("vc")
        rows = sb("gc_beta_chunk", [BETA_ROW + R, CH])
        gcc, bcc = rows[0:R, :], rows[BETA_ROW:, :]
        diag = sb("diag", [P, 2 * HP, CH])
        col = sb("col", [P, 2 * HP])
        expo = sb("expo", [P, 3, HP])
        kb, rel, egb, at, attT, qd = sb("kb"), sb("rel"), sb("egb"), sb("at"), sb("attT"), sb("qd")
        lev = sb("lev", [P, 6, HP, CH])
        U, W, M = sb("U"), sb("W"), sb("M")
        bsc, kbe, kd, vb = sb("bsc", [P, HP]), sb("kbe"), sb("kd"), sb("vb")
        wtn, vnew, o_nat, S = sb("wtn"), sb("vnew"), sb("o_nat"), sb("S")
        psA = c.ps(ctx, "ps_bcast", [P, 2, HP, CH])
        psB = c.ps(ctx, "ps_nat", [P, 2, HP, CH])
        psC = c.ps(ctx, "ps_att", [P, 2, HP, CH])
        psD = c.ps(ctx, "ps_W", [P, 2, HP, CH])
        psE = c.ps(ctx, "ps_M", [P, 2, HP, CH])
        psF = c.ps(ctx, "ps_F", [P, 2, HP, CH])
        psG = c.ps(ctx, "ps_G", [P, 2, HP, CH])
        psH = c.ps(ctx, "ps_oT", [P, 2, HP, CH])
        s = {n: c.sem(n) for n in (
            "cut", "bcast", "nat", "kb_made", "scored", "decayed", "small_exp", "U_made", "lev_made",
            "W_ps", "W_made", "M_ps", "M_made", "step_ps", "step_taken", "dve", "wt_ps", "wt_made", "kbe_made",
            "vnew_ps", "vnew_made", "o_ps", "o_made", "dS_ps", "S_made", "oT_ps", "oT_made", "q_made")}
        block = ctx.enter_context(nc.Block())
        bc = lambda x: x.unsqueeze(2).broadcast_to([P, x.shape[1], CH])
        over = lambda m: m.unsqueeze(1).broadcast_to([P, HP, CH])
        DV_DIAG, DV_COL, DV_REL = 1, 2, 7
        DV = 14

        LV = 5

        @block.gpsimd
        def _(pool):
            def chunk(n):
                past(pool, s["oT_ps"], n)
                sl = bass.ts(n, CH)
                for i, (dst, src) in enumerate(((gcc, gc[:, sl]), (bcc, beta[:, sl]), (kc[:], kT[:, :, sl]),
                                                (qc[:], qT[:, :, sl]), (vc[:], vT[:, :, sl]))):
                    if i < 3:
                        past(pool, s["cut"], 5 * n + i)
                    pool.tensor_copy(dst, src).then_inc(s["cut"], 1)

            chunk(0)
            with pool.Fori(1, NCH) as n:
                chunk(n)

        @block.tensor
        def _(pe):
            def stacked(out, lhs, rhs, start=True, stop=True):
                for h in range(2):
                    r = slice(h * CH, (h + 1) * CH)
                    last = pe.matmul(out[r], lhs[r], rhs[r], start=start, stop=stop)
                return last

            def each(out, lhs, rhs):
                for hp in range(HP):
                    last = stacked(out[:, hp], lhs[:, hp], rhs if rhs is c.ident2 else rhs[:, hp])
                return last

            def chunk(n):
                first = isinstance(n, int) and n == 0
                pe.wait_ge(s["cut"], 5 * n + 2)
                past(pe, s["S_made"], 2 * n + 1 if not first else 0)
                for kind, row in ((0, gcc), (1, bcc)):
                    pick = c.sel[BETA_ROW * kind:BETA_ROW * kind + R]
                    for hp in range(HP):
                        last = pe.matmul((psA[:, 0], psF[:, 1])[kind][:, hp], pick[:, hp], row, start=True, stop=True)
                last.then_inc(s["bcast"], 1)
                wait_apart(pe, s["cut"], 5 * n + 5)
                each(psB[:, 0], kc, c.ident2)
                each(psB[:, 1], vc, c.ident2).then_inc(s["nat"], 1)
                each(psC[:, 0], kc, qc)
                wait_apart(pe, s["kb_made"], n + 1)
                each(psC[:, 1], kc, kb).then_inc(s["scored"], 1)
                wait_apart(pe, s["U_made"], n + 1)
                each(psD[:, 0], U, c.ident2).then_inc(s["W_ps"], 1)
                pe.wait_ge(s["W_made"], n + 1)
                wait_apart(pe, s["lev_made"], n + 1)
                for lv in range(1, LV + 1):
                    k = LV * n + lv
                    if lv > 1:
                        wait_apart(pe, s["step_taken"], k - 1)
                    each(psE[:, 0], lev[:, lv], W).then_inc(s["M_ps"], 1)
                    wait_apart(pe, s["M_made"], k)
                    last = each(psF[:, 0], M, U)
                    if lv < LV:
                        last = each(psG[:, 0], U, M)
                    last.then_inc(s["step_ps"], 1)
                pe.wait_ge(s["step_taken"], LV * n + LV)
                wait_apart(pe, s["kbe_made"], n + 1)
                each(psE[:, 0], kbe, U).then_inc(s["wt_ps"], 1)
                pe.wait_ge(s["wt_made"], n + 1)
                wait_apart(pe, s["S_made"], 2 * n + 1)
                for hp in range(HP):
                    stacked(psG[:, 0, hp], U[:, hp], vb[:, hp], True, False)
                    last = stacked(psG[:, 0, hp], wtn[:, hp], S[:, hp], False, True)
                last.then_inc(s["vnew_ps"], 1)
                pe.wait_ge(s["vnew_made"], n + 1)
                wait_apart(pe, s["q_made"], n + 1)
                for hp in range(HP):
                    stacked(psF[:, 0, hp], qd[:, hp], S[:, hp], True, False)
                    last = stacked(psF[:, 0, hp], attT[:, hp], vnew[:, hp], False, True)
                last.then_inc(s["o_ps"], 1)
                each(psD[:, 0], kd, vnew).then_inc(s["dS_ps"], 1)
                past(pe, s["oT_made"], n)
                wait_apart(pe, s["o_made"], n + 1)
                each(psH[:, 0], o_nat, c.ident2).then_inc(s["oT_ps"], 1)

            chunk(0)
            with pe.Fori(1, NCH) as n:
                chunk(n)

        @block.scalar
        def _(act):
            def chunk(n):
                act.wait_ge(s["dve"], DV * n + DV_REL)
                act.activation(expo[:], expo[:], ACT.Exp).then_inc(s["small_exp"], 1)
                act.activation(egb[:], psA[:, 0], ACT.Exp).then_inc(s["small_exp"], 1)
                act.activation(rel[:], rel[:], ACT.Exp).then_inc(s["decayed"], 1)
                act.wait_ge(s["W_ps"], n + 1)
                act.activation(W[:], psD[:, 0], ACT.Copy).then_inc(s["W_made"], 1)
                for lv in range(1, LV + 1):
                    act.wait_ge(s["M_ps"], LV * n + lv)
                    act.activation(M[:], psE[:, 0], ACT.Copy).then_inc(s["M_made"], 1)
                act.wait_ge(s["wt_ps"], n + 1)
                act.activation(wtn[:], psE[:, 0], ACT.Copy, scale=-1.0).then_inc(s["wt_made"], 1)
                act.wait_ge(s["vnew_ps"], n + 1)
                act.activation(vnew[:], psG[:, 0], ACT.Copy).then_inc(s["vnew_made"], 1)
                act.wait_ge(s["o_ps"], n + 1)
                act.activation(o_nat[:], psF[:, 0], ACT.Copy).then_inc(s["o_made"], 1)

            chunk(0)
            with act.Fori(1, NCH) as n:
                chunk(n)

        @block.vector
        def _(dve):
            def chunk(n):
                k = [0]
                first = isinstance(n, int) and n == 0

                def step(ins):
                    ins.then_inc(s["dve"], 1)
                    k[0] += 1

                def own(count):
                    dve.wait_ge(s["dve"], DV * n + count)

                dve.wait_ge(s["bcast"], n + 1)
                dve.wait_ge(s["cut"], 5 * n + 5)
                dve.tensor_tensor(diag[:, 0:HP], psA[:, 0], over(c.ident2[:]), ALU.mult)
                step(dve.tensor_tensor(diag[:, HP:], psF[:, 1], over(c.ident2[:]), ALU.mult))
                dve.tensor_tensor(kb[:], kc[:], psF[:, 1], ALU.mult).then_inc(s["kb_made"], 1)
                own(DV_DIAG)
                step(dve.tensor_reduce(col[:], diag[:], AX_X, ALU.add))
                own(DV_COL)
                last_gc = psA[:, 0, :, CH - 1]
                step(dve.tensor_copy(expo[:, 0, :], col[:, 0:HP]))
                step(dve.tensor_tensor(expo[:, 1, :], last_gc, col[:, 0:HP], ALU.subtract))
                step(dve.tensor_copy(expo[:, 2, :], last_gc))
                step(dve.tensor_tensor(rel[:], psA[:, 0], bc(col[:, 0:HP]), ALU.subtract))
                own(6)
                step(dve.tensor_scalar(rel[:], rel[:], 0.0, None, ALU.min))
                dve.wait_ge(s["small_exp"], 2 * n + 2)
                step(dve.tensor_tensor(bsc[:], col[:, HP:], expo[:, 0, :], ALU.mult))
                dve.wait_ge(s["decayed"], n + 1)
                step(dve.tensor_tensor(rel[:], rel[:], over(c.masks[:, 6]), ALU.mult))
                own(9)
                dve.wait_ge(s["scored"], n + 1)
                step(dve.tensor_tensor(at[:], psC[:, 1], rel[:], ALU.mult))
                own(10)
                step(dve.tensor_tensor(lev[:, 0], at[:], over(c.masks[:, 0]), ALU.mult))
                own(11)
                dve.tensor_tensor(U[:], over(c.ident2[:]), lev[:, 0], ALU.subtract).then_inc(s["U_made"], 1)
                for lv in range(1, LV + 1):
                    last = dve.tensor_tensor(lev[:, lv], at[:], over(c.masks[:, lv]), ALU.mult)
                last.then_inc(s["lev_made"], 1)
                step(dve.tensor_tensor(attT[:], psC[:, 0], rel[:], ALU.mult))
                dve.tensor_tensor(qd[:], qc[:], egb[:], ALU.mult).then_inc(s["q_made"], 1)
                dve.wait_ge(s["nat"], n + 1)
                step(dve.tensor_tensor(kd[:], psB[:, 0], bc(expo[:, 1, :]), ALU.mult))
                step(dve.tensor_tensor(vb[:], psB[:, 1], bc(col[:, HP:]), ALU.mult))
                dve.tensor_tensor(kbe[:], psB[:, 0], bc(bsc[:]), ALU.mult).then_inc(s["kbe_made"], 1)
                for lv in range(1, LV + 1):
                    dve.wait_ge(s["step_ps"], LV * n + lv)
                    if lv < LV:
                        dve.tensor_tensor(W[:], W[:], psG[:, 0], ALU.subtract)
                    dve.tensor_tensor(U[:], U[:], psF[:, 0], ALU.subtract).then_inc(s["step_taken"], 1)
                dve.wait_ge(s["dS_ps"], n + 1)
                dve.tensor_tensor(S[:], S[:], bc(expo[:, 2, :]), ALU.mult).then_inc(s["S_made"], 1)
                dve.wait_ge(s["S_made"], 2 * n + 2)
                dve.tensor_tensor(S[:], S[:], psD[:, 0], ALU.add).then_inc(s["S_made"], 1)
                dve.wait_ge(s["oT_ps"], n + 1)
                dve.tensor_copy(qT[:, :, bass.ts(n, CH)], psH[:, 0]).then_inc(s["oT_made"], 1)
                assert k[0] == DV

            dve.memset(S[:], 0.0).then_inc(s["S_made"], 1)
            chunk(0)
            with dve.Fori(1, NCH) as n:
                chunk(n)


def attention_phase(core, a, obT):
    nc, c = core.nc, core
    NQ = T // P
    with ExitStack() as ctx:
        ring = Ring(c, ctx, 3)
        q, k = c.sb(ctx, "q", [P, T]), c.sb(ctx, "k", [P, T])
        v = c.sb(ctx, "v", [P, NQ, P])
        bias = c.sb(ctx, "bias", [P, T])
        sc = c.sb(ctx, "scores", [P, 2, 2, T])
        pT = c.sb(ctx, "probs_t", [P, NQ, P])
        neg_max = c.sb(ctx, "neg_max", [P, 2, 2])
        total = c.sb(ctx, "total", [P, 2, 2])
        ps_s = c.ps(ctx, "ps_scores", [P, 2, NH, HALF])
        ps_t = c.ps(ctx, "ps_turned", [P, 2, 4, P])
        ps_o = c.ps(ctx, "ps_out", [P, 2, HALF])
        s = {n: c.sem(n) for n in (
            "bias", "projected", "evacuated", "v_turned", "v_made", "scored", "biased", "maxed", "negated",
            "exped", "inverted", "combining", "combined", "turned", "pT_made", "o_ps", "o_made")}
        block = ctx.enter_context(nc.Block())
        kinds = [column_tiles(a["w_in"], off, DF_HEADS) for off in (OFF_Q, OFF_K, OFF_V)]
        flat = lambda x: x.rearrange("p h t -> p (h t)")
        NTB = sum((i // 4) + 1 for i in range(NQ))
        tb0 = [sum((j // 4) + 1 for j in range(i)) for i in range(NQ + 1)]

        @block.sync
        def _(sp):
            def load(h, kind):
                past(sp, ring.lo_made, 3 * h + kind - 2)
                sp.dma_start(ring.raw[:, kind], kinds[kind][h]).then_inc(ring.landed[kind], 16)

            for kind in range(3):
                load(0, kind)
            with sp.Fori(1, DF_HEADS) as h:
                for kind in range(3):
                    load(h, kind)

        @block.gpsimd
        def _(pool):
            pool.iota(bias[:], pattern=[[1, T]], base=-(T - P), channel_multiplier=-1,
                      allow_small_or_imprecise_dtypes=True).then_inc(s["bias"], 1)
            pool.wait_ge(s["bias"], 1)
            pool.affine_select(out=bias[:], in_=bias[:], compare_op=ALU.is_ge, fill=NEG, base=T - P,
                               pattern=[[-1, T]], channel_multiplier=1).then_inc(s["bias"], 1)

        @block.tensor
        def _(pe):
            def head(h):
                for kind in range(3):
                    pe.wait_ge(ring.lo_made, 3 * h + kind + 1)
                    if kind < 2:
                        past(pe, s["biased"], 2 * NQ * h)
                    else:
                        pe.wait_ge(s["evacuated"], 3 * h + 1)
                    project(pe, c, ring, kind, [ps_s[:, kind % 2, 0], ps_s[:, kind % 2, 1]]).then_inc(s["projected"], 1)
                pe.wait_ge(s["evacuated"], 3 * h + 3)
                past(pe, s["pT_made"], NTB * h)
                for g in range(2):
                    for j in range(4):
                        kb = 4 * g + j
                        last = pe.transpose(ps_t[:, g, j], sc[:, 0, 0, kb * P:(kb + 1) * P], c.ident[:])
                    last.then_inc(s["v_turned"], 1)

                def scores(i):
                    n = (i + 1) * P
                    if i:
                        pe.wait_ge(s["biased"], 2 * NQ * h + 2 * i)
                    for m in range(2):
                        r = slice(m * HD, (m + 1) * HD)
                        for g in range((n + HALF - 1) // HALF):
                            w = min(HALF, n - g * HALF)
                            last = pe.matmul(ps_s[:, m, g, 0:w], q[r, i * P:(i + 1) * P],
                                             k[r, g * HALF:g * HALF + w], start=True, stop=True)
                    last.then_inc(s["scored"], 1)

                scores(0)
                pe.wait_ge(s["v_made"], 2 * h + 2)
                for i in range(NQ):
                    if i + 1 < NQ:
                        scores(i + 1)
                    pe.wait_ge(s["combined"], NQ * h + i + 1)
                    for g in range(i // 4 + 1):
                        b = tb0[i] + g
                        if i:
                            pe.wait_ge(s["pT_made"], NTB * h + (tb0[i - 1] + min(g, (i - 1) // 4) + 1))
                        for j in range(min(4, i + 1 - 4 * g)):
                            kb = 4 * g + j
                            last = pe.transpose(ps_t[:, g, j], sc[:, i % 2, 0, kb * P:(kb + 1) * P], c.ident[:])
                        last.then_inc(s["turned"], 1)
                    pe.wait_ge(s["pT_made"], NTB * h + tb0[i + 1])
                    past(pe, s["o_made"], NQ * h + i - 1)
                    for kb in range(i + 1):
                        last = pe.matmul(ps_o[:, i % 2, 0:P], v[:, kb], pT[:, kb], start=(kb == 0), stop=(kb == i))
                    last.then_inc(s["o_ps"], 1)

            head(0)
            with pe.Fori(1, DF_HEADS) as h:
                head(h)

        @block.scalar
        def _(act):
            def hi(h, kind):
                act.wait_ge(ring.landed[kind], 16 * h + 16)
                past(act, s["projected"], 3 * h + kind - 2)
                act.activation(ring.hi[:, kind], ring.raw[:, kind], ACT.Copy).then_inc(ring.hi_made, 1)

            def head(h, last=False):
                hi(h, 2)
                for kind, dst, scale in ((0, q[:], HD ** -0.5), (1, k[:], 1.0), (2, sc[:, 0, 0, :], 1.0)):
                    act.wait_ge(s["projected"], 3 * h + kind + 1)
                    if kind == 0:
                        past(act, s["o_ps"], NQ * h)
                    act.activation(dst, flat(ps_s[:, kind % 2]), ACT.Copy, scale=scale).then_inc(s["evacuated"], 1)
                if not last:
                    hi(h + 1, 0)
                    hi(h + 1, 1)

                def exps(i):
                    act.wait_ge(s["negated"], NQ * h + i + 1)
                    for m in range(2):
                        act.activation(sc[:, i % 2, m, 0:(i + 1) * P], sc[:, i % 2, m, 0:(i + 1) * P], ACT.Exp,
                                       bias=neg_max[:, i % 2, m:m + 1],
                                       accum_out=total[:, i % 2, m:m + 1]).then_inc(s["exped"], 1)

                def take_turned(i):
                    for g in range(i // 4 + 1):
                        w = min(4, i + 1 - 4 * g)
                        act.wait_ge(s["turned"], NTB * h + tb0[i] + g + 1)
                        past(act, s["o_ps"], NQ * h + i)
                        act.activation(pT[:, 4 * g:4 * g + w], ps_t[:, g, 0:w], ACT.Copy).then_inc(s["pT_made"], 1)

                def take_out(i):
                    wait_apart(act, s["o_ps"], NQ * h + i + 1)
                    act.activation(obT[:, h, i * P:(i + 1) * P], ps_o[:, i % 2, 0:P], ACT.Copy).then_inc(s["o_made"], 1)

                exps(0)
                for i in range(NQ):
                    if i + 1 < NQ:
                        exps(i + 1)
                    take_turned(i)
                    if i:
                        take_out(i - 1)
                take_out(NQ - 1)

            hi(0, 0)
            hi(0, 1)
            head(0)
            with act.Fori(1, DF_HEADS - 1) as h:
                head(h)
            head(DF_HEADS - 1, True)

        @block.vector
        def _(dve):
            def lo(h, kind):
                dve.wait_ge(ring.hi_made, 3 * h + kind + 1)
                dve.tensor_tensor(ring.lo[:, kind], ring.raw[:, kind], ring.hi[:, kind].bitcast(F32),
                                  ALU.subtract).then_inc(ring.lo_made, 1)

            def head(h, last=False):
                lo(h, 2)
                for g in range(2):
                    dve.wait_ge(s["v_turned"], 2 * h + g + 1)
                    dve.tensor_copy(v[:, 4 * g:4 * g + 4], ps_t[:, g]).then_inc(s["v_made"], 1)
                if not last:
                    lo(h + 1, 0)
                    lo(h + 1, 1)

                def bias_and_max(i):
                    n = (i + 1) * P
                    dve.wait_ge(s["scored"], NQ * h + i + 1)
                    if i >= 2:
                        dve.wait_ge(s["turned"], NTB * h + tb0[i - 1])
                    for m in range(2):
                        dve.scalar_tensor_tensor(out=sc[:, i % 2, m, 0:n], in0=bias[:, T - n:T],
                                                 scalar=c.slopes[:, bass.ts(h, 1)],
                                                 in1=flat(ps_s[:, m])[:, 0:n], op0=ALU.mult,
                                                 op1=ALU.add).then_inc(s["biased"], 1)
                    dve.wait_ge(s["biased"], 2 * NQ * h + 2 * i + 2)
                    dve.tensor_reduce(neg_max[:, i % 2], sc[:, i % 2, :, 0:n], AX_X, ALU.max).then_inc(s["maxed"], 1)
                    dve.wait_ge(s["maxed"], NQ * h + i + 1)
                    dve.tensor_scalar(neg_max[:, i % 2], neg_max[:, i % 2], -1.0, None, ALU.mult).then_inc(s["negated"], 1)

                def combine(i):
                    n = (i + 1) * P
                    w = total[:, i % 2]
                    dve.wait_ge(s["exped"], 2 * NQ * h + 2 * i + 2)
                    dve.reciprocal(w, w).then_inc(s["combining"], 1)
                    dve.wait_ge(s["combining"], 3 * (NQ * h + i) + 1)
                    dve.tensor_scalar(w[:, 1:2], w[:, 1:2], c.neg_lam[:], None, ALU.mult).then_inc(s["combining"], 1)
                    dve.wait_ge(s["combining"], 3 * (NQ * h + i) + 2)
                    dve.tensor_scalar(sc[:, i % 2, 1, 0:n], sc[:, i % 2, 1, 0:n], w[:, 1:2], None,
                                      ALU.mult).then_inc(s["combining"], 1)
                    dve.wait_ge(s["combining"], 3 * (NQ * h + i) + 3)
                    dve.scalar_tensor_tensor(out=sc[:, i % 2, 0, 0:n], in0=sc[:, i % 2, 0, 0:n], scalar=w[:, 0:1],
                                             in1=sc[:, i % 2, 1, 0:n], op0=ALU.mult,
                                             op1=ALU.add).then_inc(s["combined"], 1)

                bias_and_max(0)
                for i in range(NQ):
                    if i + 1 < NQ:
                        bias_and_max(i + 1)
                    combine(i)

            dve.wait_ge(s["bias"], 2)
            lo(0, 0)
            lo(0, 1)
            with dve.Fori(0, DF_HEADS - 1) as h:
                head(h)
            head(DF_HEADS - 1, True)


def branch_norm_phase(core, a, raw, lo_parts, hi_parts):
    nc, c = core.nc, core
    with ExitStack() as ctx:
        ring = Ring(c, ctx, 2)
        sq = c.sb(ctx, "squares", [P, T])
        root = c.sb(ctx, "root", [P, T])
        gate = c.sb(ctx, "silu_z", [P, T])
        val = c.sb(ctx, "value", [P, T])
        ps_z = c.ps(ctx, "ps_z", [P, NH, HALF])
        ps_s = c.ps(ctx, "ps_sum", [P, NH, HALF])
        s = {n: c.sem(n) for n in ("z_ps", "z_gate", "squared", "summed", "rooted", "dve", "value", "hi", "lo")}
        block = ctx.enter_context(nc.Block())
        flat = lambda x: x.rearrange("p h t -> p (h t)")
        z_tiles = column_tiles(a["w_in"], OFF_Z, HP)

        @block.sync
        def _(sp):
            for t in range(HP):
                past(sp, ring.lo_made, t - 1)
                sp.dma_start(ring.raw[:, t % 2], z_tiles[t]).then_inc(ring.landed[t % 2], 16)

        @block.tensor
        def _(pe):
            for t in range(HP):
                for b, ones in enumerate((c.head_ones, c.ones)):
                    j = 2 * t + b
                    pe.wait_ge(s["squared"], j + 1)
                    past(pe, s["rooted"], j)
                    for h in range(NH):
                        last = pe.matmul(ps_s[:, h], ones[:], sq[:, h * HALF:(h + 1) * HALF], start=True, stop=True)
                    last.then_inc(s["summed"], 1)
                    if b == 0:
                        pe.wait_ge(ring.lo_made, t + 1)
                        past(pe, s["z_gate"], t)
                        project(pe, c, ring, t % 2, [ps_z[:, 0], ps_z[:, 1]]).then_inc(s["z_ps"], 1)

        @block.scalar
        def _(act):
            def hi(t):
                act.wait_ge(ring.landed[t % 2], 16 * (t // 2) + 16)
                past(act, s["z_ps"], t - 1)
                act.activation(ring.hi[:, t % 2], ring.raw[:, t % 2], ACT.Copy).then_inc(ring.hi_made, 1)

            hi(0)
            hi(1)
            for t in range(HP):
                for b in range(2):
                    j = 2 * t + b
                    past(act, s["summed"], j)
                    act.activation(sq[:], raw[b][:, t, :], ACT.Square).then_inc(s["squared"], 1)
                    act.wait_ge(s["summed"], j + 1)
                    past(act, s["value"], j)
                    act.activation(root[:], flat(ps_s[:]), ACT.Sqrt, scale=1.0 / (HD if b == 0 else P),
                                   bias=c.eps[:, b:b + 1]).then_inc(s["rooted"], 1)
                    if b == 0:
                        act.wait_ge(s["z_ps"], t + 1)
                        past(act, s["value"], j - 1)
                        act.activation(gate[:], flat(ps_z[:]), ACT.Silu).then_inc(s["z_gate"], 1)
                        if t + 2 < HP:
                            hi(t + 2)
                    act.wait_ge(s["value"], j + 1)
                    act.activation(hi_parts[b][:, t, :], val[:], ACT.Copy).then_inc(s["hi"], 1)

        @block.vector
        def _(dve):
            def lo(t):
                dve.wait_ge(ring.hi_made, t + 1)
                dve.tensor_tensor(ring.lo[:, t % 2], ring.raw[:, t % 2], ring.hi[:, t % 2].bitcast(F32),
                                  ALU.subtract).then_inc(ring.lo_made, 1)

            lo(0)
            lo(1)
            steps = 0
            for t in range(HP):
                for b in range(2):
                    j = 2 * t + b
                    dve.wait_ge(s["rooted"], j + 1)
                    dve.reciprocal(root[:], root[:]).then_inc(s["dve"], 1)
                    steps += 1
                    dve.wait_ge(s["dve"], steps)
                    past(dve, s["lo"], j)
                    out = val[:]
                    ins = dve.scalar_tensor_tensor(out=out, in0=raw[b][:, t, :], scalar=c.branch_gain[:, b:b + 1],
                                                   in1=root[:], op0=ALU.mult, op1=ALU.mult)
                    if b == 0:
                        ins.then_inc(s["dve"], 1)
                        steps += 1
                        dve.wait_ge(s["dve"], steps)
                        dve.wait_ge(s["z_gate"], t + 1)
                        ins = dve.tensor_tensor(out, out, gate[:], ALU.mult)
                    ins.then_inc(s["value"], 1)
                    dve.wait_ge(s["hi"], j + 1)
                    dve.tensor_tensor(lo_parts[b][:, t, :], val[:], hi_parts[b][:, t, :].bitcast(F32),
                                      ALU.subtract).then_inc(s["lo"], 1)
                    if b == 0 and t + 2 < HP:
                        lo(t + 2)


def merge_phase(core, a, o_hi, o_lo):
    nc, c = core.nc, core
    with ExitStack() as ctx:
        ring = Ring(c, ctx, 2)
        ga = c.sb(ctx, "gated_a", [P, T])
        gb = c.sb(ctx, "gated_b", [P, T])
        m_hi = c.sb(ctx, "merged_hi", [P, T], F32R)
        m_lo = c.sb(ctx, "merged_lo", [P, T], F32R)
        ps_y = c.ps(ctx, "ps_y", [P, 2, NH, HALF])
        ps_g = c.ps(ctx, "ps_gate", [P, NH, HALF])
        ps_d = c.ps(ctx, "ps_out", [P, NH, HALF])
        s = {n: c.sem(n) for n in ("branches", "gates", "sig", "mul", "m_hi", "m_lo", "out_ps", "added")}
        block = ctx.enter_context(nc.Block())
        flat = lambda x: x.rearrange("p h t -> p (h t)")
        gates_a = column_tiles(a["w_in"], OFF_G, DC)
        gates_b = column_tiles(a["w_in"], OFF_G + D_MODEL, DC)
        br = [w[0].rearrange("(k p) (f c) -> f p k c", p=P, c=P) for w in (a["w_branch_a"], a["w_branch_b"])]
        w_out = a["w_out"][0].rearrange("(f p) (k c) -> f p k c", p=P, c=P)
        KB = DN_W // P
        BR, OUT, GA, GB = range(4)
        NO = DC * NH

        def number(d, kind):
            if isinstance(d, int) and d == 0:
                return {BR: 0, GA: 1, GB: 2}[kind]
            return 4 * d - 1 + kind

        def place(d, kind):
            if isinstance(d, int) and d == 0:
                return {BR: (0, 32), GA: (1, 16), GB: (0, 48)}[kind]
            return {BR: (1, 48 * d), OUT: (0, 32 * d + 32), GA: (1, 48 * d + 16), GB: (0, 32 * d + 48)}[kind]

        @block.sync
        def _(sp):
            def load(d, kind, src):
                slot, _ = place(d, kind)
                past(sp, ring.lo_made, number(d, kind) - 1)
                if kind == BR:
                    for b in range(2):
                        sp.dma_start(ring.raw[:, slot, b * KB:(b + 1) * KB], br[b][d]).then_inc(ring.landed[slot], 16)
                else:
                    sp.dma_start(ring.raw[:, slot], src).then_inc(ring.landed[slot], 16)

            load(0, BR, None)
            load(0, GA, gates_a[0])
            load(0, GB, gates_b[0])
            with sp.Fori(1, DC) as d:
                load(d, BR, None)
                load(d, OUT, w_out[d - 1])
                load(d, GA, gates_a[d])
                load(d, GB, gates_b[d])
            sp.wait_ge(ring.lo_made, 4 * DC - 2)
            sp.dma_start(ring.raw[:, 1], w_out[DC - 1]).then_inc(ring.landed[1], 16)

        @block.scalar
        def _(act):
            def split(slot, landed):
                act.wait_ge(ring.landed[slot], landed)
                act.activation(ring.hi[:, slot], ring.raw[:, slot], ACT.Copy).then_inc(ring.hi_made, 1)

            def hi(d, kind):
                if kind == BR:
                    past(act, s["gates"], 2 * d - 1)
                elif kind == OUT:
                    act.wait_ge(s["gates"], 2 * d)
                elif kind == GA:
                    past(act, s["branches"], d + 1 if not (isinstance(d, int) and d == 0) else 0)
                elif isinstance(d, int) and d == 0:
                    act.wait_ge(s["branches"], 1)
                else:
                    act.wait_ge(s["out_ps"], NO * d)
                split(*place(d, kind))

            def gate(d, b, dst):
                act.wait_ge(s["gates"], 2 * d + b + 1)
                past(act, s["m_lo"], d)
                act.activation(dst[:], flat(ps_g[:]), ACT.Sigmoid).then_inc(s["sig"], 1)

            def merged(d):
                act.wait_ge(s["mul"], 3 * d + 3)
                past(act, s["out_ps"], NO * d)
                act.activation(m_hi[:], ga[:], ACT.Copy).then_inc(s["m_hi"], 1)

            hi(0, BR)
            hi(0, GA)
            hi(0, GB)
            gate(0, 0, ga)
            hi(1, BR)
            gate(0, 1, gb)
            hi(1, OUT)
            merged(0)

            def chunk(d, last=False):
                hi(d, GA)
                hi(d, GB)
                gate(d, 0, ga)
                if not last:
                    hi(d + 1, BR)
                else:
                    split(1, 48 * DC - 16)
                gate(d, 1, gb)
                if not last:
                    hi(d + 1, OUT)
                merged(d)

            with act.Fori(1, DC - 1) as d:
                chunk(d)
            chunk(DC - 1, True)

        @block.vector
        def _(dve):
            def lo(t, slot):
                dve.wait_ge(ring.hi_made, t + 1)
                dve.tensor_tensor(ring.lo[:, slot], ring.raw[:, slot], ring.hi[:, slot].bitcast(F32),
                                  ALU.subtract).then_inc(ring.lo_made, 1)

            def gated(d, b, dst):
                dve.wait_ge(s["sig"], 2 * d + b + 1)
                dve.tensor_tensor(dst[:], dst[:], flat(ps_y[:, b]), ALU.mult).then_inc(s["mul"], 1)

            def merged(d):
                dve.wait_ge(s["mul"], 3 * d + 2)
                dve.tensor_tensor(ga[:], ga[:], gb[:], ALU.add).then_inc(s["mul"], 1)

            def merged_lo(d):
                dve.wait_ge(s["m_hi"], d + 1)
                dve.tensor_tensor(m_lo[:], ga[:], m_hi[:].bitcast(F32), ALU.subtract).then_inc(s["m_lo"], 1)

            def add_out(d):
                for e in range(DC):
                    for h in range(NH):
                        dve.wait_ge(s["out_ps"], NO * d + NH * e + h + 1)
                        x = c.xT[:, e, h * HALF:(h + 1) * HALF]
                        dve.tensor_tensor(x, x, ps_d[:, h], ALU.add).then_inc(s["added"], 1)

            lo(0, 0)
            lo(1, 1)
            lo(2, 0)
            gated(0, 0, ga)
            lo(number(1, BR), 1)
            gated(0, 1, gb)
            merged(0)
            lo(number(1, OUT), 0)
            merged_lo(0)

            def chunk(d, last=False):
                lo(4 * d + 1, 1)
                add_out(d - 1)
                lo(4 * d + 2, 0)
                gated(d, 0, ga)
                lo(4 * d + 3, 1)
                gated(d, 1, gb)
                merged(d)
                if not last:
                    lo(4 * d + 4, 0)
                merged_lo(d)

            with dve.Fori(1, DC - 1) as d:
                chunk(d)
            chunk(DC - 1, True)
            add_out(DC - 1)

        @block.tensor
        def _(pe):
            def branches(d):
                slot, _ = place(d, BR)
                pe.wait_ge(ring.lo_made, number(d, BR) + 1)
                past(pe, s["mul"], 3 * d)
                for b in range(2):
                    for k in range(KB):
                        last = three_pass(pe, [ps_y[:, b, 0], ps_y[:, b, 1]], ring.hi[:, slot, b * KB + k],
                                          ring.lo[:, slot, b * KB + k], o_hi[b][:, k], o_lo[b][:, k],
                                          k == 0, k == KB - 1)
                last.then_inc(s["branches"], 1)

            def gate(d, b):
                slot, _ = place(d, (GA, GB)[b])
                pe.wait_ge(ring.lo_made, number(d, (GA, GB)[b]) + 1)
                past(pe, s["sig"], 2 * d + b)
                project(pe, c, ring, slot, [ps_g[:, 0], ps_g[:, 1]]).then_inc(s["gates"], 1)

            def out(d, t, slot):
                pe.wait_ge(ring.lo_made, t + 1)
                pe.wait_ge(s["m_lo"], d + 1)
                for e in range(DC):
                    for h in range(NH):
                        past(pe, s["added"], NO * d + NH * e + h - 1)
                        hs = slice(h * HALF, (h + 1) * HALF)
                        pe.matmul(ps_d[:, h], ring.hi[:, slot, e], m_hi[:, hs], start=True, stop=False)
                        pe.matmul(ps_d[:, h], ring.hi[:, slot, e], m_lo[:, hs], start=False, stop=False)
                        pe.matmul(ps_d[:, h], ring.lo[:, slot, e], m_hi[:, hs], start=False,
                                  stop=True).then_inc(s["out_ps"], 1)

            branches(0)
            gate(0, 0)
            gate(0, 1)
            branches(1)
            out(0, 4, 0)
            gate(1, 0)
            gate(1, 1)
            with pe.Fori(2, DC) as d:
                branches(d)
                out(d - 1, 4 * d, 0)
                gate(d, 0)
                gate(d, 1)
            out(DC - 1, 4 * DC - 1, 1)


def mixer(core, a):
    nc, c = core.nc, core
    with ExitStack() as ctx:
        SH = [P, HP, T]
        q_hi, qT = c.sb_shared(ctx, "oa", SH)
        with ExitStack() as dn:
            kT, vT = c.sb(dn, "kT", SH), c.sb(dn, "vT", SH)
            gc_beta = c.sb(dn, "gc_beta", [BETA_ROW + 2 * DN_HEADS, T])
            gc, beta = gc_beta[0:2 * DN_HEADS, :], gc_beta[BETA_ROW:, :]
            dn_project_phase(c, a, [qT, kT, vT], gc, beta)
            core.end_phase()
            dn_phase(c, [qT, kT, vT], gc, beta)
            core.end_phase()
        b_hi, obT = c.sb_shared(ctx, "ob", SH)
        attention_phase(c, a, obT)
        core.end_phase()
        a_lo, b_lo = c.sb(ctx, "oa_lo", SH, F32R), c.sb(ctx, "ob_lo", SH, F32R)
        branch_norm_phase(c, a, [qT, obT], [a_lo, b_lo], [q_hi, b_hi])
        core.end_phase()
        merge_phase(c, a, [q_hi, b_hi], [a_lo, b_lo])
        core.end_phase()


def build(nc, a, out):
    with ExitStack() as ctx:
        core = Core(nc, ctx)
        setup_phase(core, a)
        core.end_phase()
        norm_phase(core, 0)
        core.end_phase()
        ffn_phase(core, a["ffn1_w_gate"], a["ffn1_w_up"], a["ffn1_w_down"])
        core.end_phase()
        norm_phase(core, 1)
        core.end_phase()
        mixer_setup(core, a)
        core.end_phase()
        mixer(core, a)
        norm_phase(core, 2)
        core.end_phase()
        ffn_phase(core, a["ffn2_w_gate"], a["ffn2_w_up"], a["ffn2_w_down"])
        core.end_phase()
        norm_phase(core, 3, out)
        core.end_phase()


_INS = ["x", "ffn1_norm", "ffn1_w_gate", "ffn1_w_up", "ffn1_w_down", "mix_norm", "w_in", "conv_qkv",
        "dn_a_log", "dn_dt_bias", "dn_out_norm", "diff_lambda_q1", "diff_lambda_k1", "diff_lambda_q2",
        "diff_lambda_k2", "diff_subln", "w_branch_a", "w_branch_b", "w_out", "ffn2_norm", "ffn2_w_gate",
        "ffn2_w_up", "ffn2_w_down", "final_norm"]


def kernel(**inputs):
    import numpy as np
    import concourse.bacc as bacc
    from concourse.bass_utils import run_bass_kernel_spmd

    nc = bacc.Bacc("TRN2", target_bir_lowering=False, num_devices=1)
    arrays, handles = {}, {}
    for name in _INS:
        arr = np.ascontiguousarray(inputs[name])
        arrays[f"in_{name}"] = arr
        handles[name] = nc.dram_tensor(f"in_{name}", arr.shape, mybir.dt.from_np(arr.dtype),
                                       kind="ExternalInput").ap()
    out = nc.dram_tensor("y_out", (1, T, D_MODEL), F32, kind="ExternalOutput").ap()
    build(nc, handles, out)
    res = run_bass_kernel_spmd(nc, [arrays], core_ids=[0])
    return res.results[0]["y_out"]
```

```python
from contextlib import ExitStack

import concourse.bass as bass
from concourse import mybir

F32 = mybir.dt.float32
F32R = mybir.dt.float32r
ACT = mybir.ActivationFunctionType
ALU = mybir.AluOpType
AX_X = mybir.AxisListType.X

P = 128
D_MODEL = 1024
T = 1024
DC = D_MODEL // P
HALF = 512
NH = T // HALF
D_FF = 2816
FC = D_FF // P
HD = 64
DN_HEADS = 8
HP = DN_HEADS // 2
DN_W = DN_HEADS * HD
CH = 64
NCH = T // CH
DF_HEADS = 4
CONV = 4
RMS_EPS = 1e-6
SUBLN_EPS = 1e-5
L2_EPS = 1e-6
LAM_INIT = 0.8 - 0.6
OFF_Z = 3 * DN_W
OFF_AB = OFF_Z + DN_W
OFF_Q = OFF_AB + 2 * DN_HEADS
OFF_K = OFF_Q + DF_HEADS * P
OFF_V = OFF_K + DF_HEADS * P
OFF_G = OFF_V + DF_HEADS * P
NEG = -3.0e38
BETA_ROW = 32


class Core:

    def __init__(self, nc, ctx):
        self.nc = nc
        self.ctx = ctx
        self.n = 0
        self.sems = []

    def sb(self, ctx, name, shape, dt=F32):
        self.n += 1
        return ctx.enter_context(self.nc.sbuf_tensor(f"{name}_{self.n}", shape, dt))

    def sb_shared(self, ctx, name, shape):
        split = self.sb(ctx, f"{name}_hi", shape, F32R)
        size = 4
        for s in shape[1:]:
            size *= s
        return split, self.nc.alloc_sbuf_tensor_at(f"{name}_raw_{self.n}", shape, F32,
                                                   offset=self.nc.sbuf_base - size)

    def ps(self, ctx, name, shape):
        self.n += 1
        return ctx.enter_context(self.nc.psum_tensor(f"{name}_{self.n}", shape, F32))

    def sem(self, name):
        self.n += 1
        self.sems.append(self.nc.alloc_semaphore(name=f"{name}_{self.n}"))
        return self.sems[-1]

    def end_phase(self):
        self.nc.clear_and_free_semaphores(self.sems)
        self.nc.all_engine_barrier()
        self.sems = []


def three_pass(pe, banks, w_hi, w_lo, x_hi, x_lo, start, stop):
    for h, bank in enumerate(banks):
        pe.matmul(bank, w_hi, x_hi[:, h * HALF:(h + 1) * HALF], start=start, stop=False)
    for h, bank in enumerate(banks):
        pe.matmul(bank, w_hi, x_lo[:, h * HALF:(h + 1) * HALF], start=False, stop=False)
    for h, bank in enumerate(banks):
        last = pe.matmul(bank, w_lo, x_hi[:, h * HALF:(h + 1) * HALF], start=False, stop=stop)
    return last


class Ring:

    def __init__(self, core, ctx, depth):
        self.depth = depth
        self.raw = core.sb(ctx, "w_raw", [P, depth, DC, P])
        self.hi = core.sb(ctx, "w_hi", [P, depth, DC, P], F32R)
        self.lo = core.sb(ctx, "w_lo", [P, depth, DC, P], F32R)
        self.landed = [core.sem(f"w_landed{s}") for s in range(depth)]
        self.hi_made = core.sem("w_hi_made")
        self.lo_made = core.sem("w_lo_made")


def setup_phase(core, a):
    nc = core.nc
    c = core
    per = core.ctx
    c.xT = c.sb(per, "xT", [P, DC, T])
    c.n_hi = c.sb(per, "n_hi", [P, DC, T], F32R)
    c.n_lo = c.sb(per, "n_lo", [P, DC, T], F32R)
    c.ident = c.sb(per, "ident", [P, P])
    c.ones = c.sb(per, "ones", [P, P])
    c.head_ones = c.sb(per, "head_ones", [P, P])
    c.ident2 = c.sb(per, "ident2", [P, CH])
    c.gains = c.sb(per, "gains", [P, 4, DC])
    c.eps = c.sb(per, "eps", [P, 2])

    gains_in = c.sem("gains_loaded")
    zeroed = c.sem("consts_zeroed")
    made = c.sem("consts_made")
    turned = c.sem("x_turned")
    taken = c.sem("x_taken")
    with ExitStack() as ctx:
        xin = c.sb(ctx, "x_in", [P, 2, D_MODEL])
        xps = c.ps(ctx, "x_ps", [P, 4, HALF])
        slot_in = [c.sem("x_in_slot0"), c.sem("x_in_slot1")]
        block = ctx.enter_context(nc.Block())
        xrows = a["x"].rearrange("b (t p) d -> (b t) p d", p=P)

        @block.sync
        def _(sp):
            for i, name in enumerate(("ffn1_norm", "mix_norm", "ffn2_norm")):
                sp.dma_start(c.gains[:, i, :], a[name].rearrange("l (c p) -> p (l c)", p=P),
                             allow_slow_non_contiguous=True).then_inc(gains_in, 16)
            sp.dma_start(c.gains[:, 3, :], a["final_norm"].rearrange("(c p) -> p c", p=P),
                             allow_slow_non_contiguous=True).then_inc(gains_in, 16)
            for t in range(T // P):
                if t >= 2:
                    sp.wait_ge(turned, 2 * (t - 1))
                sp.dma_start(xin[:, t % 2, :], xrows[t]).then_inc(slot_in[t % 2], 16)
            sp.wait_ge(gains_in, 64)

        @block.gpsimd
        def _(pool):
            pool.memset(c.ident[:], 0.0).then_inc(zeroed, 1)
            pool.memset(c.ones[:], 1.0).then_inc(zeroed, 1)
            pool.memset(c.eps[:, 0:1], RMS_EPS).then_inc(zeroed, 1)
            pool.memset(c.eps[:, 1:2], SUBLN_EPS).then_inc(zeroed, 1)
            pool.memset(c.head_ones[:], 0.0).then_inc(zeroed, 1)
            pool.wait_ge(zeroed, 5)
            pool.affine_select(out=c.ident[:], in_=c.ident[:], compare_op=ALU.not_equal, fill=1.0, base=0,
                               pattern=[[-1, P]], channel_multiplier=1).then_inc(made, 1)

        @block.tensor
        def _(pe):
            pe.wait_ge(made, 1)
            for t in range(T // P):
                pe.wait_ge(slot_in[t % 2], 16 * (t // 2 + 1))
                for g in range(2):
                    k = 2 * t + g
                    if k >= 4:
                        pe.wait_ge(taken, k - 3)
                    for j in range(4):
                        d = 4 * g + j
                        last = pe.transpose(xps[:, k % 4, j * P:(j + 1) * P],
                                            xin[:, t % 2, d * P:(d + 1) * P], c.ident[:])
                    last.then_inc(turned, 1)

        @block.vector
        def _(dve):
            dve.wait_ge(zeroed, 5)
            for h in range(2):
                dve.memset(c.head_ones[h * HD:(h + 1) * HD, h * HD:(h + 1) * HD], 1.0)
            dve.wait_ge(made, 1)
            dve.tensor_tensor(c.ident2[:], c.ident[:, 0:CH], c.ident[:, CH:P], ALU.add)
            for t in range(T // P):
                for g in range(2):
                    k = 2 * t + g
                    dve.wait_ge(turned, k + 1)
                    dve.tensor_copy(c.xT[:, 4 * g:4 * g + 4, t * P:(t + 1) * P],
                                    xps[:, k % 4, :].rearrange("p (j q) -> p j q", j=4)).then_inc(taken, 1)


def norm_phase(core, which, out=None):
    nc, c = core.nc, core
    gain = c.gains[:, which, :]
    squared = c.sem("squared")
    summed = c.sem("summed")
    rooted = c.sem("rooted")
    inverted = c.sem("inverted")
    scaled = c.sem("scaled")
    hi_made = c.sem("n_hi_made")
    lo_made = c.sem("n_lo_made")
    turned = c.sem("y_turned")
    copied = c.sem("y_copied")
    with ExitStack() as ctx:
        sq = c.sb(ctx, "sq", [P, 2, T])
        rstd = c.sb(ctx, "rstd", [P, T])
        nrm = c.sb(ctx, "nrm", [P, 2 if out is None else DC, T])
        NB = 2 if out is None else DC
        ss = c.ps(ctx, "ss", [P, NH, HALF])
        if out is not None:
            y = c.sb(ctx, "y", [P, 2, D_MODEL])
            yps = c.ps(ctx, "yps", [P, 4, HALF])
            slot_out = [c.sem("y_out0"), c.sem("y_out1")]
        block = ctx.enter_context(nc.Block())

        @block.scalar
        def _(act):
            for k in range(DC):
                if k >= 2:
                    act.wait_ge(summed, k - 1)
                act.activation(sq[:, k % 2, :], c.xT[:, k, :], ACT.Square).then_inc(squared, 1)
            act.wait_ge(summed, DC)
            act.activation(rstd[:], ss[:].rearrange("p h t -> p (h t)"), ACT.Sqrt, scale=1.0 / D_MODEL,
                           bias=c.eps[:, 0:1]).then_inc(rooted, 1)
            if out is None:
                for k in range(DC):
                    act.wait_ge(scaled, k + 1)
                    act.activation(c.n_hi[:, k, :], nrm[:, k % NB, :], ACT.Copy).then_inc(hi_made, 1)

        @block.tensor
        def _(pe):
            for k in range(DC):
                pe.wait_ge(squared, k + 1)
                for h in range(NH):
                    last = pe.matmul(ss[:, h, :], c.ones[:], sq[:, k % 2, h * HALF:(h + 1) * HALF],
                                     start=(k == 0), stop=(k == DC - 1))
                last.then_inc(summed, 1)
            if out is not None:
                pe.wait_ge(scaled, DC)
                for t in range(T // P):
                    for g in range(2):
                        k = 2 * t + g
                        if k >= 4:
                            pe.wait_ge(copied, k - 3)
                        for j in range(4):
                            last = pe.transpose(yps[:, k % 4, j * P:(j + 1) * P],
                                                nrm[:, 4 * g + j, t * P:(t + 1) * P], c.ident[:])
                        last.then_inc(turned, 1)

        @block.vector
        def _(dve):
            dve.wait_ge(rooted, 1)
            dve.reciprocal(rstd[:], rstd[:]).then_inc(inverted, 1)
            dve.wait_ge(inverted, 1)
            for k in range(DC):
                if k >= NB:
                    dve.wait_ge(lo_made, k - NB + 1)
                dve.scalar_tensor_tensor(out=nrm[:, k % NB, :], in0=c.xT[:, k, :], scalar=gain[:, k:k + 1],
                                         in1=rstd[:], op0=ALU.mult, op1=ALU.mult).then_inc(scaled, 1)
                if out is None and k >= 1:
                    dve.wait_ge(hi_made, k)
                    dve.tensor_tensor(c.n_lo[:, k - 1, :], nrm[:, (k - 1) % NB, :], c.n_hi[:, k - 1, :].bitcast(F32),
                                      ALU.subtract).then_inc(lo_made, 1)
            if out is None:
                dve.wait_ge(hi_made, DC)
                dve.tensor_tensor(c.n_lo[:, DC - 1, :], nrm[:, (DC - 1) % NB, :],
                                  c.n_hi[:, DC - 1, :].bitcast(F32), ALU.subtract).then_inc(lo_made, 1)
            else:
                for t in range(T // P):
                    if t >= 2:
                        dve.wait_ge(slot_out[t % 2], 16 * (t // 2))
                    for g in range(2):
                        k = 2 * t + g
                        dve.wait_ge(turned, k + 1)
                        dve.tensor_copy(y[:, t % 2, g * HALF:(g + 1) * HALF], yps[:, k % 4, :]).then_inc(copied, 1)

        if out is not None:
            orow = out.rearrange("b (t p) d -> (b t) p d", p=P)

            @block.sync
            def _(sp):
                for t in range(T // P):
                    sp.wait_ge(copied, 2 * (t + 1))
                    sp.dma_start(orow[t], y[:, t % 2, :]).then_inc(slot_out[t % 2], 16)
                sp.wait_ge(slot_out[0], 16 * (T // P // 2))
                sp.wait_ge(slot_out[1], 16 * (T // P // 2))


def ffn_phase(core, w_gate, w_up, w_down):
    nc, c = core.nc, core
    PAIRS = FC // 2
    with ExitStack() as ctx:
        ring = Ring(c, ctx, 3)
        sg = c.sb(ctx, "silu_gate", [P, T])
        h_raw = c.sb(ctx, "h_raw", [P, 2, T])
        h_hi = c.sb(ctx, "h_hi", [P, 2, T], F32R)
        h_lo = c.sb(ctx, "h_lo", [P, 2, T], F32R)
        ps_g = c.ps(ctx, "ps_gate", [P, NH, HALF])
        ps_u = c.ps(ctx, "ps_up", [P, NH, HALF])
        ps_d = c.ps(ctx, "ps_down", [P, 2, NH, HALF])
        product_done = c.sem("product_done")
        silu_done = c.sem("silu_done")
        h_made = c.sem("h_made")
        h_hi_made = c.sem("h_hi_made")
        h_lo_made = c.sem("h_lo_made")
        down_done = c.sem("down_done")
        added = c.sem("added")
        block = ctx.enter_context(nc.Block())
        cols = lambda w: w.rearrange("l (k p) (f c) -> (l f) p k c", p=P, c=P)
        gate_t, up_t = cols(w_gate), cols(w_up)
        down_t = w_down.rearrange("l (f p) (k c) -> (l f) p k c", p=P, c=P)
        slot = lambda k: (k - 2) % 3
        rnd = lambda i, k: 2 * i + (k - 2) // 3
        tile = lambda i, k: 6 * i - 2 + k

        @block.sync
        def _(sp):
            def load(i, k, src, first=False):
                if not first:
                    sp.wait_ge(ring.lo_made, tile(i, k) - 2)
                sp.dma_start(ring.raw[:, slot(k)], src).then_inc(ring.landed[slot(k)], 16)

            load(0, 2, gate_t[0], True)
            load(0, 3, up_t[0], True)
            load(0, 4, gate_t[1], True)
            load(0, 5, up_t[1])
            with sp.Fori(1, PAIRS) as i:
                load(i, 0, gate_t[2 * i])
                load(i, 1, down_t[2 * i - 2])
                load(i, 2, down_t[2 * i - 1])
                load(i, 3, up_t[2 * i])
                load(i, 4, gate_t[2 * i + 1])
                load(i, 5, up_t[2 * i + 1])
            load(PAIRS, 0, down_t[FC - 2])
            load(PAIRS, 1, down_t[FC - 1])

        @block.scalar
        def _(act):
            def hi(i, k, first=False):
                act.wait_ge(ring.landed[slot(k)], 16 * (rnd(i, k) + 1))
                if k >= 4 and not first:
                    act.wait_ge(down_done, DC * i)
                elif not first:
                    act.wait_ge(product_done, 4 * i + {0: -2, 1: -1, 2: 0, 3: 1}[k])
                act.activation(ring.hi[:, slot(k)], ring.raw[:, slot(k)], ACT.Copy).then_inc(ring.hi_made, 1)

            def silu(i, j):
                act.wait_ge(product_done, 4 * i + 2 * j + 1)
                if j or not (isinstance(i, int) and i == 0):
                    act.wait_ge(h_made, 2 * i + j)
                act.activation(sg[:], ps_g[:].rearrange("p h t -> p (h t)"), ACT.Silu).then_inc(silu_done, 1)

            def h_split(i, j):
                act.wait_ge(h_made, 2 * i + j + 1)
                act.activation(h_hi[:, j, :], h_raw[:, j, :], ACT.Copy).then_inc(h_hi_made, 1)

            hi(0, 2, True)
            hi(0, 3, True)
            hi(0, 4, True)
            silu(0, 0)
            act.wait_ge(product_done, 1)
            hi(0, 5, True)
            h_split(0, 0)
            hi(1, 0)
            silu(0, 1)
            hi(1, 1)

            def pair(i):
                hi(i, 2)
                h_split(i - 1, 1)
                hi(i, 3)
                silu(i, 0)
                hi(i, 4)
                hi(i, 5)
                h_split(i, 0)
                hi(i + 1, 0)
                silu(i, 1)
                hi(i + 1, 1)

            with act.Fori(1, PAIRS) as i:
                pair(i)
            h_split(PAIRS - 1, 1)

        @block.vector
        def _(dve):
            def lo(i, k):
                dve.wait_ge(ring.hi_made, tile(i, k) + 1)
                dve.tensor_tensor(ring.lo[:, slot(k)], ring.raw[:, slot(k)], ring.hi[:, slot(k)].bitcast(F32),
                                  ALU.subtract).then_inc(ring.lo_made, 1)

            def gated(i, j):
                dve.wait_ge(silu_done, 2 * i + j + 1)
                dve.wait_ge(product_done, 4 * i + 2 * j + 2)
                dve.tensor_tensor(h_raw[:, j, :], sg[:], ps_u[:].rearrange("p h t -> p (h t)"),
                                  ALU.mult).then_inc(h_made, 1)

            def h_rest(i, j):
                dve.wait_ge(h_hi_made, 2 * i + j + 1)
                dve.tensor_tensor(h_lo[:, j, :], h_raw[:, j, :], h_hi[:, j, :].bitcast(F32),
                                  ALU.subtract).then_inc(h_lo_made, 1)

            def add_down(i):
                for d in range(DC):
                    dve.wait_ge(down_done, DC * i + d + 1)
                    dve.scalar_tensor_tensor(out=c.xT[:, d, :], in0=ps_d[:, d % 2].rearrange("p h t -> p (h t)"),
                                             scalar=0.5, in1=c.xT[:, d, :], op0=ALU.mult,
                                             op1=ALU.add).then_inc(added, 1)

            lo(0, 2)
            lo(0, 3)
            lo(0, 4)
            lo(0, 5)
            gated(0, 0)
            h_rest(0, 0)
            lo(1, 0)
            lo(1, 1)

            def pair(i):
                gated(i - 1, 1)
                lo(i, 2)
                h_rest(i - 1, 1)
                lo(i, 3)
                add_down(i - 1)
                lo(i, 4)
                lo(i, 5)
                gated(i, 0)
                h_rest(i, 0)
                lo(i + 1, 0)
                lo(i + 1, 1)

            with dve.Fori(1, PAIRS) as i:
                pair(i)
            gated(PAIRS - 1, 1)
            h_rest(PAIRS - 1, 1)
            add_down(PAIRS - 1)

        @block.tensor
        def _(pe):
            def gate(i, k, j, first=False):
                if not first:
                    pe.wait_ge(silu_done, 2 * i + j)
                pe.wait_ge(ring.lo_made, tile(i, k) + 1)
                for d in range(DC):
                    last = three_pass(pe, [ps_g[:, 0], ps_g[:, 1]], ring.hi[:, slot(k), d], ring.lo[:, slot(k), d],
                                      c.n_hi[:, d], c.n_lo[:, d], d == 0, d == DC - 1)
                last.then_inc(product_done, 1)

            def up(i, k, j, first=False):
                if not first:
                    pe.wait_ge(h_made, 2 * i + j)
                pe.wait_ge(ring.lo_made, tile(i, k) + 1)
                for d in range(DC):
                    last = three_pass(pe, [ps_u[:, 0], ps_u[:, 1]], ring.hi[:, slot(k), d], ring.lo[:, slot(k), d],
                                      c.n_hi[:, d], c.n_lo[:, d], d == 0, d == DC - 1)
                last.then_inc(product_done, 1)

            def down(i, ki, k, first=False):
                pe.wait_ge(ring.lo_made, tile(ki, k + 1) + 1)
                pe.wait_ge(h_lo_made, 2 * i + 2)
                for d in range(DC):
                    if not (first and d < 2):
                        pe.wait_ge(added, DC * i + d - 1)
                    for j in range(2):
                        last = three_pass(pe, [ps_d[:, d % 2, 0], ps_d[:, d % 2, 1]],
                                          ring.hi[:, slot(k + j), d], ring.lo[:, slot(k + j), d],
                                          h_hi[:, j], h_lo[:, j], j == 0, j == 1)
                    last.then_inc(down_done, 1)

            gate(0, 2, 0, True)
            up(0, 3, 0, True)
            gate(0, 4, 1)
            up(0, 5, 1)
            gate(1, 0, 0)
            down(0, 1, 1, True)
            up(1, 3, 0)
            gate(1, 4, 1)
            up(1, 5, 1)
            with pe.Fori(2, PAIRS) as i:
                gate(i, 0, 0)
                down(i - 1, i, 1)
                up(i, 3, 0)
                gate(i, 4, 1)
                up(i, 5, 1)
            down(PAIRS - 1, PAIRS, 0)


def past(engine, sem, value):
    if not (isinstance(value, int) and value <= 0):
        engine.wait_ge(sem, value)


def wait_apart(engine, sem, value):
    engine.wait_ge(sem, value)
    engine.nop(nofuse=True)


def mixer_setup(core, a):
    nc, c, per = core.nc, core, core.ctx
    c.masks = c.sb(per, "masks", [P, 7, CH])
    c.sel = c.sb(per, "sel", [BETA_ROW + 2 * DN_HEADS, HP, P])
    c.conv_w = c.sb(per, "conv_w", [P, 3, HP, CONV])
    c.branch_gain = c.sb(per, "branch_gain", [P, 2])
    c.dt_bias = c.sb(per, "dt_bias", [2 * DN_HEADS, 1])
    c.neg_a = c.sb(per, "neg_a", [2 * DN_HEADS, 1])
    c.slopes = c.sb(per, "slopes", [P, DF_HEADS])
    c.neg_lam = c.sb(per, "neg_lam", [P, 1])
    with ExitStack() as ctx:
        wide = c.sb(ctx, "wide_masks", [P, 7, P])
        lam_in = c.sb(ctx, "lam_in", [1, 4, HD])
        lam_sum = c.sb(ctx, "lam_sum", [1, 4])
        lam_ps = c.ps(ctx, "lam_ps", [P, HALF])
        cleared = c.sem("cleared")
        loaded = c.sem("params_loaded")
        cut = c.sem("masks_cut")
        step = c.sem("lam_step")
        exped = c.sem("lam_exped")
        lam_ready = c.sem("lam_ready")
        block = ctx.enter_context(nc.Block())

        @block.sync
        def _(sp):
            for kind in range(3):
                for hp in range(HP):
                    col = kind * DN_W + hp * P
                    sp.dma_start(c.conv_w[:, kind, hp, :], a["conv_qkv"][0, :, col:col + P].rearrange("w p -> p w"),
                                 allow_slow_non_contiguous=True).then_inc(loaded, 16)
            for h in range(2):
                sp.dma_start(c.branch_gain[h * HD:(h + 1) * HD, 0:1], a["dn_out_norm"].rearrange("l e -> e l"),
                             allow_slow_non_contiguous=True).then_inc(loaded, 16)
            sp.dma_start(c.branch_gain[:, 1:2], a["diff_subln"].rearrange("l e -> e l"),
                         allow_slow_non_contiguous=True).then_inc(loaded, 16)
            for i, name in enumerate(("diff_lambda_q1", "diff_lambda_k1", "diff_lambda_q2", "diff_lambda_k2")):
                sp.dma_start(lam_in[:, i, :], a[name]).then_inc(loaded, 16)
            sp.wait_ge(cleared, 3)
            sp.dma_start(c.dt_bias[0:DN_HEADS, :], a["dn_dt_bias"].rearrange("l h -> h l"),
                         allow_slow_non_contiguous=True).then_inc(loaded, 16)
            sp.dma_start(c.neg_a[0:DN_HEADS, :], a["dn_a_log"].rearrange("l h -> h l"),
                         allow_slow_non_contiguous=True).then_inc(loaded, 16)

        N_LOADS = 3 * HP + 3 + 4 + 2

        @block.gpsimd
        def _(pool):
            made = [0]

            def select(view, op, fill, base, pattern, mult):
                pool.wait_ge(cut, made[0])
                pool.affine_select(out=view, in_=view, compare_op=op, fill=fill, base=base, pattern=pattern,
                                   channel_multiplier=mult).then_inc(cut, 1)
                made[0] += 1

            pool.memset(wide[:], 1.0).then_inc(cut, 1)
            pool.memset(c.sel[:], 0.0).then_inc(cut, 1)
            made[0] = 2
            for lv in range(6):
                s = 1 << lv
                view = wide[:, lv, :].rearrange("p (b r) -> p b r", r=2 * s)
                nb = P // (2 * s)
                select(view, ALU.is_ge, 0.0, 0, [[-2 * s, nb], [0, 2 * s]], 1)
                select(view, ALU.is_ge, 0.0, s - 1, [[2 * s, nb], [0, 2 * s]], -1)
                select(view, ALU.is_ge, 0.0, -s, [[0, nb], [1, 2 * s]], 0)
            view = wide[:, 6, :].rearrange("p (b r) -> p b r", r=CH)
            select(view, ALU.is_ge, 0.0, 0, [[-CH, 2], [0, CH]], 1)
            select(view, ALU.is_ge, 0.0, 0, [[CH, 2], [1, CH]], -1)
            for kind in range(2):
                view = c.sel[BETA_ROW * kind:BETA_ROW * kind + 2 * DN_HEADS].rearrange("r h (b q) -> r h b q", b=2)
                select(view, ALU.not_equal, 1.0, -DN_HEADS * kind, [[-2, HP], [-1, 2], [0, CH]], 1)

        N_CUT = 2 + 18 + 2 + 2

        @block.vector
        def _(dve):
            dve.memset(c.dt_bias[:], 0.0).then_inc(cleared, 1)
            dve.memset(c.neg_a[:], 0.0).then_inc(cleared, 1)
            dve.memset(lam_sum[:], 0.0).then_inc(cleared, 1)
            for h in range(DF_HEADS):
                dve.memset(c.slopes[:, h:h + 1], 2.0 ** (-8.0 * (h + 1) / DF_HEADS))
            dve.wait_ge(loaded, 16 * N_LOADS)
            dve.tensor_scalar(c.branch_gain[:, 1:2], c.branch_gain[:, 1:2], 1.0 - LAM_INIT, None, ALU.mult)
            for m in range(2):
                dve.tensor_tensor(lam_in[:, m, :], lam_in[:, 2 * m, :], lam_in[:, 2 * m + 1, :],
                                  ALU.mult).then_inc(step, 1)
                dve.wait_ge(step, m + 1)
            dve.tensor_reduce(lam_sum[:, 0:2], lam_in[:, 0:2, :], AX_X, ALU.add).then_inc(step, 1)
            dve.wait_ge(exped, 1)
            dve.tensor_tensor(lam_sum[:, 2:3], lam_sum[:, 1:2], lam_sum[:, 0:1], ALU.subtract).then_inc(step, 1)
            dve.wait_ge(step, 4)
            dve.tensor_scalar(lam_sum[:, 3:4], lam_sum[:, 2:3], -LAM_INIT, None, ALU.add).then_inc(step, 1)
            dve.wait_ge(lam_ready, 1)
            dve.tensor_copy(c.neg_lam[:], lam_ps[:, 0:1])
            dve.wait_ge(cut, N_CUT)
            dve.tensor_tensor(c.masks[:], wide[:, :, 0:CH], wide[:, :, CH:P], ALU.add)
            dve.wait_ge(exped, 2)
            dve.tensor_scalar(c.neg_a[:], c.neg_a[:], -1.0, None, ALU.mult)

        @block.scalar
        def _(act):
            act.wait_ge(step, 3)
            act.activation(lam_sum[:, 0:2], lam_sum[:, 0:2], ACT.Exp).then_inc(exped, 1)
            act.wait_ge(loaded, 16 * N_LOADS)
            act.activation(c.neg_a[:], c.neg_a[:], ACT.Exp).then_inc(exped, 1)

        @block.tensor
        def _(pe):
            pe.wait_ge(step, 5)
            pe.matmul(lam_ps[:, 0:1], c.ones[0:1, :], lam_sum[:, 3:4], start=True, stop=True).then_inc(lam_ready, 1)


def column_tiles(w, first, count):
    return w[0, :, first:first + count * P].rearrange("(k p) (f c) -> f p k c", p=P, c=P)


def project(pe, core, ring, slot, banks):
    for d in range(DC):
        last = three_pass(pe, banks, ring.hi[:, slot, d], ring.lo[:, slot, d], core.n_hi[:, d], core.n_lo[:, d],
                          d == 0, d == DC - 1)
    return last


def dn_project_phase(core, a, qkv, gc, beta):
    nc, c = core.nc, core
    with ExitStack() as ctx:
        ring = Ring(c, ctx, 3)
        pad = c.sb(ctx, "padded", [P, CONV - 1 + T])
        acc = c.sb(ctx, "conv_acc", [P, T])
        sq = c.sb(ctx, "squares", [P, T])
        root = c.sb(ctx, "root", [P, T])
        ps_x = c.ps(ctx, "ps_proj", [P, 3, NH, HALF])
        ps_s = c.ps(ctx, "ps_sum", [P, NH, HALF])
        projected = c.sem("projected")
        padded = c.sem("padded")
        pad_zero = c.sem("pad_zero")
        conv_step = c.sem("conv_step")
        silu_done = c.sem("silu_done")
        squared = c.sem("squared")
        head_summed = c.sem("head_summed")
        rooted = c.sem("rooted")
        inverted = c.sem("inverted")
        normed = c.sem("normed")
        gate_step = c.sem("decay_step")
        gate_act = c.sem("decay_act")
        block = ctx.enter_context(nc.Block())
        w_in = a["w_in"]
        kinds = [column_tiles(w_in, kind * DN_W, HP) for kind in range(3)]
        NT = 3 * HP
        flat = lambda x: x.rearrange("p h t -> p (h t)")

        @block.sync
        def _(sp):
            def load(i, kind):
                past(sp, ring.lo_made, 3 * i + kind - 2)
                sp.dma_start(ring.raw[:, kind], kinds[kind][i]).then_inc(ring.landed[kind], 16)

            for kind in range(3):
                load(0, kind)
            with sp.Fori(1, HP) as i:
                for kind in range(3):
                    load(i, kind)
            sp.wait_ge(ring.lo_made, NT - 2)
            sp.dma_start(ring.raw[:, 0], column_tiles(w_in, OFF_AB, 1)[0]).then_inc(ring.landed[0], 16)

        @block.scalar
        def _(act):
            def hi(i, kind):
                act.wait_ge(ring.landed[kind], 16 * i + 16)
                past(act, projected, 3 * i + kind - 2)
                act.activation(ring.hi[:, kind], ring.raw[:, kind], ACT.Copy).then_inc(ring.hi_made, 1)

            def root_of(i, kind):
                act.wait_ge(head_summed, 2 * i + kind + 1)
                past(act, normed, 2 * i + kind)
                act.activation(root[:], flat(ps_s[:]), ACT.Sqrt, bias=c.eps[:, 0:1]).then_inc(rooted, 1)

            def pair(i, last=False):
                for kind in range(3):
                    if not (last and kind == 2):
                        hi(i + (kind + 2) // 3, (kind + 2) % 3)
                    act.wait_ge(projected, 3 * i + kind + 1)
                    past(act, conv_step, 4 * (3 * i + kind))
                    act.activation(pad[:, CONV - 1:], flat(ps_x[:, kind]), ACT.Copy).then_inc(padded, 1)
                    if kind:
                        root_of(i, kind - 1)
                    wait_apart(act, conv_step, 4 * (3 * i + kind) + 4)
                    act.activation(qkv[kind][:, i, :], acc[:], ACT.Silu).then_inc(silu_done, 1)
                    if kind < 2:
                        past(act, head_summed, 2 * i + kind)
                        wait_apart(act, silu_done, 3 * i + kind + 1)
                        act.activation(sq[:], qkv[kind][:, i, :], ACT.Square).then_inc(squared, 1)

            hi(0, 0)
            hi(0, 1)
            pair(0)
            with act.Fori(1, HP - 1) as i:
                pair(i)
            pair(HP - 1, True)
            R = 2 * DN_HEADS
            ab = flat(ps_x[0:R, 0])
            act.wait_ge(projected, NT + 1)
            act.wait_ge(normed, 2 * HP)
            act.activation(pad[0:R, 0:T], ab, ACT.Identity, bias=c.dt_bias[:]).then_inc(gate_act, 1)
            act.activation(beta, ab, ACT.Sigmoid).then_inc(gate_act, 1)
            act.wait_ge(gate_act, 1)
            act.activation(acc[0:R, :], pad[0:R, 0:T], ACT.Abs).then_inc(gate_act, 1)
            act.wait_ge(gate_act, 3)
            act.activation(sq[0:R, :], acc[0:R, :], ACT.Exp, scale=-1.0).then_inc(gate_act, 1)
            act.wait_ge(gate_act, 4)
            act.activation(root[0:R, :], sq[0:R, :], ACT.Ln, bias=1.0).then_inc(gate_act, 1)

        @block.vector
        def _(dve):
            def lo(i, kind):
                dve.wait_ge(ring.hi_made, 3 * i + kind + 1)
                dve.tensor_tensor(ring.lo[:, kind], ring.raw[:, kind], ring.hi[:, kind].bitcast(F32),
                                  ALU.subtract).then_inc(ring.lo_made, 1)

            def normalise(i, kind):
                m = 2 * i + kind
                dve.wait_ge(rooted, m + 1)
                dve.reciprocal(root[:], root[:]).then_inc(inverted, 1)
                dve.wait_ge(inverted, m + 1)
                x = qkv[kind][:, i, :]
                dve.scalar_tensor_tensor(out=x, in0=x, scalar=(HD ** -0.5 if kind == 0 else 1.0), in1=root[:],
                                         op0=ALU.mult, op1=ALU.mult).then_inc(normed, 1)

            def pair(i, last=False):
                for kind in range(3):
                    if not (last and kind == 2):
                        lo(i + (kind + 2) // 3, (kind + 2) % 3)
                    s0 = 4 * (3 * i + kind)
                    w = lambda tap: c.conv_w[:, kind, i, tap:tap + 1]
                    dve.wait_ge(padded, 3 * i + kind + 1)
                    past(dve, silu_done, 3 * i + kind)
                    dve.tensor_scalar(acc[:], pad[:, CONV - 1:], w(CONV - 1), None, ALU.mult).then_inc(conv_step, 1)
                    for tap in range(CONV - 1):
                        dve.wait_ge(conv_step, s0 + tap + 1)
                        dve.scalar_tensor_tensor(out=acc[:], in0=pad[:, tap:tap + T], scalar=w(tap), in1=acc[:],
                                                 op0=ALU.mult, op1=ALU.add).then_inc(conv_step, 1)
                    if kind:
                        normalise(i, kind - 1)

            dve.memset(pad[:, 0:CONV - 1], 0.0).then_inc(pad_zero, 1)
            dve.wait_ge(pad_zero, 1)
            lo(0, 0)
            lo(0, 1)
            pair(0)
            with dve.Fori(1, HP - 1) as i:
                pair(i)
            pair(HP - 1, True)
            R = 2 * DN_HEADS
            dve.wait_ge(gate_act, 5)
            dve.scalar_tensor_tensor(out=root[0:R, :], in0=pad[0:R, 0:T], scalar=0.0, in1=root[0:R, :], op0=ALU.max,
                                     op1=ALU.add).then_inc(gate_step, 1)
            dve.memset(acc[0:R, :], 1.0).then_inc(gate_step, 1)
            dve.wait_ge(gate_step, 2)
            dve.memset(acc[0:R, :].rearrange("r (n s) -> r n s", s=CH)[:, :, 0:1], 0.0).then_inc(gate_step, 1)
            dve.tensor_scalar(root[0:R, :], root[0:R, :], c.neg_a[:], None, ALU.mult).then_inc(gate_step, 1)
            dve.wait_ge(gate_step, 4)
            dve.tensor_tensor_scan(gc, acc[0:R, :], root[0:R, :], 0.0, ALU.mult, ALU.add)

        @block.tensor
        def _(pe):
            def tile(i, kind):
                pe.wait_ge(ring.lo_made, 3 * i + kind + 1)
                past(pe, padded, 3 * i + kind - 2)
                project(pe, c, ring, kind, [ps_x[:, kind, 0], ps_x[:, kind, 1]]).then_inc(projected, 1)

            def head_sum(i, kind):
                pe.wait_ge(squared, 2 * i + kind + 1)
                past(pe, rooted, 2 * i + kind)
                for h in range(NH):
                    last = pe.matmul(ps_s[:, h], c.head_ones[:], sq[:, h * HALF:(h + 1) * HALF], start=True, stop=True)
                last.then_inc(head_summed, 1)

            def pair(i):
                tile(i, 0)
                tile(i, 1)
                head_sum(i, 0)
                tile(i, 2)
                head_sum(i, 1)

            pair(0)
            with pe.Fori(1, HP) as i:
                pair(i)
            tile(HP, 0)


def dn_phase(core, qkv, gc, beta):
    nc, c = core.nc, core
    qT, kT, vT = qkv
    R = 2 * DN_HEADS
    C2 = 2
    UN = C2 * HP
    STEPS = NCH // C2
    SM = [P, UN, CH]
    with ExitStack() as ctx:
        sb = lambda name, shape=SM: c.sb(ctx, name, shape)
        kc, qc, vc = sb("kc"), sb("qc"), sb("vc")
        rows = sb("gc_beta_chunk", [BETA_ROW + R, C2 * CH])
        gcc, bcc = rows[0:R, :], rows[BETA_ROW:, :]
        diag = sb("diag", [P, 2, UN, CH])
        col = sb("col", [P, 2, UN])
        expo = sb("expo", [P, 3, UN])
        kb, rel, at, attT = sb("kb"), sb("rel"), sb("at"), sb("attT")
        qd = sb("qd")
        lev = sb("lev", [P, 6, UN, CH])
        U, W, M = sb("U"), sb("W"), sb("M")
        bsc, kbe, kd, vb = sb("bsc", [P, UN]), sb("kbe"), sb("kd"), sb("vb")
        wtn = sb("wtn")
        vnew, o_nat = sb("vnew", [P, HP, CH]), sb("o_nat")
        S = sb("state", [P, 2, HP, CH])
        psA, psB, psC, psD, psE, psF, psG, psH = (
            c.ps(ctx, f"ps_{n}", SM) for n in ("gc", "k_nat", "v_nat", "att", "AT", "beta", "g", "h"))
        psM, psU, psW = (psE, psH), (psF, psA), (psG, psD)
        s = {n: c.sem(n) for n in (
            "cut", "bcast", "nat", "kb_made", "scored", "decayed", "small_exp", "U_made", "lev_made",
            "W_ps", "W_made", "M_ps", "M_made", "step_ps", "dve", "wt_ps", "wt_made", "kbe_made",
            "vnew_ps", "vnew_made", "o_ps", "o_made", "dS_ps", "S_faded", "S_made", "oT_ps", "oT_made", "q_made")}
        taken = [c.sem(f"step_taken{i}") for i in range(C2)]
        block = ctx.enter_context(nc.Block())
        bc = lambda x: x.unsqueeze(2).broadcast_to([P, x.shape[1], CH])
        over = lambda m: m.unsqueeze(1).broadcast_to([P, UN, CH])
        pair_of = lambda x, m: x[:, :, bass.ts(m, C2 * CH)].rearrange("p h (c s) -> p c h s", c=C2)
        units = lambda x: x[:].rearrange("p (c h) s -> p c h s", c=C2)
        of_chunk = lambda x, i: x[:, i * HP:(i + 1) * HP]
        DV_DIAG, DV_COL, DV_REL = 1, 2, 7
        DV = 14

        LV = 5

        @block.gpsimd
        def _(pool):
            def step(m):
                past(pool, s["scored"], m)
                past(pool, s["q_made"], m)
                sl = bass.ts(m, C2 * CH)
                for i, (dst, src) in enumerate(((gcc, gc[:, sl]), (bcc, beta[:, sl]), (units(kc), pair_of(kT, m)),
                                                (units(qc), pair_of(qT, m)), (units(vc), pair_of(vT, m)))):
                    if i < 3:
                        past(pool, s["cut"], 5 * m + i)
                    pool.tensor_copy(dst, src).then_inc(s["cut"], 1)

            step(0)
            with pool.Fori(1, STEPS) as m:
                step(m)

        @block.tensor
        def _(pe):
            def stacked(out, lhs, rhs, start=True, stop=True):
                for h in range(2):
                    r = slice(h * CH, (h + 1) * CH)
                    last = pe.matmul(out[r], lhs[r], rhs[r], start=start, stop=stop)
                return last

            def each(out, lhs, rhs):
                for u in range(out.shape[1]):
                    last = stacked(out[:, u], lhs[:, u], rhs if rhs is c.ident2 else rhs[:, u])
                return last

            def step(m):
                pe.wait_ge(s["cut"], 5 * m + 2)
                past(pe, s["S_made"], C2 * m + 1 if not isinstance(m, int) else 0)
                for kind, row in ((0, gcc), (1, bcc)):
                    pick = c.sel[BETA_ROW * kind:BETA_ROW * kind + R]
                    for u in range(UN):
                        i = u // HP
                        last = pe.matmul((psA, psF)[kind][:, u], pick[:, u % HP], row[:, i * CH:(i + 1) * CH],
                                         start=True, stop=True)
                last.then_inc(s["bcast"], 1)
                past(pe, s["oT_made"], m)
                wait_apart(pe, s["cut"], 5 * m + 5)
                each(psB, kc, c.ident2)
                each(psC, vc, c.ident2).then_inc(s["nat"], 1)
                each(psD, kc, qc)
                wait_apart(pe, s["kb_made"], m + 1)
                each(psE, kc, kb).then_inc(s["scored"], 1)
                pe.wait_ge(s["small_exp"], 2 * m + 2)
                wait_apart(pe, s["U_made"], m + 1)
                each(psA, U, c.ident2).then_inc(s["W_ps"], 1)
                pe.wait_ge(s["W_made"], m + 1)
                wait_apart(pe, s["lev_made"], m + 1)
                for lv in range(1, LV + 1):
                    k = LV * m + lv
                    for i in range(C2):
                        if lv > 1:
                            wait_apart(pe, taken[i], k - 1)
                        each(of_chunk(psM[i], i), of_chunk(lev[:, lv], i), of_chunk(W, i)).then_inc(s["M_ps"], 1)
                    for i in range(C2):
                        if i and lv == 1:
                            pe.wait_ge(s["q_made"], m + 1)
                        wait_apart(pe, s["M_made"], C2 * (k - 1) + i + 1)
                        last = each(of_chunk(psU[i], i), of_chunk(M, i), of_chunk(U, i))
                        if lv < LV:
                            last = each(of_chunk(psW[i], i), of_chunk(U, i), of_chunk(M, i))
                        last.then_inc(s["step_ps"], 1)
                pe.wait_ge(s["kbe_made"], m + 1)
                for i in range(C2):
                    wait_apart(pe, taken[i], LV * m + LV)
                    each(of_chunk(psM[i], i), of_chunk(kbe, i), of_chunk(U, i)).then_inc(s["wt_ps"], 1)
                for i in range(C2):
                    k = C2 * m + i
                    pe.wait_ge(s["wt_made"], k + 1)
                    wait_apart(pe, s["S_made"], k + 1)
                    for hp in range(HP):
                        u = i * HP + hp
                        stacked(psW[i][:, u], U[:, u], vb[:, u], True, False)
                        last = stacked(psW[i][:, u], wtn[:, u], S[:, i, hp], False, True)
                    last.then_inc(s["vnew_ps"], 1)
                    pe.wait_ge(s["q_made"], m + 1)
                    wait_apart(pe, s["vnew_made"], k + 1)
                    each(of_chunk(psB, i), of_chunk(kd, i), vnew).then_inc(s["dS_ps"], 1)
                    for hp in range(HP):
                        u = i * HP + hp
                        bank = psU[i]
                        stacked(bank[:, u], qd[:, u], S[:, i, hp], True, False)
                        last = stacked(bank[:, u], attT[:, u], vnew[:, hp], False, True)
                    last.then_inc(s["o_ps"], 1)
                wait_apart(pe, s["o_made"], C2 * m + C2)
                each(psC, o_nat, c.ident2).then_inc(s["oT_ps"], 1)

            step(0)
            with pe.Fori(1, STEPS) as m:
                step(m)

        @block.scalar
        def _(act):
            def step(m):
                act.wait_ge(s["dve"], DV * m + DV_REL)
                act.activation(expo[:], expo[:], ACT.Exp).then_inc(s["small_exp"], 1)
                act.activation(rel[:], rel[:], ACT.Exp).then_inc(s["decayed"], 1)
                act.activation(qd[:], psA[:], ACT.Exp).then_inc(s["small_exp"], 1)
                act.wait_ge(s["W_ps"], m + 1)
                act.activation(W[:], psA[:], ACT.Copy).then_inc(s["W_made"], 1)
                for lv in range(1, LV + 1):
                    for i in range(C2):
                        act.wait_ge(s["M_ps"], C2 * (LV * m + lv - 1) + i + 1)
                        act.activation(of_chunk(M, i), of_chunk(psM[i], i), ACT.Copy).then_inc(s["M_made"], 1)
                for i in range(C2):
                    act.wait_ge(s["wt_ps"], C2 * m + i + 1)
                    act.activation(of_chunk(wtn, i), of_chunk(psM[i], i), ACT.Copy, scale=-1.0).then_inc(s["wt_made"], 1)
                for i in range(C2):
                    act.wait_ge(s["vnew_ps"], C2 * m + i + 1)
                    past(act, s["o_ps"], C2 * m + i)
                    act.activation(vnew[:], of_chunk(psW[i], i), ACT.Copy).then_inc(s["vnew_made"], 1)
                    act.wait_ge(s["o_ps"], C2 * m + i + 1)
                    act.activation(of_chunk(o_nat, i), of_chunk(psU[i], i), ACT.Copy).then_inc(s["o_made"], 1)

            step(0)
            with act.Fori(1, STEPS) as m:
                step(m)

        @block.vector
        def _(dve):
            def step(m):
                n = [0]

                def ordered(ins):
                    ins.then_inc(s["dve"], 1)
                    n[0] += 1

                def own(count):
                    dve.wait_ge(s["dve"], DV * m + count)

                dve.wait_ge(s["bcast"], m + 1)
                dve.wait_ge(s["cut"], 5 * m + 5)
                dve.tensor_tensor(diag[:, 0], psA[:], over(c.ident2[:]), ALU.mult)
                ordered(dve.tensor_tensor(diag[:, 1], psF[:], over(c.ident2[:]), ALU.mult))
                dve.tensor_tensor(kb[:], kc[:], psF[:], ALU.mult).then_inc(s["kb_made"], 1)
                own(DV_DIAG)
                ordered(dve.tensor_reduce(col[:], diag[:], AX_X, ALU.add))
                own(DV_COL)
                last_gc = psA[:, :, CH - 1]
                ordered(dve.tensor_copy(expo[:, 0, :], col[:, 0]))
                ordered(dve.tensor_tensor(expo[:, 1, :], last_gc, col[:, 0], ALU.subtract))
                ordered(dve.tensor_copy(expo[:, 2, :], last_gc))
                ordered(dve.tensor_tensor(rel[:], psA[:], bc(col[:, 0]), ALU.subtract))
                own(6)
                ordered(dve.tensor_scalar(rel[:], rel[:], 0.0, None, ALU.min))
                dve.wait_ge(s["decayed"], m + 1)
                ordered(dve.tensor_tensor(rel[:], rel[:], over(c.masks[:, 6]), ALU.mult))
                own(8)
                dve.wait_ge(s["scored"], m + 1)
                ordered(dve.tensor_tensor(at[:], psE[:], rel[:], ALU.mult))
                own(9)
                ordered(dve.tensor_tensor(lev[:, 0], at[:], over(c.masks[:, 0]), ALU.mult))
                own(10)
                dve.tensor_tensor(U[:], over(c.ident2[:]), lev[:, 0], ALU.subtract).then_inc(s["U_made"], 1)
                for lv in range(1, LV + 1):
                    last = dve.tensor_tensor(lev[:, lv], at[:], over(c.masks[:, lv]), ALU.mult)
                last.then_inc(s["lev_made"], 1)

                def rest():
                    ordered(dve.tensor_tensor(attT[:], psD[:], rel[:], ALU.mult))
                    dve.wait_ge(s["small_exp"], 2 * m + 2)
                    ordered(dve.tensor_tensor(bsc[:], col[:, 1], expo[:, 0, :], ALU.mult))
                    dve.tensor_tensor(qd[:], qc[:], qd[:], ALU.mult).then_inc(s["q_made"], 1)
                    yield
                    ordered(dve.tensor_tensor(kd[:], psB[:], bc(expo[:, 1, :]), ALU.mult))
                    ordered(dve.tensor_tensor(vb[:], psC[:], bc(col[:, 1]), ALU.mult))
                    yield
                    own(12)
                    dve.tensor_tensor(kbe[:], psB[:], bc(bsc[:]), ALU.mult).then_inc(s["kbe_made"], 1)
                    yield

                gaps = rest()
                for lv in range(1, LV + 1):
                    if lv <= 3:
                        next(gaps)
                    for i in range(C2):
                        dve.wait_ge(s["step_ps"], C2 * (LV * m + lv - 1) + i + 1)
                        if lv < LV:
                            dve.tensor_tensor(of_chunk(W, i), of_chunk(W, i), of_chunk(psW[i], i), ALU.subtract)
                        dve.tensor_tensor(of_chunk(U, i), of_chunk(U, i), of_chunk(psU[i], i),
                                          ALU.subtract).then_inc(taken[i], 1)
                for i in range(C2):
                    k = C2 * m + i
                    fade = bc(expo[:, 2, i * HP:(i + 1) * HP])
                    after = S[:, 1 - i]
                    past(dve, s["o_ps"], k)
                    dve.wait_ge(s["S_made"], k + 1)
                    dve.tensor_tensor(after, S[:, i], fade, ALU.mult).then_inc(s["S_faded"], 1)
                    dve.wait_ge(s["S_faded"], k + 1)
                    dve.wait_ge(s["dS_ps"], k + 1)
                    dve.tensor_tensor(after, after, of_chunk(psB, i), ALU.add).then_inc(s["S_made"], 1)
                dve.wait_ge(s["oT_ps"], m + 1)
                dve.tensor_copy(pair_of(qT, m), units(psC)).then_inc(s["oT_made"], 1)
                assert n[0] == DV, n

            dve.memset(S[:], 0.0).then_inc(s["S_made"], 1)
            step(0)
            with dve.Fori(1, STEPS) as m:
                step(m)


def attention_phase(core, a, obT):
    nc, c = core.nc, core
    NQ = T // P
    NB = DF_HEADS * NQ
    V, Q, K = range(3)
    NT = 3 * DF_HEADS
    SPREAD = [(V, 3), (V, 3), (V, 2), (Q, 3), (Q, 3), (Q, 2), (K, 4), (K, 4)]
    ENDS = {2: V, 5: Q, 7: K}

    def ending(b):
        h, part = (b + 1) // NQ + 1, (b + 1) % NQ
        return 3 * h + ENDS[part] if h < DF_HEADS and part in ENDS else None

    with ExitStack() as ctx:
        ring = Ring(c, ctx, 2)
        q, k = c.sb(ctx, "q", [P, 2, T]), c.sb(ctx, "k", [P, 2, T])
        v = c.sb(ctx, "v", [P, 2, NQ, P])
        bias = c.sb(ctx, "bias", [P, T])
        sc = c.sb(ctx, "scores", [P, 2, 2, T])
        pT = c.sb(ctx, "probs_t", [P, NQ, P])
        neg_max = c.sb(ctx, "neg_max", [P, 2, 2])
        total = c.sb(ctx, "total", [P, 2, 2])
        ps_s = c.ps(ctx, "ps_scores", [P, 2, NH, HALF])
        ps_p = c.ps(ctx, "ps_proj", [P, NH, HALF])
        ps_t = c.ps(ctx, "ps_turned", [P, 4, P])
        ps_o = c.ps(ctx, "ps_out", [P, HALF])
        s = {n: c.sem(n) for n in (
            "bias", "projected", "evacuated", "scored", "biased", "maxed", "negated", "exped", "combining",
            "combined", "turned", "taken", "o_ps", "o_made")}
        block = ctx.enter_context(nc.Block())
        kinds = [column_tiles(a["w_in"], off, DF_HEADS) for off in (OFF_V, OFF_Q, OFF_K)]
        flat = lambda x: x.rearrange("p h t -> p (h t)")
        keys = lambda b: (b % NQ + 1) * P
        groups = lambda b: b % NQ // 4 + 1
        fill, n_fills = {}, 0
        for g in range(2):
            fill["v", 0, g] = n_fills
            n_fills += 1
        for b in range(NB):
            for g in range(groups(b)):
                fill[b, g] = n_fills
                n_fills += 1
            if b % NQ == 3 and b // NQ + 1 < DF_HEADS:
                for g in range(2):
                    fill["v", b // NQ + 1, g] = n_fills
                    n_fills += 1

        @block.sync
        def _(sp):
            for t in range(NT):
                past(sp, ring.lo_made, t - 1)
                sp.dma_start(ring.raw[:, t % 2], kinds[t % 3][t // 3]).then_inc(ring.landed[t % 2], 16)

        @block.gpsimd
        def _(pool):
            pool.iota(bias[:], pattern=[[1, T]], base=-(T - P), channel_multiplier=-1,
                      allow_small_or_imprecise_dtypes=True).then_inc(s["bias"], 1)
            pool.wait_ge(s["bias"], 1)
            pool.affine_select(out=bias[:], in_=bias[:], compare_op=ALU.is_ge, fill=NEG, base=T - P,
                               pattern=[[-1, T]], channel_multiplier=1).then_inc(s["bias"], 1)

        @block.tensor
        def _(pe):
            def projection(t, d0, d1):
                if d0 == 0:
                    pe.wait_ge(ring.lo_made, t + 1)
                    past(pe, s["evacuated"], t)
                for d in range(d0, d1):
                    last = three_pass(pe, [ps_p[:, 0], ps_p[:, 1]], ring.hi[:, t % 2, d], ring.lo[:, t % 2, d],
                                      c.n_hi[:, d], c.n_lo[:, d], d == 0, d == DC - 1)
                if d1 == DC:
                    last.then_inc(s["projected"], 1)

            def turn(number, src, pieces):
                past(pe, s["taken"], number)
                for j in range(pieces):
                    last = pe.transpose(ps_t[:, j], src[:, j * P:(j + 1) * P], c.ident[:])
                last.then_inc(s["turned"], 1)

            def turn_v(h):
                pe.wait_ge(s["evacuated"], 3 * h + V + 1)
                for g in range(2):
                    turn(fill["v", h, g], q[:, h % 2, g * HALF:(g + 1) * HALF], 4)

            def scores(b):
                h, i, n = b // NQ, b % NQ, keys(b)
                pe.wait_ge(s["evacuated"], 3 * h + K + 1)
                past(pe, s["biased"], 2 * b)
                for m in range(2):
                    r = slice(m * HD, (m + 1) * HD)
                    for g in range((n + HALF - 1) // HALF):
                        w = min(HALF, n - g * HALF)
                        last = pe.matmul(ps_s[:, m, g, 0:w], q[r, h % 2, i * P:(i + 1) * P],
                                         k[r, h % 2, g * HALF:g * HALF + w], start=True, stop=True)
                last.then_inc(s["scored"], 1)

            projection(V, 0, DC)
            projection(Q, 0, 1)
            turn_v(0)
            projection(Q, 1, DC)
            def part_of_projections(number):
                h, part = number // NQ + 1, number % NQ
                if h < DF_HEADS:
                    kind, steps = SPREAD[part]
                    d0 = sum(n for kd, n in SPREAD[:part] if kd == kind)
                    projection(3 * h + kind, d0, d0 + steps)

            projection(K, 0, DC)
            scores(0)
            part_of_projections(0)
            scores(1)
            for b in range(NB):
                h, i = b // NQ, b % NQ
                part_of_projections(b + 1)
                if b + 2 < NB:
                    scores(b + 2)
                pe.wait_ge(s["combined"], b + 1)
                for g in range(groups(b)):
                    turn(fill[b, g], sc[:, b % 2, 0, g * HALF:], min(4, i + 1 - 4 * g))
                pe.wait_ge(s["taken"], fill[b, groups(b) - 1] + 1)
                past(pe, s["o_made"], b)
                for kb in range(i + 1):
                    last = pe.matmul(ps_o[:, 0:P], v[:, h % 2, kb], pT[:, kb], start=(kb == 0), stop=(kb == i))
                last.then_inc(s["o_ps"], 1)
                if i == 3 and h + 1 < DF_HEADS:
                    turn_v(h + 1)

        @block.scalar
        def _(act):
            def hi(t):
                if t < NT:
                    act.wait_ge(ring.landed[t % 2], 16 * (t // 2) + 16)
                    past(act, s["projected"], t - 1)
                    act.activation(ring.hi[:, t % 2], ring.raw[:, t % 2], ACT.Copy).then_inc(ring.hi_made, 1)

            def evacuate(t):
                h, kind = t // 3, t % 3
                act.wait_ge(s["projected"], t + 1)
                past(act, s["scored"], NQ * (h - 1))
                if kind == Q:
                    act.wait_ge(s["turned"], fill["v", h, 1] + 1)
                act.activation((q, q, k)[kind][:, h % 2], flat(ps_p[:]), ACT.Copy,
                               scale=HD ** -0.5 if kind == Q else 1.0).then_inc(s["evacuated"], 1)

            def exps(b):
                act.wait_ge(s["negated"], b + 1)
                for m in range(2):
                    x = sc[:, b % 2, m, 0:keys(b)]
                    act.activation(x, x, ACT.Exp, bias=neg_max[:, b % 2, m:m + 1],
                                   accum_out=total[:, b % 2, m:m + 1]).then_inc(s["exped"], 1)

            def take_out(b):
                h, i = b // NQ, b % NQ
                act.wait_ge(s["o_ps"], b + 1)
                act.activation(obT[:, h, i * P:(i + 1) * P], ps_o[:, 0:P], ACT.Copy).then_inc(s["o_made"], 1)

            hi(0)
            hi(1)
            for kind in range(3):
                evacuate(kind)
                hi(kind + 2)
            exps(0)
            for b in range(NB):
                h, i = b // NQ, b % NQ
                t = ending(b)
                if t and t % 3 == K:
                    evacuate(t)
                if b + 1 < NB:
                    exps(b + 1)
                if b:
                    take_out(b - 1)
                for g in range(groups(b)):
                    w = min(4, i + 1 - 4 * g)
                    act.wait_ge(s["turned"], fill[b, g] + 1)
                    past(act, s["o_ps"], b)
                    act.activation(pT[:, 4 * g:4 * g + w], ps_t[:, 0:w], ACT.Copy).then_inc(s["taken"], 1)
                if t:
                    if t % 3 != K:
                        evacuate(t)
                    hi(t + 2)
            take_out(NB - 1)

        @block.vector
        def _(dve):
            def lo(t):
                if t < NT:
                    dve.wait_ge(ring.hi_made, t + 1)
                    dve.tensor_tensor(ring.lo[:, t % 2], ring.raw[:, t % 2], ring.hi[:, t % 2].bitcast(F32),
                                      ALU.subtract).then_inc(ring.lo_made, 1)

            def take_v(h):
                past(dve, s["o_ps"], NQ * (h - 1))
                for g in range(2):
                    dve.wait_ge(s["turned"], fill["v", h, g] + 1)
                    dve.tensor_copy(v[:, h % 2, 4 * g:4 * g + 4], ps_t[:]).then_inc(s["taken"], 1)

            def bias_and_max(b):
                n, h = keys(b), b // NQ
                dve.wait_ge(s["scored"], b + 1)
                if b >= 2:
                    dve.wait_ge(s["turned"], fill[b - 2, groups(b - 2) - 1] + 1)
                for m in range(2):
                    dve.scalar_tensor_tensor(out=sc[:, b % 2, m, 0:n], in0=bias[:, T - n:T],
                                             scalar=c.slopes[:, h:h + 1], in1=flat(ps_s[:, m])[:, 0:n],
                                             op0=ALU.mult, op1=ALU.add).then_inc(s["biased"], 1)
                dve.wait_ge(s["biased"], 2 * b + 2)
                dve.tensor_reduce(neg_max[:, b % 2], sc[:, b % 2, :, 0:n], AX_X, ALU.max).then_inc(s["maxed"], 1)
                dve.wait_ge(s["maxed"], b + 1)
                dve.tensor_scalar(neg_max[:, b % 2], neg_max[:, b % 2], -1.0, None, ALU.mult).then_inc(s["negated"], 1)

            def combine(b):
                n, w = keys(b), total[:, b % 2]
                p1, p2 = sc[:, b % 2, 0, 0:n], sc[:, b % 2, 1, 0:n]
                dve.wait_ge(s["exped"], 2 * b + 2)
                dve.reciprocal(w, w).then_inc(s["combining"], 1)
                dve.wait_ge(s["combining"], 2 * b + 1)
                dve.tensor_scalar(p2, p2, w[:, 1:2], c.neg_lam[:], ALU.mult, ALU.mult).then_inc(s["combining"], 1)
                dve.wait_ge(s["combining"], 2 * b + 2)
                dve.scalar_tensor_tensor(out=p1, in0=p1, scalar=w[:, 0:1], in1=p2, op0=ALU.mult,
                                         op1=ALU.add).then_inc(s["combined"], 1)

            dve.wait_ge(s["bias"], 2)
            lo(0)
            lo(1)
            take_v(0)
            for kind in range(3):
                lo(kind + 2)
            bias_and_max(0)
            for b in range(NB):
                h, i = b // NQ, b % NQ
                if b + 1 < NB:
                    bias_and_max(b + 1)
                combine(b)
                if i == 3 and h + 1 < DF_HEADS:
                    take_v(h + 1)
                if ending(b):
                    lo(ending(b) + 2)


def branch_norm_phase(core, a, raw, lo_parts, hi_parts):
    nc, c = core.nc, core
    with ExitStack() as ctx:
        ring = Ring(c, ctx, 2)
        sq = c.sb(ctx, "squares", [P, T])
        root = c.sb(ctx, "root", [P, T])
        gate = c.sb(ctx, "silu_z", [P, T])
        val = c.sb(ctx, "value", [P, T])
        ps_z = c.ps(ctx, "ps_z", [P, NH, HALF])
        ps_s = c.ps(ctx, "ps_sum", [P, NH, HALF])
        s = {n: c.sem(n) for n in ("z_ps", "z_gate", "squared", "summed", "rooted", "dve", "value", "hi", "lo")}
        block = ctx.enter_context(nc.Block())
        flat = lambda x: x.rearrange("p h t -> p (h t)")
        z_tiles = column_tiles(a["w_in"], OFF_Z, HP)

        @block.sync
        def _(sp):
            for t in range(HP):
                past(sp, ring.lo_made, t - 1)
                sp.dma_start(ring.raw[:, t % 2], z_tiles[t]).then_inc(ring.landed[t % 2], 16)

        @block.tensor
        def _(pe):
            for t in range(HP):
                for b, ones in enumerate((c.head_ones, c.ones)):
                    j = 2 * t + b
                    pe.wait_ge(s["squared"], j + 1)
                    past(pe, s["rooted"], j)
                    for h in range(NH):
                        last = pe.matmul(ps_s[:, h], ones[:], sq[:, h * HALF:(h + 1) * HALF], start=True, stop=True)
                    last.then_inc(s["summed"], 1)
                    if b == 0:
                        pe.wait_ge(ring.lo_made, t + 1)
                        past(pe, s["z_gate"], t)
                        project(pe, c, ring, t % 2, [ps_z[:, 0], ps_z[:, 1]]).then_inc(s["z_ps"], 1)

        @block.scalar
        def _(act):
            def hi(t):
                act.wait_ge(ring.landed[t % 2], 16 * (t // 2) + 16)
                past(act, s["z_ps"], t - 1)
                act.activation(ring.hi[:, t % 2], ring.raw[:, t % 2], ACT.Copy).then_inc(ring.hi_made, 1)

            hi(0)
            hi(1)
            for t in range(HP):
                for b in range(2):
                    j = 2 * t + b
                    past(act, s["summed"], j)
                    act.activation(sq[:], raw[b][:, t, :], ACT.Square).then_inc(s["squared"], 1)
                    act.wait_ge(s["summed"], j + 1)
                    past(act, s["value"], j)
                    act.activation(root[:], flat(ps_s[:]), ACT.Sqrt, scale=1.0 / (HD if b == 0 else P),
                                   bias=c.eps[:, b:b + 1]).then_inc(s["rooted"], 1)
                    if b == 0:
                        act.wait_ge(s["z_ps"], t + 1)
                        past(act, s["value"], j - 1)
                        act.activation(gate[:], flat(ps_z[:]), ACT.Silu).then_inc(s["z_gate"], 1)
                        if t + 2 < HP:
                            hi(t + 2)
                    act.wait_ge(s["value"], j + 1)
                    act.activation(hi_parts[b][:, t, :], val[:], ACT.Copy).then_inc(s["hi"], 1)

        @block.vector
        def _(dve):
            def lo(t):
                dve.wait_ge(ring.hi_made, t + 1)
                dve.tensor_tensor(ring.lo[:, t % 2], ring.raw[:, t % 2], ring.hi[:, t % 2].bitcast(F32),
                                  ALU.subtract).then_inc(ring.lo_made, 1)

            lo(0)
            lo(1)
            steps = 0
            for t in range(HP):
                for b in range(2):
                    j = 2 * t + b
                    dve.wait_ge(s["rooted"], j + 1)
                    dve.reciprocal(root[:], root[:]).then_inc(s["dve"], 1)
                    steps += 1
                    dve.wait_ge(s["dve"], steps)
                    past(dve, s["lo"], j)
                    out = val[:]
                    ins = dve.scalar_tensor_tensor(out=out, in0=raw[b][:, t, :], scalar=c.branch_gain[:, b:b + 1],
                                                   in1=root[:], op0=ALU.mult, op1=ALU.mult)
                    if b == 0:
                        ins.then_inc(s["dve"], 1)
                        steps += 1
                        dve.wait_ge(s["dve"], steps)
                        dve.wait_ge(s["z_gate"], t + 1)
                        ins = dve.tensor_tensor(out, out, gate[:], ALU.mult)
                    ins.then_inc(s["value"], 1)
                    dve.wait_ge(s["hi"], j + 1)
                    dve.tensor_tensor(lo_parts[b][:, t, :], val[:], hi_parts[b][:, t, :].bitcast(F32),
                                      ALU.subtract).then_inc(s["lo"], 1)
                    if b == 0 and t + 2 < HP:
                        lo(t + 2)


def merge_phase(core, a, o_hi, o_lo):
    nc, c = core.nc, core
    with ExitStack() as ctx:
        ring = Ring(c, ctx, 2)
        ga = c.sb(ctx, "gated_a", [P, T])
        gb = c.sb(ctx, "gated_b", [P, T])
        m_hi = c.sb(ctx, "merged_hi", [P, T], F32R)
        m_lo = c.sb(ctx, "merged_lo", [P, T], F32R)
        ps_y = c.ps(ctx, "ps_y", [P, 2, NH, HALF])
        ps_g = c.ps(ctx, "ps_gate", [P, NH, HALF])
        ps_d = c.ps(ctx, "ps_out", [P, NH, HALF])
        s = {n: c.sem(n) for n in ("branches", "gates", "sig", "mul", "m_hi", "m_lo", "out_ps", "added")}
        block = ctx.enter_context(nc.Block())
        flat = lambda x: x.rearrange("p h t -> p (h t)")
        gates_a = column_tiles(a["w_in"], OFF_G, DC)
        gates_b = column_tiles(a["w_in"], OFF_G + D_MODEL, DC)
        br = [w[0].rearrange("(k p) (f c) -> f p k c", p=P, c=P) for w in (a["w_branch_a"], a["w_branch_b"])]
        w_out = a["w_out"][0].rearrange("(f p) (k c) -> f p k c", p=P, c=P)
        KB = DN_W // P
        BR, OUT, GA, GB = range(4)
        NO = DC * NH

        def number(d, kind):
            if isinstance(d, int) and d == 0:
                return {BR: 0, GA: 1, GB: 2}[kind]
            return 4 * d - 1 + kind

        def place(d, kind):
            if isinstance(d, int) and d == 0:
                return {BR: (0, 32), GA: (1, 16), GB: (0, 48)}[kind]
            return {BR: (1, 48 * d), OUT: (0, 32 * d + 32), GA: (1, 48 * d + 16), GB: (0, 32 * d + 48)}[kind]

        @block.sync
        def _(sp):
            def load(d, kind, src):
                slot, _ = place(d, kind)
                past(sp, ring.lo_made, number(d, kind) - 1)
                if kind == BR:
                    for b in range(2):
                        sp.dma_start(ring.raw[:, slot, b * KB:(b + 1) * KB], br[b][d]).then_inc(ring.landed[slot], 16)
                else:
                    sp.dma_start(ring.raw[:, slot], src).then_inc(ring.landed[slot], 16)

            load(0, BR, None)
            load(0, GA, gates_a[0])
            load(0, GB, gates_b[0])
            with sp.Fori(1, DC) as d:
                load(d, BR, None)
                load(d, OUT, w_out[d - 1])
                load(d, GA, gates_a[d])
                load(d, GB, gates_b[d])
            sp.wait_ge(ring.lo_made, 4 * DC - 2)
            sp.dma_start(ring.raw[:, 1], w_out[DC - 1]).then_inc(ring.landed[1], 16)

        @block.scalar
        def _(act):
            def split(slot, landed):
                act.wait_ge(ring.landed[slot], landed)
                act.activation(ring.hi[:, slot], ring.raw[:, slot], ACT.Copy).then_inc(ring.hi_made, 1)

            def hi(d, kind):
                if kind == BR:
                    past(act, s["gates"], 2 * d - 1)
                elif kind == OUT:
                    act.wait_ge(s["gates"], 2 * d)
                elif kind == GA:
                    past(act, s["branches"], d + 1 if not (isinstance(d, int) and d == 0) else 0)
                elif isinstance(d, int) and d == 0:
                    act.wait_ge(s["branches"], 1)
                else:
                    act.wait_ge(s["out_ps"], NO * d)
                split(*place(d, kind))

            def gate(d, b, dst):
                act.wait_ge(s["gates"], 2 * d + b + 1)
                past(act, s["m_lo"], d)
                act.activation(dst[:], flat(ps_g[:]), ACT.Sigmoid).then_inc(s["sig"], 1)

            def merged(d):
                act.wait_ge(s["mul"], 3 * d + 3)
                past(act, s["out_ps"], NO * d)
                act.activation(m_hi[:], ga[:], ACT.Copy).then_inc(s["m_hi"], 1)

            hi(0, BR)
            hi(0, GA)
            hi(0, GB)
            gate(0, 0, ga)
            hi(1, BR)
            gate(0, 1, gb)
            hi(1, OUT)
            merged(0)

            def chunk(d, last=False):
                hi(d, GA)
                hi(d, GB)
                gate(d, 0, ga)
                if not last:
                    hi(d + 1, BR)
                else:
                    split(1, 48 * DC - 16)
                gate(d, 1, gb)
                if not last:
                    hi(d + 1, OUT)
                merged(d)

            with act.Fori(1, DC - 1) as d:
                chunk(d)
            chunk(DC - 1, True)

        @block.vector
        def _(dve):
            def lo(t, slot):
                dve.wait_ge(ring.hi_made, t + 1)
                dve.tensor_tensor(ring.lo[:, slot], ring.raw[:, slot], ring.hi[:, slot].bitcast(F32),
                                  ALU.subtract).then_inc(ring.lo_made, 1)

            def gated(d, b, dst):
                dve.wait_ge(s["sig"], 2 * d + b + 1)
                dve.tensor_tensor(dst[:], dst[:], flat(ps_y[:, b]), ALU.mult).then_inc(s["mul"], 1)

            def merged(d):
                dve.wait_ge(s["mul"], 3 * d + 2)
                dve.tensor_tensor(ga[:], ga[:], gb[:], ALU.add).then_inc(s["mul"], 1)

            def merged_lo(d):
                dve.wait_ge(s["m_hi"], d + 1)
                dve.tensor_tensor(m_lo[:], ga[:], m_hi[:].bitcast(F32), ALU.subtract).then_inc(s["m_lo"], 1)

            def add_out(d):
                for e in range(DC):
                    for h in range(NH):
                        dve.wait_ge(s["out_ps"], NO * d + NH * e + h + 1)
                        x = c.xT[:, e, h * HALF:(h + 1) * HALF]
                        dve.tensor_tensor(x, x, ps_d[:, h], ALU.add).then_inc(s["added"], 1)

            lo(0, 0)
            lo(1, 1)
            lo(2, 0)
            gated(0, 0, ga)
            lo(number(1, BR), 1)
            gated(0, 1, gb)
            merged(0)
            lo(number(1, OUT), 0)
            merged_lo(0)

            def chunk(d, last=False):
                lo(4 * d + 1, 1)
                add_out(d - 1)
                lo(4 * d + 2, 0)
                gated(d, 0, ga)
                lo(4 * d + 3, 1)
                gated(d, 1, gb)
                merged(d)
                if not last:
                    lo(4 * d + 4, 0)
                merged_lo(d)

            with dve.Fori(1, DC - 1) as d:
                chunk(d)
            chunk(DC - 1, True)
            add_out(DC - 1)

        @block.tensor
        def _(pe):
            def branches(d):
                slot, _ = place(d, BR)
                pe.wait_ge(ring.lo_made, number(d, BR) + 1)
                past(pe, s["mul"], 3 * d)
                for b in range(2):
                    for k in range(KB):
                        last = three_pass(pe, [ps_y[:, b, 0], ps_y[:, b, 1]], ring.hi[:, slot, b * KB + k],
                                          ring.lo[:, slot, b * KB + k], o_hi[b][:, k], o_lo[b][:, k],
                                          k == 0, k == KB - 1)
                last.then_inc(s["branches"], 1)

            def gate(d, b):
                slot, _ = place(d, (GA, GB)[b])
                pe.wait_ge(ring.lo_made, number(d, (GA, GB)[b]) + 1)
                past(pe, s["sig"], 2 * d + b)
                project(pe, c, ring, slot, [ps_g[:, 0], ps_g[:, 1]]).then_inc(s["gates"], 1)

            def out(d, t, slot):
                pe.wait_ge(ring.lo_made, t + 1)
                pe.wait_ge(s["m_lo"], d + 1)
                for e in range(DC):
                    for h in range(NH):
                        past(pe, s["added"], NO * d + NH * e + h - 1)
                        hs = slice(h * HALF, (h + 1) * HALF)
                        pe.matmul(ps_d[:, h], ring.hi[:, slot, e], m_hi[:, hs], start=True, stop=False)
                        pe.matmul(ps_d[:, h], ring.hi[:, slot, e], m_lo[:, hs], start=False, stop=False)
                        pe.matmul(ps_d[:, h], ring.lo[:, slot, e], m_hi[:, hs], start=False,
                                  stop=True).then_inc(s["out_ps"], 1)

            branches(0)
            gate(0, 0)
            gate(0, 1)
            branches(1)
            out(0, 4, 0)
            gate(1, 0)
            gate(1, 1)
            with pe.Fori(2, DC) as d:
                branches(d)
                out(d - 1, 4 * d, 0)
                gate(d, 0)
                gate(d, 1)
            out(DC - 1, 4 * DC - 1, 1)


def mixer(core, a):
    nc, c = core.nc, core
    with ExitStack() as ctx:
        SH = [P, HP, T]
        q_hi, qT = c.sb_shared(ctx, "oa", SH)
        with ExitStack() as dn:
            kT, vT = c.sb(dn, "kT", SH), c.sb(dn, "vT", SH)
            gc_beta = c.sb(dn, "gc_beta", [BETA_ROW + 2 * DN_HEADS, T])
            gc, beta = gc_beta[0:2 * DN_HEADS, :], gc_beta[BETA_ROW:, :]
            dn_project_phase(c, a, [qT, kT, vT], gc, beta)
            core.end_phase()
            dn_phase(c, [qT, kT, vT], gc, beta)
            core.end_phase()
        b_hi, obT = c.sb_shared(ctx, "ob", SH)
        attention_phase(c, a, obT)
        core.end_phase()
        a_lo, b_lo = c.sb(ctx, "oa_lo", SH, F32R), c.sb(ctx, "ob_lo", SH, F32R)
        branch_norm_phase(c, a, [qT, obT], [a_lo, b_lo], [q_hi, b_hi])
        core.end_phase()
        merge_phase(c, a, [q_hi, b_hi], [a_lo, b_lo])
        core.end_phase()


def build(nc, a, out):
    with ExitStack() as ctx:
        core = Core(nc, ctx)
        setup_phase(core, a)
        core.end_phase()
        norm_phase(core, 0)
        core.end_phase()
        ffn_phase(core, a["ffn1_w_gate"], a["ffn1_w_up"], a["ffn1_w_down"])
        core.end_phase()
        norm_phase(core, 1)
        core.end_phase()
        mixer_setup(core, a)
        core.end_phase()
        mixer(core, a)
        norm_phase(core, 2)
        core.end_phase()
        ffn_phase(core, a["ffn2_w_gate"], a["ffn2_w_up"], a["ffn2_w_down"])
        core.end_phase()
        norm_phase(core, 3, out)
        core.end_phase()


_INS = ["x", "ffn1_norm", "ffn1_w_gate", "ffn1_w_up", "ffn1_w_down", "mix_norm", "w_in", "conv_qkv",
        "dn_a_log", "dn_dt_bias", "dn_out_norm", "diff_lambda_q1", "diff_lambda_k1", "diff_lambda_q2",
        "diff_lambda_k2", "diff_subln", "w_branch_a", "w_branch_b", "w_out", "ffn2_norm", "ffn2_w_gate",
        "ffn2_w_up", "ffn2_w_down", "final_norm"]


def kernel(**inputs):
    import numpy as np
    import concourse.bacc as bacc
    from concourse.bass_utils import run_bass_kernel_spmd

    nc = bacc.Bacc("TRN2", target_bir_lowering=False, num_devices=1)
    arrays, handles = {}, {}
    for name in _INS:
        arr = np.ascontiguousarray(inputs[name])
        arrays[f"in_{name}"] = arr
        handles[name] = nc.dram_tensor(f"in_{name}", arr.shape, mybir.dt.from_np(arr.dtype),
                                       kind="ExternalInput").ap()
    out = nc.dram_tensor("y_out", (1, T, D_MODEL), F32, kind="ExternalOutput").ap()
    build(nc, handles, out)
    res = run_bass_kernel_spmd(nc, [arrays], core_ids=[0])
    return res.results[0]["y_out"]
```

```python
from contextlib import ExitStack

import concourse.bass as bass
from concourse import mybir

F32 = mybir.dt.float32
F32R = mybir.dt.float32r
ACT = mybir.ActivationFunctionType
ALU = mybir.AluOpType
AX_X = mybir.AxisListType.X

P = 128
D_MODEL = 1024
T = 1024
DC = D_MODEL // P
HALF = 512
NH = T // HALF
D_FF = 2816
FC = D_FF // P
HD = 64
DN_HEADS = 8
HP = DN_HEADS // 2
DN_W = DN_HEADS * HD
CH = 64
NCH = T // CH
DF_HEADS = 4
CONV = 4
RMS_EPS = 1e-6
SUBLN_EPS = 1e-5
L2_EPS = 1e-6
LAM_INIT = 0.8 - 0.6
OFF_Z = 3 * DN_W
OFF_AB = OFF_Z + DN_W
OFF_Q = OFF_AB + 2 * DN_HEADS
OFF_K = OFF_Q + DF_HEADS * P
OFF_V = OFF_K + DF_HEADS * P
OFF_G = OFF_V + DF_HEADS * P
NEG = -3.0e38
BETA_ROW = 32


class Core:

    def __init__(self, nc, ctx):
        self.nc = nc
        self.ctx = ctx
        self.n = 0
        self.sems = []

    def sb(self, ctx, name, shape, dt=F32):
        self.n += 1
        return ctx.enter_context(self.nc.sbuf_tensor(f"{name}_{self.n}", shape, dt))

    def sb_shared(self, ctx, name, shape):
        split = self.sb(ctx, f"{name}_hi", shape, F32R)
        size = 4
        for s in shape[1:]:
            size *= s
        return split, self.nc.alloc_sbuf_tensor_at(f"{name}_raw_{self.n}", shape, F32,
                                                   offset=self.nc.sbuf_base - size)

    def ps(self, ctx, name, shape):
        self.n += 1
        return ctx.enter_context(self.nc.psum_tensor(f"{name}_{self.n}", shape, F32))

    def sem(self, name):
        self.n += 1
        self.sems.append(self.nc.alloc_semaphore(name=f"{name}_{self.n}"))
        return self.sems[-1]

    def end_phase(self):
        self.nc.clear_and_free_semaphores(self.sems)
        self.nc.all_engine_barrier()
        self.sems = []


def three_pass(pe, banks, w_hi, w_lo, x_hi, x_lo, start, stop):
    for h, bank in enumerate(banks):
        pe.matmul(bank, w_hi, x_hi[:, h * HALF:(h + 1) * HALF], start=start, stop=False)
    for h, bank in enumerate(banks):
        pe.matmul(bank, w_hi, x_lo[:, h * HALF:(h + 1) * HALF], start=False, stop=False)
    for h, bank in enumerate(banks):
        last = pe.matmul(bank, w_lo, x_hi[:, h * HALF:(h + 1) * HALF], start=False, stop=stop)
    return last


class Ring:

    def __init__(self, core, ctx, depth):
        self.depth = depth
        self.raw = core.sb(ctx, "w_raw", [P, depth, DC, P])
        self.hi = core.sb(ctx, "w_hi", [P, depth, DC, P], F32R)
        self.lo = core.sb(ctx, "w_lo", [P, depth, DC, P], F32R)
        self.landed = [core.sem(f"w_landed{s}") for s in range(depth)]
        self.hi_made = core.sem("w_hi_made")
        self.lo_made = core.sem("w_lo_made")


def setup_phase(core, a):
    nc = core.nc
    c = core
    per = core.ctx
    c.xT = c.sb(per, "xT", [P, DC, T])
    c.n_hi = c.sb(per, "n_hi", [P, DC, T], F32R)
    c.n_lo, c.n_raw = c.sb_shared(per, "n_lo", [P, DC, T])
    c.ident = c.sb(per, "ident", [P, P])
    c.ones = c.sb(per, "ones", [P, P])
    c.head_ones = c.sb(per, "head_ones", [P, P])
    c.ident2 = c.sb(per, "ident2", [P, CH])
    c.gains = c.sb(per, "gains", [P, 4, DC])
    c.eps = c.sb(per, "eps", [P, 2])

    gains_in = c.sem("gains_loaded")
    zeroed = c.sem("consts_zeroed")
    made = c.sem("consts_made")
    turned = c.sem("x_turned")
    taken = c.sem("x_taken")
    with ExitStack() as ctx:
        mixer_part = mixer_setup(core, a, ctx)
        xin = c.sb(ctx, "x_in", [P, 2, D_MODEL])
        xps = c.ps(ctx, "x_ps", [P, 4, HALF])
        slot_in = [c.sem("x_in_slot0"), c.sem("x_in_slot1")]
        block = ctx.enter_context(nc.Block())
        xrows = a["x"].rearrange("b (t p) d -> (b t) p d", p=P)

        @block.sync
        def _(sp):
            for i, name in enumerate(("ffn1_norm", "mix_norm", "ffn2_norm")):
                sp.dma_start(c.gains[:, i, :], a[name].rearrange("l (c p) -> p (l c)", p=P),
                             allow_slow_non_contiguous=True).then_inc(gains_in, 16)
            sp.dma_start(c.gains[:, 3, :], a["final_norm"].rearrange("(c p) -> p c", p=P),
                             allow_slow_non_contiguous=True).then_inc(gains_in, 16)
            for t in range(T // P):
                if t >= 2:
                    sp.wait_ge(turned, 2 * (t - 1))
                sp.dma_start(xin[:, t % 2, :], xrows[t]).then_inc(slot_in[t % 2], 16)
            sp.wait_ge(gains_in, 64)

        @block.gpsimd
        def _(pool):
            pool.memset(c.ident[:], 0.0).then_inc(zeroed, 1)
            pool.memset(c.ones[:], 1.0).then_inc(zeroed, 1)
            pool.memset(c.eps[:, 0:1], RMS_EPS).then_inc(zeroed, 1)
            pool.memset(c.eps[:, 1:2], SUBLN_EPS).then_inc(zeroed, 1)
            pool.memset(c.head_ones[:], 0.0).then_inc(zeroed, 1)
            pool.wait_ge(zeroed, 5)
            pool.affine_select(out=c.ident[:], in_=c.ident[:], compare_op=ALU.not_equal, fill=1.0, base=0,
                               pattern=[[-1, P]], channel_multiplier=1).then_inc(made, 1)
            mixer_part["gpsimd"](pool)

        @block.scalar
        def _(act):
            mixer_part["scalar"](act)

        @block.tensor
        def _(pe):
            pe.wait_ge(made, 1)
            for t in range(T // P):
                pe.wait_ge(slot_in[t % 2], 16 * (t // 2 + 1))
                for g in range(2):
                    k = 2 * t + g
                    if k >= 4:
                        pe.wait_ge(taken, k - 3)
                    for j in range(4):
                        d = 4 * g + j
                        last = pe.transpose(xps[:, k % 4, j * P:(j + 1) * P],
                                            xin[:, t % 2, d * P:(d + 1) * P], c.ident[:])
                    last.then_inc(turned, 1)
            mixer_part["tensor"](pe)

        @block.vector
        def _(dve):
            mixer_part["clear"](dve)
            dve.wait_ge(zeroed, 5)
            for h in range(2):
                dve.memset(c.head_ones[h * HD:(h + 1) * HD, h * HD:(h + 1) * HD], 1.0)
            dve.wait_ge(made, 1)
            dve.tensor_tensor(c.ident2[:], c.ident[:, 0:CH], c.ident[:, CH:P], ALU.add)
            for t in range(T // P):
                for g in range(2):
                    k = 2 * t + g
                    dve.wait_ge(turned, k + 1)
                    dve.tensor_copy(c.xT[:, 4 * g:4 * g + 4, t * P:(t + 1) * P],
                                    xps[:, k % 4, :].rearrange("p (j q) -> p j q", j=4)).then_inc(taken, 1)
            mixer_part["vector"](dve)


class Norm:

    def __init__(self, core, which, rstd, ss, split=True):
        self.core, self.gain, self.rstd, self.ss, self.split = core, core.gains[:, which, :], rstd, ss, split
        self.squared = core.sem("squared")
        self.paired = core.sem("squares_paired")
        self.summed = core.sem("squares_summed")
        self.rooted = core.sem("rooted")
        self.inverted = core.sem("inverted")
        self.scaled = core.sem("scaled")
        self.hi_made = core.sem("n_hi_made")
        self.lo_made = [core.sem("n_lo_even_made"), core.sem("n_lo_odd_made")]

    def squares(self, act):
        for k in range(DC):
            act.activation(self.core.n_raw[:, k, :], self.core.xT[:, k, :], ACT.Square).then_inc(self.squared, 1)

    def root(self, act):
        act.wait_ge(self.summed, 1)
        act.activation(self.rstd[:], self.ss.rearrange("p h t -> p (h t)"), ACT.Sqrt, scale=1.0 / D_MODEL,
                       bias=self.core.eps[:, 0:1]).then_inc(self.rooted, 1)

    def hi_parts(self, act):
        for k in range(DC):
            act.wait_ge(self.scaled, k + 1)
            act.activation(self.core.n_hi[:, k, :], self.core.n_raw[:, k, :], ACT.Copy).then_inc(self.hi_made, 1)

    def pairs(self, dve):
        for k in range(0, DC, 2):
            dve.wait_ge(self.squared, k + 2)
            x = self.core.n_raw[:, k, :]
            dve.tensor_tensor(x, x, self.core.n_raw[:, k + 1, :], ALU.add).then_inc(self.paired, 1)

    def sums(self, pe):
        for k in range(0, DC, 2):
            pe.wait_ge(self.paired, k // 2 + 1)
            for h in range(NH):
                last = pe.matmul(self.ss[:, h, :], self.core.ones[:], self.core.n_raw[:, k, h * HALF:(h + 1) * HALF],
                                 start=(k == 0), stop=(k == DC - 2))
        last.then_inc(self.summed, 1)

    def scale(self, dve):
        c = self.core
        dve.wait_ge(self.rooted, 1)
        dve.reciprocal(self.rstd[:], self.rstd[:]).then_inc(self.inverted, 1)
        dve.wait_ge(self.inverted, 1)
        for k in range(DC):
            dve.scalar_tensor_tensor(out=c.n_raw[:, k, :], in0=c.xT[:, k, :], scalar=self.gain[:, k:k + 1],
                                     in1=self.rstd[:], op0=ALU.mult, op1=ALU.mult).then_inc(self.scaled, 1)
            if self.split and k % 2:
                self.lo_part(dve, k - 1)

    def lo_part(self, engine, k):
        c = self.core
        engine.wait_ge(self.hi_made, k + 1)
        engine.tensor_tensor(c.n_lo[:, k, :], c.n_raw[:, k, :], c.n_hi[:, k, :].bitcast(F32),
                             ALU.subtract).then_inc(self.lo_made[k % 2], 1)

    def odd_lo_parts(self, pool):
        for k in range(1, DC, 2):
            self.lo_part(pool, k)

    def wait_chunk(self, pe, k):
        pe.wait_ge(self.lo_made[k % 2], k // 2 + 1)


def output_phase(core, which, out):
    nc, c = core.nc, core
    turned = c.sem("y_turned")
    copied = c.sem("y_copied_even")
    copied_act = c.sem("y_copied_odd")
    with ExitStack() as ctx:
        rstd = c.sb(ctx, "rstd", [P, T])
        ss = c.ps(ctx, "ss", [P, NH, HALF])
        y = c.sb(ctx, "y", [P, 2, D_MODEL])
        yps = c.ps(ctx, "yps", [P, 4, HALF])
        slot_out = [c.sem("y_out0"), c.sem("y_out1")]
        norm = Norm(c, which, rstd, ss[:], split=False)
        block = ctx.enter_context(nc.Block())
        orow = out.rearrange("b (t p) d -> (b t) p d", p=P)

        @block.scalar
        def _(act):
            norm.squares(act)
            norm.root(act)
            for t in range(T // P):
                k = 2 * t + 1
                if t >= 2:
                    act.wait_ge(slot_out[t % 2], 16 * (t // 2))
                act.wait_ge(turned, k + 1)
                act.activation(y[:, t % 2, HALF:], yps[:, k % 4, :], ACT.Copy).then_inc(copied_act, 1)

        @block.tensor
        def _(pe):
            norm.sums(pe)
            pe.wait_ge(norm.scaled, DC)
            for t in range(T // P):
                for g in range(2):
                    k = 2 * t + g
                    past(pe, (copied, copied_act)[g], t - 1)
                    for j in range(4):
                        last = pe.transpose(yps[:, k % 4, j * P:(j + 1) * P],
                                            c.n_raw[:, 4 * g + j, t * P:(t + 1) * P], c.ident[:])
                    last.then_inc(turned, 1)

        @block.vector
        def _(dve):
            norm.pairs(dve)
            norm.scale(dve)
            for t in range(T // P):
                k = 2 * t
                if t >= 2:
                    dve.wait_ge(slot_out[t % 2], 16 * (t // 2))
                dve.wait_ge(turned, k + 1)
                dve.tensor_copy(y[:, t % 2, 0:HALF], yps[:, k % 4, :]).then_inc(copied, 1)

        @block.sync
        def _(sp):
            for t in range(T // P):
                sp.wait_ge(copied, t + 1)
                sp.wait_ge(copied_act, t + 1)
                sp.dma_start(orow[t], y[:, t % 2, :]).then_inc(slot_out[t % 2], 16)
            sp.wait_ge(slot_out[0], 16 * (T // P // 2))
            sp.wait_ge(slot_out[1], 16 * (T // P // 2))


def ffn_phase(core, which, w_gate, w_up, w_down):
    nc, c = core.nc, core
    PAIRS = FC // 2
    with ExitStack() as ctx:
        ring = Ring(c, ctx, 3)
        sg = c.sb(ctx, "silu_gate", [P, T])
        h_raw = c.sb(ctx, "h_raw", [P, 2, T])
        h_hi = c.sb(ctx, "h_hi", [P, 2, T], F32R)
        h_lo = c.sb(ctx, "h_lo", [P, 2, T], F32R)
        ps_g = c.ps(ctx, "ps_gate", [P, NH, HALF])
        ps_u = c.ps(ctx, "ps_up", [P, NH, HALF])
        ps_d = c.ps(ctx, "ps_down", [P, 2, NH, HALF])
        product_done = c.sem("product_done")
        silu_done = c.sem("silu_done")
        h_made = c.sem("h_made")
        h_hi_made = c.sem("h_hi_made")
        h_lo_made = c.sem("h_lo_made")
        down_done = c.sem("down_done")
        added = c.sem("added")
        norm = Norm(c, which, sg, ps_u[:])
        block = ctx.enter_context(nc.Block())
        cols = lambda w: w.rearrange("l (k p) (f c) -> (l f) p k c", p=P, c=P)
        gate_t, up_t = cols(w_gate), cols(w_up)
        down_t = w_down.rearrange("l (f p) (k c) -> (l f) p k c", p=P, c=P)
        slot = lambda k: (k - 2) % 3
        rnd = lambda i, k: 2 * i + (k - 2) // 3
        tile = lambda i, k: 6 * i - 2 + k

        @block.sync
        def _(sp):
            def load(i, k, src, first=False):
                if not first:
                    sp.wait_ge(ring.lo_made, tile(i, k) - 2)
                sp.dma_start(ring.raw[:, slot(k)], src).then_inc(ring.landed[slot(k)], 16)

            load(0, 2, gate_t[0], True)
            load(0, 3, up_t[0], True)
            load(0, 4, gate_t[1], True)
            load(0, 5, up_t[1])
            with sp.Fori(1, PAIRS) as i:
                load(i, 0, gate_t[2 * i])
                load(i, 1, down_t[2 * i - 2])
                load(i, 2, down_t[2 * i - 1])
                load(i, 3, up_t[2 * i])
                load(i, 4, gate_t[2 * i + 1])
                load(i, 5, up_t[2 * i + 1])
            load(PAIRS, 0, down_t[FC - 2])
            load(PAIRS, 1, down_t[FC - 1])

        @block.gpsimd
        def _(pool):
            norm.odd_lo_parts(pool)

        @block.scalar
        def _(act):
            def hi(i, k, first=False):
                act.wait_ge(ring.landed[slot(k)], 16 * (rnd(i, k) + 1))
                if k >= 4 and not first:
                    act.wait_ge(down_done, DC * i)
                elif not first:
                    act.wait_ge(product_done, 4 * i + {0: -2, 1: -1, 2: 0, 3: 1}[k])
                act.activation(ring.hi[:, slot(k)], ring.raw[:, slot(k)], ACT.Copy).then_inc(ring.hi_made, 1)

            def silu(i, j):
                act.wait_ge(product_done, 4 * i + 2 * j + 1)
                if j or not (isinstance(i, int) and i == 0):
                    act.wait_ge(h_made, 2 * i + j)
                act.activation(sg[:], ps_g[:].rearrange("p h t -> p (h t)"), ACT.Silu).then_inc(silu_done, 1)

            def h_split(i, j):
                act.wait_ge(h_made, 2 * i + j + 1)
                act.activation(h_hi[:, j, :], h_raw[:, j, :], ACT.Copy).then_inc(h_hi_made, 1)

            norm.squares(act)
            hi(0, 2, True)
            norm.root(act)
            hi(0, 3, True)
            hi(0, 4, True)
            norm.hi_parts(act)
            silu(0, 0)
            act.wait_ge(product_done, 1)
            hi(0, 5, True)
            h_split(0, 0)
            hi(1, 0)
            silu(0, 1)
            hi(1, 1)

            def pair(i):
                hi(i, 2)
                h_split(i - 1, 1)
                hi(i, 3)
                silu(i, 0)
                hi(i, 4)
                hi(i, 5)
                h_split(i, 0)
                hi(i + 1, 0)
                silu(i, 1)
                hi(i + 1, 1)

            with act.Fori(1, PAIRS) as i:
                pair(i)
            h_split(PAIRS - 1, 1)

        @block.vector
        def _(dve):
            def lo(i, k):
                dve.wait_ge(ring.hi_made, tile(i, k) + 1)
                dve.tensor_tensor(ring.lo[:, slot(k)], ring.raw[:, slot(k)], ring.hi[:, slot(k)].bitcast(F32),
                                  ALU.subtract).then_inc(ring.lo_made, 1)

            def gated(i, j):
                dve.wait_ge(silu_done, 2 * i + j + 1)
                dve.wait_ge(product_done, 4 * i + 2 * j + 2)
                dve.tensor_tensor(h_raw[:, j, :], sg[:], ps_u[:].rearrange("p h t -> p (h t)"),
                                  ALU.mult).then_inc(h_made, 1)

            def h_rest(i, j):
                dve.wait_ge(h_hi_made, 2 * i + j + 1)
                dve.tensor_tensor(h_lo[:, j, :], h_raw[:, j, :], h_hi[:, j, :].bitcast(F32),
                                  ALU.subtract).then_inc(h_lo_made, 1)

            def add_down(i):
                for d in range(DC):
                    dve.wait_ge(down_done, DC * i + d + 1)
                    dve.scalar_tensor_tensor(out=c.xT[:, d, :], in0=ps_d[:, d % 2].rearrange("p h t -> p (h t)"),
                                             scalar=0.5, in1=c.xT[:, d, :], op0=ALU.mult,
                                             op1=ALU.add).then_inc(added, 1)

            norm.pairs(dve)
            lo(0, 2)
            norm.scale(dve)
            lo(0, 3)
            lo(0, 4)
            lo(0, 5)
            gated(0, 0)
            h_rest(0, 0)
            lo(1, 0)
            lo(1, 1)

            def pair(i):
                gated(i - 1, 1)
                lo(i, 2)
                h_rest(i - 1, 1)
                lo(i, 3)
                add_down(i - 1)
                lo(i, 4)
                lo(i, 5)
                gated(i, 0)
                h_rest(i, 0)
                lo(i + 1, 0)
                lo(i + 1, 1)

            with dve.Fori(1, PAIRS) as i:
                pair(i)
            gated(PAIRS - 1, 1)
            h_rest(PAIRS - 1, 1)
            add_down(PAIRS - 1)

        @block.tensor
        def _(pe):
            def gate(i, k, j, first=False):
                if not first:
                    pe.wait_ge(silu_done, 2 * i + j)
                pe.wait_ge(ring.lo_made, tile(i, k) + 1)
                for d in range(DC):
                    if first:
                        norm.wait_chunk(pe, d)
                    last = three_pass(pe, [ps_g[:, 0], ps_g[:, 1]], ring.hi[:, slot(k), d], ring.lo[:, slot(k), d],
                                      c.n_hi[:, d], c.n_lo[:, d], d == 0, d == DC - 1)
                last.then_inc(product_done, 1)

            def up(i, k, j, first=False):
                if not first:
                    pe.wait_ge(h_made, 2 * i + j)
                pe.wait_ge(ring.lo_made, tile(i, k) + 1)
                for d in range(DC):
                    last = three_pass(pe, [ps_u[:, 0], ps_u[:, 1]], ring.hi[:, slot(k), d], ring.lo[:, slot(k), d],
                                      c.n_hi[:, d], c.n_lo[:, d], d == 0, d == DC - 1)
                last.then_inc(product_done, 1)

            def down(i, ki, k, first=False):
                pe.wait_ge(ring.lo_made, tile(ki, k + 1) + 1)
                pe.wait_ge(h_lo_made, 2 * i + 2)
                for d in range(DC):
                    if not (first and d < 2):
                        pe.wait_ge(added, DC * i + d - 1)
                    for j in range(2):
                        last = three_pass(pe, [ps_d[:, d % 2, 0], ps_d[:, d % 2, 1]],
                                          ring.hi[:, slot(k + j), d], ring.lo[:, slot(k + j), d],
                                          h_hi[:, j], h_lo[:, j], j == 0, j == 1)
                    last.then_inc(down_done, 1)

            norm.sums(pe)
            gate(0, 2, 0, True)
            up(0, 3, 0, True)
            gate(0, 4, 1)
            up(0, 5, 1)
            gate(1, 0, 0)
            down(0, 1, 1, True)
            up(1, 3, 0)
            gate(1, 4, 1)
            up(1, 5, 1)
            with pe.Fori(2, PAIRS) as i:
                gate(i, 0, 0)
                down(i - 1, i, 1)
                up(i, 3, 0)
                gate(i, 4, 1)
                up(i, 5, 1)
            down(PAIRS - 1, PAIRS, 0)


def past(engine, sem, value):
    if not (isinstance(value, int) and value <= 0):
        engine.wait_ge(sem, value)


def wait_apart(engine, sem, value):
    engine.wait_ge(sem, value)
    engine.nop(nofuse=True)


def mixer_setup(core, a, ctx):
    nc, c, per = core.nc, core, core.ctx
    c.masks = c.sb(per, "masks", [P, 7, CH])
    c.sel = c.sb(per, "sel", [BETA_ROW + 2 * DN_HEADS, HP, P])
    c.conv_w = c.sb(per, "conv_w", [P, 3, HP, CONV])
    c.branch_gain = c.sb(per, "branch_gain", [P, 2])
    c.dt_bias = c.sb(per, "dt_bias", [2 * DN_HEADS, 1])
    c.neg_a = c.sb(per, "neg_a", [2 * DN_HEADS, 1])
    c.slopes = c.sb(per, "slopes", [P, DF_HEADS])
    c.neg_lam = c.sb(per, "neg_lam", [P, 1])
    wide = c.sb(ctx, "wide_masks", [P, 7, P])
    lam_in = c.sb(ctx, "lam_in", [1, 4, HD])
    lam_sum = c.sb(ctx, "lam_sum", [1, 4])
    lam_ps = c.ps(ctx, "lam_ps", [P, HALF])
    cleared = c.sem("cleared")
    loaded = c.sem("params_loaded")
    cut = c.sem("masks_cut")
    step = c.sem("lam_step")
    exped = c.sem("lam_exped")
    lam_ready = c.sem("lam_ready")

    def scalar_part(act):
        for kind in range(3):
            for hp in range(HP):
                col = kind * DN_W + hp * P
                act.dma_start(c.conv_w[:, kind, hp, :], a["conv_qkv"][0, :, col:col + P].rearrange("w p -> p w"),
                             allow_slow_non_contiguous=True).then_inc(loaded, 16)
        for h in range(2):
            act.dma_start(c.branch_gain[h * HD:(h + 1) * HD, 0:1], a["dn_out_norm"].rearrange("l e -> e l"),
                         allow_slow_non_contiguous=True).then_inc(loaded, 16)
        act.dma_start(c.branch_gain[:, 1:2], a["diff_subln"].rearrange("l e -> e l"),
                     allow_slow_non_contiguous=True).then_inc(loaded, 16)
        for i, name in enumerate(("diff_lambda_q1", "diff_lambda_k1", "diff_lambda_q2", "diff_lambda_k2")):
            act.dma_start(lam_in[:, i, :], a[name]).then_inc(loaded, 16)
        act.wait_ge(cleared, 3)
        act.dma_start(c.dt_bias[0:DN_HEADS, :], a["dn_dt_bias"].rearrange("l h -> h l"),
                     allow_slow_non_contiguous=True).then_inc(loaded, 16)
        act.dma_start(c.neg_a[0:DN_HEADS, :], a["dn_a_log"].rearrange("l h -> h l"),
                     allow_slow_non_contiguous=True).then_inc(loaded, 16)
        act.wait_ge(step, 3)
        act.activation(lam_sum[:, 0:2], lam_sum[:, 0:2], ACT.Exp).then_inc(exped, 1)
        act.wait_ge(loaded, 16 * N_LOADS)
        act.activation(c.neg_a[:], c.neg_a[:], ACT.Exp).then_inc(exped, 1)

    N_LOADS = 3 * HP + 3 + 4 + 2

    def gpsimd_part(pool):
        made = [0]

        def select(view, op, fill, base, pattern, mult):
            pool.wait_ge(cut, made[0])
            pool.affine_select(out=view, in_=view, compare_op=op, fill=fill, base=base, pattern=pattern,
                               channel_multiplier=mult).then_inc(cut, 1)
            made[0] += 1

        pool.memset(wide[:], 1.0).then_inc(cut, 1)
        pool.memset(c.sel[:], 0.0).then_inc(cut, 1)
        made[0] = 2
        for lv in range(6):
            s = 1 << lv
            view = wide[:, lv, :].rearrange("p (b r) -> p b r", r=2 * s)
            nb = P // (2 * s)
            select(view, ALU.is_ge, 0.0, 0, [[-2 * s, nb], [0, 2 * s]], 1)
            select(view, ALU.is_ge, 0.0, s - 1, [[2 * s, nb], [0, 2 * s]], -1)
            select(view, ALU.is_ge, 0.0, -s, [[0, nb], [1, 2 * s]], 0)
        view = wide[:, 6, :].rearrange("p (b r) -> p b r", r=CH)
        select(view, ALU.is_ge, 0.0, 0, [[-CH, 2], [0, CH]], 1)
        select(view, ALU.is_ge, 0.0, 0, [[CH, 2], [1, CH]], -1)
        for kind in range(2):
            view = c.sel[BETA_ROW * kind:BETA_ROW * kind + 2 * DN_HEADS].rearrange("r h (b q) -> r h b q", b=2)
            select(view, ALU.not_equal, 1.0, -DN_HEADS * kind, [[-2, HP], [-1, 2], [0, CH]], 1)

    N_CUT = 2 + 18 + 2 + 2

    def clear_part(dve):
        dve.memset(c.dt_bias[:], 0.0).then_inc(cleared, 1)
        dve.memset(c.neg_a[:], 0.0).then_inc(cleared, 1)
        dve.memset(lam_sum[:], 0.0).then_inc(cleared, 1)
        for h in range(DF_HEADS):
            dve.memset(c.slopes[:, h:h + 1], 2.0 ** (-8.0 * (h + 1) / DF_HEADS))

    def vector_part(dve):
        dve.wait_ge(loaded, 16 * N_LOADS)
        dve.tensor_scalar(c.branch_gain[:, 1:2], c.branch_gain[:, 1:2], 1.0 - LAM_INIT, None, ALU.mult)
        for m in range(2):
            dve.tensor_tensor(lam_in[:, m, :], lam_in[:, 2 * m, :], lam_in[:, 2 * m + 1, :],
                              ALU.mult).then_inc(step, 1)
            dve.wait_ge(step, m + 1)
        dve.tensor_reduce(lam_sum[:, 0:2], lam_in[:, 0:2, :], AX_X, ALU.add).then_inc(step, 1)
        dve.wait_ge(exped, 1)
        dve.tensor_tensor(lam_sum[:, 2:3], lam_sum[:, 1:2], lam_sum[:, 0:1], ALU.subtract).then_inc(step, 1)
        dve.wait_ge(step, 4)
        dve.tensor_scalar(lam_sum[:, 3:4], lam_sum[:, 2:3], -LAM_INIT, None, ALU.add).then_inc(step, 1)
        dve.wait_ge(lam_ready, 1)
        dve.tensor_copy(c.neg_lam[:], lam_ps[:, 0:1])
        dve.wait_ge(cut, N_CUT)
        dve.tensor_tensor(c.masks[:], wide[:, :, 0:CH], wide[:, :, CH:P], ALU.add)
        dve.wait_ge(exped, 2)
        dve.tensor_scalar(c.neg_a[:], c.neg_a[:], -1.0, None, ALU.mult)

    def tensor_part(pe):
        pe.wait_ge(step, 5)
        pe.matmul(lam_ps[:, 0:1], c.ones[0:1, :], lam_sum[:, 3:4], start=True, stop=True).then_inc(lam_ready, 1)

    return {"clear": clear_part, "gpsimd": gpsimd_part, "vector": vector_part, "scalar": scalar_part,
            "tensor": tensor_part}


def column_tiles(w, first, count):
    return w[0, :, first:first + count * P].rearrange("(k p) (f c) -> f p k c", p=P, c=P)


def project(pe, core, ring, slot, banks):
    for d in range(DC):
        last = three_pass(pe, banks, ring.hi[:, slot, d], ring.lo[:, slot, d], core.n_hi[:, d], core.n_lo[:, d],
                          d == 0, d == DC - 1)
    return last


def dn_project_phase(core, a, qkv, gc, beta):
    nc, c = core.nc, core
    with ExitStack() as ctx:
        ring = Ring(c, ctx, 3)
        pad = c.sb(ctx, "padded", [P, CONV - 1 + T])
        acc = c.sb(ctx, "conv_acc", [P, T])
        sq = c.sb(ctx, "squares", [P, T])
        root = c.sb(ctx, "root", [P, T])
        ps_x = c.ps(ctx, "ps_proj", [P, 3, NH, HALF])
        ps_s = c.ps(ctx, "ps_sum", [P, NH, HALF])
        projected = c.sem("projected")
        padded = c.sem("padded")
        pad_zero = c.sem("pad_zero")
        conv_step = c.sem("conv_step")
        silu_done = c.sem("silu_done")
        squared = c.sem("squared")
        head_summed = c.sem("head_summed")
        rooted = c.sem("rooted")
        inverted = c.sem("inverted")
        normed = c.sem("normed")
        gate_step = c.sem("decay_step")
        gate_act = c.sem("decay_act")
        R = 2 * DN_HEADS
        ab_raw = c.sb(ctx, "ab_raw", [P, DC, R])
        ab_hi, ab_lo = c.sb(ctx, "ab_hi", [P, DC, R], F32R), c.sb(ctx, "ab_lo", [P, DC, R], F32R)
        ab_landed = c.sem("ab_landed")
        ab_hi_made = c.sem("ab_hi_made")
        ab_lo_made = c.sem("ab_lo_made")
        ab_projected = c.sem("ab_projected")
        z_rows, abs_rows, exp_rows, decay_rows = (x[0:R, i, :] for x, i in (
            (qkv[0], HP - 1), (qkv[1], HP - 1), (qkv[2], HP - 1), (qkv[2], HP - 2)))
        norm = Norm(c, 1, root, ps_s[:])
        block = ctx.enter_context(nc.Block())
        w_in = a["w_in"]
        kinds = [column_tiles(w_in, kind * DN_W, HP) for kind in range(3)]
        flat = lambda x: x.rearrange("p h t -> p (h t)")

        @block.sync
        def _(sp):
            def load(i, kind):
                past(sp, ring.lo_made, 3 * i + kind - 2)
                sp.dma_start(ring.raw[:, kind], kinds[kind][i]).then_inc(ring.landed[kind], 16)

            sp.dma_start(ab_raw[:], w_in[0, :, OFF_AB:OFF_AB + R].rearrange("(k p) c -> p k c", p=P)).then_inc(
                ab_landed, 16)
            for kind in range(3):
                load(0, kind)
            with sp.Fori(1, HP) as i:
                for kind in range(3):
                    load(i, kind)

        @block.gpsimd
        def _(pool):
            norm.odd_lo_parts(pool)

        @block.scalar
        def _(act):
            def hi(i, kind):
                act.wait_ge(ring.landed[kind], 16 * i + 16)
                past(act, projected, 3 * i + kind - 2)
                act.activation(ring.hi[:, kind], ring.raw[:, kind], ACT.Copy).then_inc(ring.hi_made, 1)

            def root_of(i, kind):
                act.wait_ge(head_summed, 2 * i + kind + 1)
                past(act, normed, 2 * i + kind)
                act.activation(root[:], flat(ps_s[:]), ACT.Sqrt, bias=c.eps[:, 0:1]).then_inc(rooted, 1)

            def pair(i, last=False):
                for kind in range(3):
                    if not (last and kind):
                        hi(i + (kind + 2) // 3, (kind + 2) % 3)
                    act.wait_ge(projected, 3 * i + kind + 1)
                    past(act, conv_step, 4 * (3 * i + kind))
                    act.activation(pad[:, CONV - 1:], flat(ps_x[:, kind]), ACT.Copy).then_inc(padded, 1)
                    if kind:
                        root_of(i, kind - 1)
                    wait_apart(act, conv_step, 4 * (3 * i + kind) + 4)
                    act.activation(qkv[kind][:, i, :], acc[:], ACT.Silu).then_inc(silu_done, 1)
                    if kind < 2:
                        past(act, head_summed, 2 * i + kind)
                        wait_apart(act, silu_done, 3 * i + kind + 1)
                        act.activation(sq[:], qkv[kind][:, i, :], ACT.Square).then_inc(squared, 1)

            norm.squares(act)
            act.wait_ge(ab_landed, 16)
            act.activation(ab_hi[:], ab_raw[:], ACT.Copy).then_inc(ab_hi_made, 1)
            hi(0, 0)
            norm.root(act)
            hi(0, 1)
            norm.hi_parts(act)
            ab = flat(ps_x[0:R, 2])
            act.wait_ge(ab_projected, 1)
            act.activation(z_rows, ab, ACT.Identity, bias=c.dt_bias[:]).then_inc(gate_act, 1)
            act.activation(beta, ab, ACT.Sigmoid).then_inc(gate_act, 1)
            act.wait_ge(gate_act, 1)
            act.activation(abs_rows, z_rows, ACT.Abs).then_inc(gate_act, 1)
            act.wait_ge(gate_act, 3)
            act.activation(exp_rows, abs_rows, ACT.Exp, scale=-1.0).then_inc(gate_act, 1)
            act.wait_ge(gate_act, 4)
            act.activation(decay_rows, exp_rows, ACT.Ln, bias=1.0).then_inc(gate_act, 1)
            pair(0)
            with act.Fori(1, HP - 1) as i:
                pair(i)
            pair(HP - 1, True)

        @block.vector
        def _(dve):
            def lo(i, kind):
                dve.wait_ge(ring.hi_made, 3 * i + kind + 1)
                dve.tensor_tensor(ring.lo[:, kind], ring.raw[:, kind], ring.hi[:, kind].bitcast(F32),
                                  ALU.subtract).then_inc(ring.lo_made, 1)

            def normalise(i, kind):
                m = 2 * i + kind
                dve.wait_ge(rooted, m + 1)
                dve.reciprocal(root[:], root[:]).then_inc(inverted, 1)
                dve.wait_ge(inverted, m + 1)
                x = qkv[kind][:, i, :]
                dve.scalar_tensor_tensor(out=x, in0=x, scalar=(HD ** -0.5 if kind == 0 else 1.0), in1=root[:],
                                         op0=ALU.mult, op1=ALU.mult).then_inc(normed, 1)

            def pair(i, last=False):
                for kind in range(3):
                    if not (last and kind):
                        lo(i + (kind + 2) // 3, (kind + 2) % 3)
                    s0 = 4 * (3 * i + kind)
                    w = lambda tap: c.conv_w[:, kind, i, tap:tap + 1]
                    dve.wait_ge(padded, 3 * i + kind + 1)
                    past(dve, silu_done, 3 * i + kind)
                    dve.tensor_scalar(acc[:], pad[:, CONV - 1:], w(CONV - 1), None, ALU.mult).then_inc(conv_step, 1)
                    for tap in range(CONV - 1):
                        dve.wait_ge(conv_step, s0 + tap + 1)
                        dve.scalar_tensor_tensor(out=acc[:], in0=pad[:, tap:tap + T], scalar=w(tap), in1=acc[:],
                                                 op0=ALU.mult, op1=ALU.add).then_inc(conv_step, 1)
                    if kind:
                        normalise(i, kind - 1)

            dve.memset(pad[:, 0:CONV - 1], 0.0).then_inc(pad_zero, 1)
            dve.wait_ge(pad_zero, 1)
            norm.pairs(dve)
            dve.wait_ge(ab_hi_made, 1)
            dve.tensor_tensor(ab_lo[:], ab_raw[:], ab_hi[:].bitcast(F32), ALU.subtract).then_inc(ab_lo_made, 1)
            lo(0, 0)
            norm.scale(dve)
            lo(0, 1)
            dve.wait_ge(gate_act, 5)
            dve.scalar_tensor_tensor(out=decay_rows, in0=z_rows, scalar=0.0, in1=decay_rows, op0=ALU.max,
                                     op1=ALU.add).then_inc(gate_step, 1)
            dve.memset(abs_rows, 1.0).then_inc(gate_step, 1)
            dve.wait_ge(gate_step, 2)
            dve.memset(abs_rows.rearrange("r (n s) -> r n s", s=CH)[:, :, 0:1], 0.0).then_inc(gate_step, 1)
            dve.tensor_scalar(decay_rows, decay_rows, c.neg_a[:], None, ALU.mult).then_inc(gate_step, 1)
            dve.wait_ge(gate_step, 4)
            dve.tensor_tensor_scan(gc, abs_rows, decay_rows, 0.0, ALU.mult, ALU.add).then_inc(gate_step, 1)
            pair(0)
            with dve.Fori(1, HP - 1) as i:
                pair(i)
            pair(HP - 1, True)

        @block.tensor
        def _(pe):
            def tile(i, kind):
                pe.wait_ge(ring.lo_made, 3 * i + kind + 1)
                past(pe, padded, 3 * i + kind - 2)
                if isinstance(i, int) and i == 0 and kind == 2:
                    pe.wait_ge(gate_act, 2)
                project(pe, c, ring, kind, [ps_x[:, kind, 0], ps_x[:, kind, 1]]).then_inc(projected, 1)

            def head_sum(i, kind):
                pe.wait_ge(squared, 2 * i + kind + 1)
                past(pe, rooted, 2 * i + kind)
                for h in range(NH):
                    last = pe.matmul(ps_s[:, h], c.head_ones[:], sq[:, h * HALF:(h + 1) * HALF], start=True, stop=True)
                last.then_inc(head_summed, 1)

            def pair(i):
                tile(i, 0)
                tile(i, 1)
                head_sum(i, 0)
                tile(i, 2)
                head_sum(i, 1)

            norm.sums(pe)
            pe.wait_ge(ab_lo_made, 1)
            for d in range(DC):
                norm.wait_chunk(pe, d)
                last = three_pass(pe, [ps_x[0:R, 2, 0], ps_x[0:R, 2, 1]], ab_hi[:, d], ab_lo[:, d], c.n_hi[:, d],
                                  c.n_lo[:, d], d == 0, d == DC - 1)
            last.then_inc(ab_projected, 1)
            pair(0)
            with pe.Fori(1, HP) as i:
                pair(i)


def dn_phase(core, qkv, gc, beta):
    nc, c = core.nc, core
    qT, kT, vT = qkv
    R = 2 * DN_HEADS
    C2 = 2
    UN = C2 * HP
    STEPS = NCH // C2
    SM = [P, UN, CH]
    with ExitStack() as ctx:
        sb = lambda name, shape=SM: c.sb(ctx, name, shape)
        kc, qc, vc = sb("kc"), sb("qc"), sb("vc")
        rows = sb("gc_beta_chunk", [BETA_ROW + R, C2 * CH])
        gcc, bcc = rows[0:R, :], rows[BETA_ROW:, :]
        diag = sb("diag", [P, 2, UN, CH])
        col = sb("col", [P, 2, UN])
        expo = sb("expo", [P, 3, UN])
        kb, rel, at, attT = sb("kb"), sb("rel"), sb("at"), sb("attT")
        qd = sb("qd")
        lev = sb("lev", [P, 6, UN, CH])
        U, W, M = sb("U"), sb("W"), sb("M")
        bsc, kbe, kd, vb = sb("bsc", [P, UN]), sb("kbe"), sb("kd"), sb("vb")
        wtn = sb("wtn")
        vnew, o_nat = sb("vnew", [P, HP, CH]), sb("o_nat")
        S = sb("state", [P, 2, HP, CH])
        psA, psB, psC, psD, psE, psF, psG, psH = (
            c.ps(ctx, f"ps_{n}", SM) for n in ("gc", "k_nat", "v_nat", "att", "AT", "beta", "g", "h"))
        psM, psU, psW = (psE, psH), (psF, psA), (psG, psD)
        s = {n: c.sem(n) for n in (
            "cut", "bcast", "nat", "kb_made", "scored", "decayed", "small_exp", "U_made", "lev_made",
            "W_ps", "W_made", "M_ps", "M_made", "step_ps", "dve", "wt_ps", "wt_made", "kbe_made",
            "vnew_ps", "vnew_made", "o_ps", "o_made", "dS_ps", "S_faded", "S_made", "oT_ps", "oT_made", "q_made")}
        taken = [c.sem(f"step_taken{i}") for i in range(C2)]
        block = ctx.enter_context(nc.Block())
        bc = lambda x: x.unsqueeze(2).broadcast_to([P, x.shape[1], CH])
        over = lambda m: m.unsqueeze(1).broadcast_to([P, UN, CH])
        pair_of = lambda x, m: x[:, :, bass.ts(m, C2 * CH)].rearrange("p h (c s) -> p c h s", c=C2)
        units = lambda x: x[:].rearrange("p (c h) s -> p c h s", c=C2)
        of_chunk = lambda x, i: x[:, i * HP:(i + 1) * HP]
        DV_DIAG, DV_COL, DV_REL = 1, 2, 7
        DV = 14

        LV = 5

        @block.gpsimd
        def _(pool):
            def step(m):
                past(pool, s["scored"], m)
                past(pool, s["q_made"], m)
                sl = bass.ts(m, C2 * CH)
                for i, (dst, src) in enumerate(((gcc, gc[:, sl]), (bcc, beta[:, sl]), (units(kc), pair_of(kT, m)),
                                                (units(qc), pair_of(qT, m)), (units(vc), pair_of(vT, m)))):
                    if i < 3:
                        past(pool, s["cut"], 5 * m + i)
                    pool.tensor_copy(dst, src).then_inc(s["cut"], 1)

            step(0)
            with pool.Fori(1, STEPS) as m:
                step(m)

        @block.tensor
        def _(pe):
            def stacked(out, lhs, rhs, start=True, stop=True):
                for h in range(2):
                    r = slice(h * CH, (h + 1) * CH)
                    last = pe.matmul(out[r], lhs[r], rhs[r], start=start, stop=stop)
                return last

            def each(out, lhs, rhs):
                for u in range(out.shape[1]):
                    last = stacked(out[:, u], lhs[:, u], rhs if rhs is c.ident2 else rhs[:, u])
                return last

            def step(m):
                pe.wait_ge(s["cut"], 5 * m + 2)
                past(pe, s["S_made"], C2 * m + 1 if not isinstance(m, int) else 0)
                for kind, row in ((0, gcc), (1, bcc)):
                    pick = c.sel[BETA_ROW * kind:BETA_ROW * kind + R]
                    for u in range(UN):
                        i = u // HP
                        last = pe.matmul((psA, psF)[kind][:, u], pick[:, u % HP], row[:, i * CH:(i + 1) * CH],
                                         start=True, stop=True)
                last.then_inc(s["bcast"], 1)
                past(pe, s["oT_made"], m)
                wait_apart(pe, s["cut"], 5 * m + 5)
                each(psB, kc, c.ident2)
                each(psC, vc, c.ident2).then_inc(s["nat"], 1)
                each(psD, kc, qc)
                wait_apart(pe, s["kb_made"], m + 1)
                each(psE, kc, kb).then_inc(s["scored"], 1)
                pe.wait_ge(s["small_exp"], 2 * m + 2)
                wait_apart(pe, s["U_made"], m + 1)
                each(psA, U, c.ident2).then_inc(s["W_ps"], 1)
                pe.wait_ge(s["W_made"], m + 1)
                wait_apart(pe, s["lev_made"], m + 1)
                for lv in range(1, LV + 1):
                    k = LV * m + lv
                    for i in range(C2):
                        if lv > 1:
                            wait_apart(pe, taken[i], k - 1)
                        each(of_chunk(psM[i], i), of_chunk(lev[:, lv], i), of_chunk(W, i)).then_inc(s["M_ps"], 1)
                    for i in range(C2):
                        if i and lv == 1:
                            pe.wait_ge(s["q_made"], m + 1)
                        wait_apart(pe, s["M_made"], C2 * (k - 1) + i + 1)
                        last = each(of_chunk(psU[i], i), of_chunk(M, i), of_chunk(U, i))
                        if lv < LV:
                            last = each(of_chunk(psW[i], i), of_chunk(U, i), of_chunk(M, i))
                        last.then_inc(s["step_ps"], 1)
                pe.wait_ge(s["kbe_made"], m + 1)
                for i in range(C2):
                    wait_apart(pe, taken[i], LV * m + LV)
                    each(of_chunk(psM[i], i), of_chunk(kbe, i), of_chunk(U, i)).then_inc(s["wt_ps"], 1)
                for i in range(C2):
                    k = C2 * m + i
                    pe.wait_ge(s["wt_made"], k + 1)
                    wait_apart(pe, s["S_made"], k + 1)
                    for hp in range(HP):
                        u = i * HP + hp
                        stacked(psW[i][:, u], U[:, u], vb[:, u], True, False)
                        last = stacked(psW[i][:, u], wtn[:, u], S[:, i, hp], False, True)
                    last.then_inc(s["vnew_ps"], 1)
                    pe.wait_ge(s["q_made"], m + 1)
                    wait_apart(pe, s["vnew_made"], k + 1)
                    each(of_chunk(psB, i), of_chunk(kd, i), vnew).then_inc(s["dS_ps"], 1)
                    for hp in range(HP):
                        u = i * HP + hp
                        bank = psU[i]
                        stacked(bank[:, u], qd[:, u], S[:, i, hp], True, False)
                        last = stacked(bank[:, u], attT[:, u], vnew[:, hp], False, True)
                    last.then_inc(s["o_ps"], 1)
                wait_apart(pe, s["o_made"], C2 * m + C2)
                each(psC, o_nat, c.ident2).then_inc(s["oT_ps"], 1)

            step(0)
            with pe.Fori(1, STEPS) as m:
                step(m)

        @block.scalar
        def _(act):
            def step(m):
                act.wait_ge(s["dve"], DV * m + DV_REL)
                act.activation(expo[:], expo[:], ACT.Exp).then_inc(s["small_exp"], 1)
                act.activation(rel[:], rel[:], ACT.Exp).then_inc(s["decayed"], 1)
                act.activation(qd[:], psA[:], ACT.Exp).then_inc(s["small_exp"], 1)
                act.wait_ge(s["W_ps"], m + 1)
                act.activation(W[:], psA[:], ACT.Copy).then_inc(s["W_made"], 1)
                for lv in range(1, LV + 1):
                    for i in range(C2):
                        act.wait_ge(s["M_ps"], C2 * (LV * m + lv - 1) + i + 1)
                        act.activation(of_chunk(M, i), of_chunk(psM[i], i), ACT.Copy).then_inc(s["M_made"], 1)
                for i in range(C2):
                    act.wait_ge(s["wt_ps"], C2 * m + i + 1)
                    act.activation(of_chunk(wtn, i), of_chunk(psM[i], i), ACT.Copy, scale=-1.0).then_inc(s["wt_made"], 1)
                for i in range(C2):
                    act.wait_ge(s["vnew_ps"], C2 * m + i + 1)
                    past(act, s["o_ps"], C2 * m + i)
                    act.activation(vnew[:], of_chunk(psW[i], i), ACT.Copy).then_inc(s["vnew_made"], 1)
                    act.wait_ge(s["o_ps"], C2 * m + i + 1)
                    act.activation(of_chunk(o_nat, i), of_chunk(psU[i], i), ACT.Copy).then_inc(s["o_made"], 1)

            step(0)
            with act.Fori(1, STEPS) as m:
                step(m)

        @block.vector
        def _(dve):
            def step(m):
                n = [0]

                def ordered(ins):
                    ins.then_inc(s["dve"], 1)
                    n[0] += 1

                def own(count):
                    dve.wait_ge(s["dve"], DV * m + count)

                dve.wait_ge(s["bcast"], m + 1)
                dve.wait_ge(s["cut"], 5 * m + 5)
                dve.tensor_tensor(diag[:, 0], psA[:], over(c.ident2[:]), ALU.mult)
                ordered(dve.tensor_tensor(diag[:, 1], psF[:], over(c.ident2[:]), ALU.mult))
                dve.tensor_tensor(kb[:], kc[:], psF[:], ALU.mult).then_inc(s["kb_made"], 1)
                own(DV_DIAG)
                ordered(dve.tensor_reduce(col[:], diag[:], AX_X, ALU.add))
                own(DV_COL)
                last_gc = psA[:, :, CH - 1]
                ordered(dve.tensor_copy(expo[:, 0, :], col[:, 0]))
                ordered(dve.tensor_tensor(expo[:, 1, :], last_gc, col[:, 0], ALU.subtract))
                ordered(dve.tensor_copy(expo[:, 2, :], last_gc))
                ordered(dve.tensor_tensor(rel[:], psA[:], bc(col[:, 0]), ALU.subtract))
                own(6)
                ordered(dve.tensor_scalar(rel[:], rel[:], 0.0, None, ALU.min))
                dve.wait_ge(s["decayed"], m + 1)
                ordered(dve.tensor_tensor(rel[:], rel[:], over(c.masks[:, 6]), ALU.mult))
                own(8)
                dve.wait_ge(s["scored"], m + 1)
                ordered(dve.tensor_tensor(at[:], psE[:], rel[:], ALU.mult))
                own(9)
                ordered(dve.tensor_tensor(lev[:, 0], at[:], over(c.masks[:, 0]), ALU.mult))
                own(10)
                dve.tensor_tensor(U[:], over(c.ident2[:]), lev[:, 0], ALU.subtract).then_inc(s["U_made"], 1)
                for lv in range(1, LV + 1):
                    last = dve.tensor_tensor(lev[:, lv], at[:], over(c.masks[:, lv]), ALU.mult)
                last.then_inc(s["lev_made"], 1)

                def rest():
                    ordered(dve.tensor_tensor(attT[:], psD[:], rel[:], ALU.mult))
                    dve.wait_ge(s["small_exp"], 2 * m + 2)
                    ordered(dve.tensor_tensor(bsc[:], col[:, 1], expo[:, 0, :], ALU.mult))
                    dve.tensor_tensor(qd[:], qc[:], qd[:], ALU.mult).then_inc(s["q_made"], 1)
                    yield
                    ordered(dve.tensor_tensor(kd[:], psB[:], bc(expo[:, 1, :]), ALU.mult))
                    ordered(dve.tensor_tensor(vb[:], psC[:], bc(col[:, 1]), ALU.mult))
                    yield
                    own(12)
                    dve.tensor_tensor(kbe[:], psB[:], bc(bsc[:]), ALU.mult).then_inc(s["kbe_made"], 1)
                    yield

                gaps = rest()
                for lv in range(1, LV + 1):
                    if lv <= 3:
                        next(gaps)
                    for i in range(C2):
                        dve.wait_ge(s["step_ps"], C2 * (LV * m + lv - 1) + i + 1)
                        if lv < LV:
                            dve.tensor_tensor(of_chunk(W, i), of_chunk(W, i), of_chunk(psW[i], i), ALU.subtract)
                        dve.tensor_tensor(of_chunk(U, i), of_chunk(U, i), of_chunk(psU[i], i),
                                          ALU.subtract).then_inc(taken[i], 1)
                for i in range(C2):
                    k = C2 * m + i
                    fade = bc(expo[:, 2, i * HP:(i + 1) * HP])
                    after = S[:, 1 - i]
                    past(dve, s["o_ps"], k)
                    dve.wait_ge(s["S_made"], k + 1)
                    dve.tensor_tensor(after, S[:, i], fade, ALU.mult).then_inc(s["S_faded"], 1)
                    dve.wait_ge(s["S_faded"], k + 1)
                    dve.wait_ge(s["dS_ps"], k + 1)
                    dve.tensor_tensor(after, after, of_chunk(psB, i), ALU.add).then_inc(s["S_made"], 1)
                dve.wait_ge(s["oT_ps"], m + 1)
                dve.tensor_copy(pair_of(qT, m), units(psC)).then_inc(s["oT_made"], 1)
                assert n[0] == DV, n

            dve.memset(S[:], 0.0).then_inc(s["S_made"], 1)
            step(0)
            with dve.Fori(1, STEPS) as m:
                step(m)


def attention_phase(core, a, obT):
    nc, c = core.nc, core
    NQ = T // P
    NB = DF_HEADS * NQ
    V, Q, K = range(3)
    NT = 3 * DF_HEADS
    SPREAD = [(V, 3), (V, 3), (V, 2), (Q, 3), (Q, 3), (Q, 2), (K, 4), (K, 4)]
    ENDS = {2: V, 5: Q, 7: K}

    def ending(b):
        h, part = (b + 1) // NQ + 1, (b + 1) % NQ
        return 3 * h + ENDS[part] if h < DF_HEADS and part in ENDS else None

    with ExitStack() as ctx:
        ring = Ring(c, ctx, 2)
        q, k = c.sb(ctx, "q", [P, 2, T]), c.sb(ctx, "k", [P, 2, T])
        v = c.sb(ctx, "v", [P, 2, NQ, P])
        bias = c.sb(ctx, "bias", [P, T])
        sc = c.sb(ctx, "scores", [P, 2, 2, T])
        pT = c.sb(ctx, "probs_t", [P, NQ, P])
        neg_max = c.sb(ctx, "neg_max", [P, 2, 2])
        total = c.sb(ctx, "total", [P, 2, 2])
        ps_s = c.ps(ctx, "ps_scores", [P, 2, NH, HALF])
        ps_p = c.ps(ctx, "ps_proj", [P, NH, HALF])
        ps_t = c.ps(ctx, "ps_turned", [P, 4, P])
        ps_o = c.ps(ctx, "ps_out", [P, HALF])
        s = {n: c.sem(n) for n in (
            "bias", "projected", "evacuated", "scored", "biased", "maxed", "negated", "exped", "combining",
            "combined", "turned", "taken", "o_ps", "o_made")}
        block = ctx.enter_context(nc.Block())
        kinds = [column_tiles(a["w_in"], off, DF_HEADS) for off in (OFF_V, OFF_Q, OFF_K)]
        flat = lambda x: x.rearrange("p h t -> p (h t)")
        keys = lambda b: (b % NQ + 1) * P
        groups = lambda b: b % NQ // 4 + 1
        fill, n_fills = {}, 0
        for g in range(2):
            fill["v", 0, g] = n_fills
            n_fills += 1
        for b in range(NB):
            for g in range(groups(b)):
                fill[b, g] = n_fills
                n_fills += 1
            if b % NQ == 3 and b // NQ + 1 < DF_HEADS:
                for g in range(2):
                    fill["v", b // NQ + 1, g] = n_fills
                    n_fills += 1

        @block.sync
        def _(sp):
            for t in range(NT):
                past(sp, ring.lo_made, t - 1)
                sp.dma_start(ring.raw[:, t % 2], kinds[t % 3][t // 3]).then_inc(ring.landed[t % 2], 16)

        @block.gpsimd
        def _(pool):
            pool.iota(bias[:], pattern=[[1, T]], base=-(T - P), channel_multiplier=-1,
                      allow_small_or_imprecise_dtypes=True).then_inc(s["bias"], 1)
            pool.wait_ge(s["bias"], 1)
            pool.affine_select(out=bias[:], in_=bias[:], compare_op=ALU.is_ge, fill=NEG, base=T - P,
                               pattern=[[-1, T]], channel_multiplier=1).then_inc(s["bias"], 1)

        @block.tensor
        def _(pe):
            def projection(t, d0, d1):
                if d0 == d1:
                    return
                if d0 == 0:
                    pe.wait_ge(ring.lo_made, t + 1)
                    past(pe, s["evacuated"], t)
                for d in range(d0, d1):
                    last = three_pass(pe, [ps_p[:, 0], ps_p[:, 1]], ring.hi[:, t % 2, d], ring.lo[:, t % 2, d],
                                      c.n_hi[:, d], c.n_lo[:, d], d == 0, d == DC - 1)
                if d1 == DC:
                    last.then_inc(s["projected"], 1)

            def turn(number, src, pieces):
                past(pe, s["taken"], number)
                for j in range(pieces):
                    last = pe.transpose(ps_t[:, j], src[:, j * P:(j + 1) * P], c.ident[:])
                last.then_inc(s["turned"], 1)

            def turn_v(h):
                pe.wait_ge(s["evacuated"], 3 * h + V + 1)
                for g in range(2):
                    turn(fill["v", h, g], q[:, h % 2, g * HALF:(g + 1) * HALF], 4)

            def scores(b):
                h, i, n = b // NQ, b % NQ, keys(b)
                pe.wait_ge(s["evacuated"], 3 * h + K + 1)
                past(pe, s["biased"], 2 * b)
                for m in range(2):
                    r = slice(m * HD, (m + 1) * HD)
                    for g in range((n + HALF - 1) // HALF):
                        w = min(HALF, n - g * HALF)
                        last = pe.matmul(ps_s[:, m, g, 0:w], q[r, h % 2, i * P:(i + 1) * P],
                                         k[r, h % 2, g * HALF:g * HALF + w], start=True, stop=True)
                last.then_inc(s["scored"], 1)

            projection(V, 0, DC)
            projection(Q, 0, 1)
            turn_v(0)
            projection(Q, 1, DC)
            def part_of_projections(number, last):
                h, part = number // NQ + 1, number % NQ
                if h < DF_HEADS:
                    kind, steps = SPREAD[part]
                    d0 = sum(n for kd, n in SPREAD[:part] if kd == kind)
                    end = d0 + steps
                    cut = end if end == DC else end - 1
                    if last:
                        projection(3 * h + kind, cut, end)
                    else:
                        projection(3 * h + kind, d0, cut)

            projection(K, 0, DC)
            scores(0)
            part_of_projections(0, False)
            part_of_projections(0, True)
            scores(1)
            for b in range(NB):
                h, i = b // NQ, b % NQ
                part_of_projections(b + 1, False)
                if b + 2 < NB:
                    scores(b + 2)
                pe.wait_ge(s["combined"], b + 1)
                for g in range(groups(b)):
                    turn(fill[b, g], sc[:, b % 2, 0, g * HALF:], min(4, i + 1 - 4 * g))
                part_of_projections(b + 1, True)
                pe.wait_ge(s["taken"], fill[b, groups(b) - 1] + 1)
                past(pe, s["o_made"], b)
                for kb in range(i + 1):
                    last = pe.matmul(ps_o[:, 0:P], v[:, h % 2, kb], pT[:, kb], start=(kb == 0), stop=(kb == i))
                last.then_inc(s["o_ps"], 1)
                if i == 3 and h + 1 < DF_HEADS:
                    turn_v(h + 1)

        @block.scalar
        def _(act):
            def hi(t):
                if t < NT:
                    act.wait_ge(ring.landed[t % 2], 16 * (t // 2) + 16)
                    past(act, s["projected"], t - 1)
                    act.activation(ring.hi[:, t % 2], ring.raw[:, t % 2], ACT.Copy).then_inc(ring.hi_made, 1)

            def evacuate(t):
                h, kind = t // 3, t % 3
                act.wait_ge(s["projected"], t + 1)
                past(act, s["scored"], NQ * (h - 1))
                if kind == Q:
                    act.wait_ge(s["turned"], fill["v", h, 1] + 1)
                act.activation((q, q, k)[kind][:, h % 2], flat(ps_p[:]), ACT.Copy,
                               scale=HD ** -0.5 if kind == Q else 1.0).then_inc(s["evacuated"], 1)

            def exps(b):
                act.wait_ge(s["negated"], b + 1)
                for m in range(2):
                    x = sc[:, b % 2, m, 0:keys(b)]
                    act.activation(x, x, ACT.Exp, bias=neg_max[:, b % 2, m:m + 1],
                                   accum_out=total[:, b % 2, m:m + 1]).then_inc(s["exped"], 1)

            def take_out(b):
                h, i = b // NQ, b % NQ
                act.wait_ge(s["o_ps"], b + 1)
                act.activation(obT[:, h, i * P:(i + 1) * P], ps_o[:, 0:P], ACT.Copy).then_inc(s["o_made"], 1)

            hi(0)
            hi(1)
            for kind in range(3):
                evacuate(kind)
                hi(kind + 2)
            exps(0)
            for b in range(NB):
                h, i = b // NQ, b % NQ
                t = ending(b)
                if t and t % 3 == K:
                    evacuate(t)
                if b + 1 < NB:
                    exps(b + 1)
                if b:
                    take_out(b - 1)
                for g in range(groups(b)):
                    w = min(4, i + 1 - 4 * g)
                    act.wait_ge(s["turned"], fill[b, g] + 1)
                    past(act, s["o_ps"], b)
                    act.activation(pT[:, 4 * g:4 * g + w], ps_t[:, 0:w], ACT.Copy).then_inc(s["taken"], 1)
                if t:
                    if t % 3 != K:
                        evacuate(t)
                    hi(t + 2)
            take_out(NB - 1)

        @block.vector
        def _(dve):
            def lo(t):
                if t < NT:
                    dve.wait_ge(ring.hi_made, t + 1)
                    dve.tensor_tensor(ring.lo[:, t % 2], ring.raw[:, t % 2], ring.hi[:, t % 2].bitcast(F32),
                                      ALU.subtract).then_inc(ring.lo_made, 1)

            def take_v(h):
                past(dve, s["o_ps"], NQ * (h - 1))
                for g in range(2):
                    dve.wait_ge(s["turned"], fill["v", h, g] + 1)
                    dve.tensor_copy(v[:, h % 2, 4 * g:4 * g + 4], ps_t[:]).then_inc(s["taken"], 1)

            def bias_and_max(b):
                n, h = keys(b), b // NQ
                dve.wait_ge(s["scored"], b + 1)
                if b >= 2:
                    dve.wait_ge(s["turned"], fill[b - 2, groups(b - 2) - 1] + 1)
                for m in range(2):
                    dve.scalar_tensor_tensor(out=sc[:, b % 2, m, 0:n], in0=bias[:, T - n:T],
                                             scalar=c.slopes[:, h:h + 1], in1=flat(ps_s[:, m])[:, 0:n],
                                             op0=ALU.mult, op1=ALU.add).then_inc(s["biased"], 1)
                dve.wait_ge(s["biased"], 2 * b + 2)
                dve.tensor_reduce(neg_max[:, b % 2], sc[:, b % 2, :, 0:n], AX_X, ALU.max).then_inc(s["maxed"], 1)
                dve.wait_ge(s["maxed"], b + 1)
                dve.tensor_scalar(neg_max[:, b % 2], neg_max[:, b % 2], -1.0, None, ALU.mult).then_inc(s["negated"], 1)

            def combine(b):
                n, w = keys(b), total[:, b % 2]
                p1, p2 = sc[:, b % 2, 0, 0:n], sc[:, b % 2, 1, 0:n]
                dve.wait_ge(s["exped"], 2 * b + 2)
                dve.reciprocal(w, w).then_inc(s["combining"], 1)
                dve.wait_ge(s["combining"], 2 * b + 1)
                dve.tensor_scalar(p2, p2, w[:, 1:2], c.neg_lam[:], ALU.mult, ALU.mult).then_inc(s["combining"], 1)
                dve.wait_ge(s["combining"], 2 * b + 2)
                dve.scalar_tensor_tensor(out=p1, in0=p1, scalar=w[:, 0:1], in1=p2, op0=ALU.mult,
                                         op1=ALU.add).then_inc(s["combined"], 1)

            dve.wait_ge(s["bias"], 2)
            lo(0)
            lo(1)
            take_v(0)
            for kind in range(3):
                lo(kind + 2)
            bias_and_max(0)
            for b in range(NB):
                h, i = b // NQ, b % NQ
                if b + 1 < NB:
                    bias_and_max(b + 1)
                combine(b)
                if i == 3 and h + 1 < DF_HEADS:
                    take_v(h + 1)
                if ending(b):
                    lo(ending(b) + 2)


def branch_norm_phase(core, a, raw, lo_parts, hi_parts):
    nc, c = core.nc, core
    NR = DN_HEADS + DF_HEADS
    NJ = 2 * HP
    steps = [(j // 2, 1 - j % 2) for j in range(NJ)]
    with ExitStack() as ctx:
        ring = Ring(c, ctx, 2)
        sq = c.sb(ctx, "squares", [P, 2, T])
        val = sq
        collect = c.sb(ctx, "collect", [P, NJ, NR])
        spread = c.sb(ctx, "spread", [NR, NJ, P])
        size, eps = c.sb(ctx, "inv_size", [NR, 1]), c.sb(ctx, "eps_rows", [NR, 1])
        rstd = c.sb(ctx, "rstd_rows", [NR, T])
        ps_z = c.ps(ctx, "ps_z", [P, NH, HALF])
        ps_s = c.ps(ctx, "ps_sums", [NR, NH, HALF])
        ps_b = c.ps(ctx, "ps_spread", [P, 2, NH, HALF])
        s = {n: c.sem(n) for n in ("cleared", "collect", "collect_turned", "spread_made", "squared", "summed", "mean",
                                   "rooted", "inverted", "spread", "z_ps", "z_gate", "ungated", "value", "hi", "lo")}
        block = ctx.enter_context(nc.Block())
        flat = lambda x: x.rearrange("p h t -> p (h t)")
        z_tiles = column_tiles(a["w_in"], OFF_Z, HP)

        @block.sync
        def _(sp):
            for t in range(HP):
                past(sp, ring.lo_made, t - 1)
                sp.dma_start(ring.raw[:, t % 2], z_tiles[t]).then_inc(ring.landed[t % 2], 16)

        @block.tensor
        def _(pe):
            def z(t):
                pe.wait_ge(ring.lo_made, t + 1)
                past(pe, s["value"], 2 * t)
                project(pe, c, ring, t % 2, [ps_z[:, 0], ps_z[:, 1]]).then_inc(s["z_ps"], 1)

            def spread_rows(j):
                past(pe, s["value"], j - 1)
                for h in range(NH):
                    last = pe.matmul(ps_b[:, j % 2, h], spread[:, j], rstd[:, h * HALF:(h + 1) * HALF],
                                     start=True, stop=True)
                last.then_inc(s["spread"], 1)

            pe.wait_ge(s["collect"], NR)
            for j in range(NJ):
                last = pe.transpose(ps_b[0:NR, 0, j // 4, j % 4 * P:(j % 4 + 1) * P], collect[:, j], c.ident[:])
            last.then_inc(s["collect_turned"], 1)
            for j in range(NJ):
                pe.wait_ge(s["squared"], j + 1)
                for h in range(NH):
                    last = pe.matmul(ps_s[:, h], collect[:, j], sq[:, j % 2, h * HALF:(h + 1) * HALF],
                                     start=(j == 0), stop=(j == NJ - 1))
                last.then_inc(s["summed"], 1)
            z(0)
            pe.wait_ge(s["inverted"], 1)
            pe.wait_ge(s["spread_made"], 1)
            for t in range(HP):
                spread_rows(2 * t)
                spread_rows(2 * t + 1)
                if t:
                    z(t)

        @block.scalar
        def _(act):
            def hi(t):
                act.wait_ge(ring.landed[t % 2], 16 * (t // 2) + 16)
                past(act, s["z_ps"], t - 1)
                act.activation(ring.hi[:, t % 2], ring.raw[:, t % 2], ACT.Copy).then_inc(ring.hi_made, 1)

            for j, (t, b) in enumerate(steps):
                past(act, s["summed"], j - 1)
                act.activation(sq[:, j % 2], raw[b][:, t, :], ACT.Square).then_inc(s["squared"], 1)
                if 4 <= j < 6:
                    hi(j - 4)
            act.wait_ge(s["mean"], 1)
            act.activation(rstd[:], rstd[:], ACT.Sqrt).then_inc(s["rooted"], 1)
            for j, (t, b) in enumerate(steps):
                if b == 0:
                    act.wait_ge(s["z_ps"], t + 1)
                    act.activation(flat(ps_z[:]), flat(ps_z[:]), ACT.Silu).then_inc(s["z_gate"], 1)
                    if t + 2 < HP:
                        hi(t + 2)
                act.wait_ge(s["value"], j + 1)
                act.activation(hi_parts[b][:, t, :], val[:, j % 2], ACT.Copy).then_inc(s["hi"], 1)

        @block.vector
        def _(dve):
            def lo(t):
                dve.wait_ge(ring.hi_made, t + 1)
                dve.tensor_tensor(ring.lo[:, t % 2], ring.raw[:, t % 2], ring.hi[:, t % 2].bitcast(F32),
                                  ALU.subtract).then_inc(ring.lo_made, 1)

            dve.memset(collect[:], 0.0).then_inc(s["cleared"], 1)
            dve.memset(size[:], 1.0 / P).then_inc(s["cleared"], 1)
            dve.memset(eps[:], SUBLN_EPS).then_inc(s["cleared"], 1)
            dve.wait_ge(s["cleared"], 3)
            dve.memset(size[0:DN_HEADS], 1.0 / HD).then_inc(s["cleared"], 1)
            dve.memset(eps[0:DN_HEADS], RMS_EPS).then_inc(s["cleared"], 1)
            for t in range(HP):
                for h in range(2):
                    dve.memset(collect[h * HD:(h + 1) * HD, 2 * t + 1, 2 * t + h:2 * t + h + 1], 1.0).then_inc(
                        s["collect"], 1)
                dve.memset(collect[:, 2 * t, DN_HEADS + t:DN_HEADS + t + 1], 1.0).then_inc(s["collect"], 1)
            dve.wait_ge(s["collect_turned"], 1)
            dve.tensor_copy(spread[:].rearrange("r j p -> r (j p)"), flat(ps_b[:, 0])[0:NR]).then_inc(s["spread_made"], 1)
            lo(0)
            lo(1)
            dve.wait_ge(s["summed"], NJ)
            dve.wait_ge(s["cleared"], 5)
            dve.tensor_scalar(rstd[:], flat(ps_s[:]), size[:], eps[:], ALU.mult, ALU.add).then_inc(s["mean"], 1)
            dve.wait_ge(s["rooted"], 1)
            dve.reciprocal(rstd[:], rstd[:]).then_inc(s["inverted"], 1)

            def split(j):
                t, b = steps[j]
                dve.wait_ge(s["hi"], j + 1)
                dve.tensor_tensor(lo_parts[b][:, t, :], val[:, j % 2], hi_parts[b][:, t, :].bitcast(F32),
                                  ALU.subtract).then_inc(s["lo"], 1)

            for j, (t, b) in enumerate(steps):
                dve.wait_ge(s["spread"], j + 1)
                past(dve, s["lo"], j - 1)
                out = val[:, j % 2]
                normed = dve.scalar_tensor_tensor(out=out, in0=raw[b][:, t, :], scalar=c.branch_gain[:, b:b + 1],
                                                  in1=flat(ps_b[:, j % 2]), op0=ALU.mult, op1=ALU.mult)
                if b:
                    normed.then_inc(s["value"], 1)
                else:
                    normed.then_inc(s["ungated"], 1)
                    split(j - 1)
                    dve.wait_ge(s["ungated"], t + 1)
                    dve.wait_ge(s["z_gate"], t + 1)
                    dve.tensor_tensor(out, out, flat(ps_z[:]), ALU.mult).then_inc(s["value"], 1)
                    split(j)
                    if t + 2 < HP:
                        lo(t + 2)


def merge_phase(core, a, o_hi, o_lo):
    nc, c = core.nc, core
    with ExitStack() as ctx:
        ring = Ring(c, ctx, 2)
        ga = c.sb(ctx, "gated_a", [P, T])
        gb = c.sb(ctx, "gated_b", [P, T])
        m_hi = c.sb(ctx, "merged_hi", [P, T], F32R)
        m_lo = c.sb(ctx, "merged_lo", [P, T], F32R)
        ps_y = c.ps(ctx, "ps_y", [P, 2, NH, HALF])
        ps_w = c.ps(ctx, "ps_work", [P, 2, NH, HALF])
        s = {n: c.sem(n) for n in ("branches", "gates", "sig", "mul", "m_hi", "m_lo", "out_ps", "added")}
        block = ctx.enter_context(nc.Block())
        flat = lambda x: x.rearrange("p h t -> p (h t)")
        gates_a = column_tiles(a["w_in"], OFF_G, DC)
        gates_b = column_tiles(a["w_in"], OFF_G + D_MODEL, DC)
        br = [w[0].rearrange("(k p) (f c) -> f p k c", p=P, c=P) for w in (a["w_branch_a"], a["w_branch_b"])]
        w_out = a["w_out"][0].rearrange("(f p) (k c) -> f p k c", p=P, c=P)
        KB = DN_W // P
        BR, OUT, GA, GB = range(4)
        NO = DC * NH

        def number(d, kind):
            if isinstance(d, int) and d == 0:
                return {BR: 0, GA: 1, GB: 2}[kind]
            return 4 * d - 1 + kind

        def place(d, kind):
            if isinstance(d, int) and d == 0:
                return {BR: (0, 32), GA: (1, 16), GB: (0, 48)}[kind]
            return {BR: (1, 48 * d), OUT: (0, 32 * d + 32), GA: (1, 48 * d + 16), GB: (0, 32 * d + 48)}[kind]

        @block.sync
        def _(sp):
            def load(d, kind, src):
                slot, _ = place(d, kind)
                past(sp, ring.lo_made, number(d, kind) - 1)
                if kind == BR:
                    for b in range(2):
                        sp.dma_start(ring.raw[:, slot, b * KB:(b + 1) * KB], br[b][d]).then_inc(ring.landed[slot], 16)
                else:
                    sp.dma_start(ring.raw[:, slot], src).then_inc(ring.landed[slot], 16)

            load(0, BR, None)
            load(0, GA, gates_a[0])
            load(0, GB, gates_b[0])
            with sp.Fori(1, DC) as d:
                load(d, BR, None)
                load(d, OUT, w_out[d - 1])
                load(d, GA, gates_a[d])
                load(d, GB, gates_b[d])
            sp.wait_ge(ring.lo_made, 4 * DC - 2)
            sp.dma_start(ring.raw[:, 1], w_out[DC - 1]).then_inc(ring.landed[1], 16)

        @block.scalar
        def _(act):
            def split(slot, landed):
                act.wait_ge(ring.landed[slot], landed)
                act.activation(ring.hi[:, slot], ring.raw[:, slot], ACT.Copy).then_inc(ring.hi_made, 1)

            def hi(d, kind):
                if kind == BR:
                    past(act, s["gates"], 2 * d - 1)
                elif kind == OUT:
                    act.wait_ge(s["gates"], 2 * d)
                elif kind == GA:
                    past(act, s["branches"], d + 1 if not (isinstance(d, int) and d == 0) else 0)
                elif isinstance(d, int) and d == 0:
                    act.wait_ge(s["branches"], 1)
                else:
                    act.wait_ge(s["out_ps"], NO * d)
                split(*place(d, kind))

            def gate(d, b, dst):
                act.wait_ge(s["gates"], 2 * d + b + 1)
                past(act, s["m_lo"], d)
                act.activation(dst[:], flat(ps_w[:, b]), ACT.Sigmoid).then_inc(s["sig"], 1)

            def merged(d):
                act.wait_ge(s["mul"], 3 * d + 3)
                past(act, s["out_ps"], NO * d)
                act.activation(m_hi[:], ga[:], ACT.Copy).then_inc(s["m_hi"], 1)

            hi(0, BR)
            hi(0, GA)
            hi(0, GB)
            gate(0, 0, ga)
            hi(1, BR)
            gate(0, 1, gb)
            hi(1, OUT)
            merged(0)

            def chunk(d, last=False):
                hi(d, GA)
                hi(d, GB)
                gate(d, 0, ga)
                if not last:
                    hi(d + 1, BR)
                else:
                    split(1, 48 * DC - 16)
                gate(d, 1, gb)
                if not last:
                    hi(d + 1, OUT)
                merged(d)

            with act.Fori(1, DC - 1) as d:
                chunk(d)
            chunk(DC - 1, True)

        @block.vector
        def _(dve):
            def lo(t, slot):
                dve.wait_ge(ring.hi_made, t + 1)
                dve.tensor_tensor(ring.lo[:, slot], ring.raw[:, slot], ring.hi[:, slot].bitcast(F32),
                                  ALU.subtract).then_inc(ring.lo_made, 1)

            def gated(d, b, dst):
                dve.wait_ge(s["sig"], 2 * d + b + 1)
                dve.tensor_tensor(dst[:], dst[:], flat(ps_y[:, b]), ALU.mult).then_inc(s["mul"], 1)

            def merged(d):
                dve.wait_ge(s["mul"], 3 * d + 2)
                dve.tensor_tensor(ga[:], ga[:], gb[:], ALU.add).then_inc(s["mul"], 1)

            def merged_lo(d):
                dve.wait_ge(s["m_hi"], d + 1)
                dve.tensor_tensor(m_lo[:], ga[:], m_hi[:].bitcast(F32), ALU.subtract).then_inc(s["m_lo"], 1)

            def add_out(d, first, end):
                for e in range(first, end):
                    for h in range(NH):
                        dve.wait_ge(s["out_ps"], NO * d + NH * e + h + 1)
                        x = c.xT[:, e, h * HALF:(h + 1) * HALF]
                        dve.tensor_tensor(x, x, ps_w[:, e % 2, h], ALU.add).then_inc(s["added"], 1)

            lo(0, 0)
            lo(1, 1)
            lo(2, 0)
            gated(0, 0, ga)
            lo(number(1, BR), 1)
            gated(0, 1, gb)
            merged(0)
            lo(number(1, OUT), 0)
            merged_lo(0)

            def chunk(d, last=False):
                add_out(d - 1, 0, 3)
                lo(4 * d + 1, 1)
                add_out(d - 1, 3, DC)
                lo(4 * d + 2, 0)
                gated(d, 0, ga)
                lo(4 * d + 3, 1)
                gated(d, 1, gb)
                merged(d)
                if not last:
                    lo(4 * d + 4, 0)
                merged_lo(d)

            with dve.Fori(1, DC - 1) as d:
                chunk(d)
            chunk(DC - 1, True)
            add_out(DC - 1, 0, DC)

        @block.tensor
        def _(pe):
            def branches(d):
                slot, _ = place(d, BR)
                pe.wait_ge(ring.lo_made, number(d, BR) + 1)
                for b in range(2):
                    past(pe, s["mul"], 3 * d - 2 + b)
                    for k in range(KB):
                        last = three_pass(pe, [ps_y[:, b, 0], ps_y[:, b, 1]], ring.hi[:, slot, b * KB + k],
                                          ring.lo[:, slot, b * KB + k], o_hi[b][:, k], o_lo[b][:, k],
                                          k == 0, k == KB - 1)
                last.then_inc(s["branches"], 1)

            def gate(d, b):
                slot, _ = place(d, (GA, GB)[b])
                pe.wait_ge(ring.lo_made, number(d, (GA, GB)[b]) + 1)
                past(pe, s["added"], NO * d - 2 * (1 - b))
                project(pe, c, ring, slot, [ps_w[:, b, 0], ps_w[:, b, 1]]).then_inc(s["gates"], 1)

            def out(d, t, slot):
                pe.wait_ge(ring.lo_made, t + 1)
                pe.wait_ge(s["m_lo"], d + 1)
                for e in range(DC):
                    for h in range(NH):
                        if e >= 2:
                            pe.wait_ge(s["added"], NO * d + NH * (e - 2) + h + 1)
                        hs, bank = slice(h * HALF, (h + 1) * HALF), ps_w[:, e % 2, h]
                        pe.matmul(bank, ring.hi[:, slot, e], m_hi[:, hs], start=True, stop=False)
                        pe.matmul(bank, ring.hi[:, slot, e], m_lo[:, hs], start=False, stop=False)
                        pe.matmul(bank, ring.lo[:, slot, e], m_hi[:, hs], start=False,
                                  stop=True).then_inc(s["out_ps"], 1)

            branches(0)
            gate(0, 0)
            gate(0, 1)
            branches(1)
            out(0, 4, 0)
            gate(1, 0)
            gate(1, 1)
            with pe.Fori(2, DC) as d:
                branches(d)
                out(d - 1, 4 * d, 0)
                gate(d, 0)
                gate(d, 1)
            out(DC - 1, 4 * DC - 1, 1)


def mixer(core, a):
    nc, c = core.nc, core
    with ExitStack() as ctx:
        SH = [P, HP, T]
        q_hi, qT = c.sb_shared(ctx, "oa", SH)
        with ExitStack() as dn:
            kT, vT = c.sb(dn, "kT", SH), c.sb(dn, "vT", SH)
            gc_beta = c.sb(dn, "gc_beta", [BETA_ROW + 2 * DN_HEADS, T])
            gc, beta = gc_beta[0:2 * DN_HEADS, :], gc_beta[BETA_ROW:, :]
            dn_project_phase(c, a, [qT, kT, vT], gc, beta)
            core.end_phase()
            dn_phase(c, [qT, kT, vT], gc, beta)
            core.end_phase()
        b_hi, obT = c.sb_shared(ctx, "ob", SH)
        attention_phase(c, a, obT)
        core.end_phase()
        a_lo, b_lo = c.sb(ctx, "oa_lo", SH, F32R), c.sb(ctx, "ob_lo", SH, F32R)
        branch_norm_phase(c, a, [qT, obT], [a_lo, b_lo], [q_hi, b_hi])
        core.end_phase()
        merge_phase(c, a, [q_hi, b_hi], [a_lo, b_lo])
        core.end_phase()


def build(nc, a, out):
    with ExitStack() as ctx:
        core = Core(nc, ctx)
        setup_phase(core, a)
        core.end_phase()
        ffn_phase(core, 0, a["ffn1_w_gate"], a["ffn1_w_up"], a["ffn1_w_down"])
        core.end_phase()
        mixer(core, a)
        ffn_phase(core, 2, a["ffn2_w_gate"], a["ffn2_w_up"], a["ffn2_w_down"])
        core.end_phase()
        output_phase(core, 3, out)
        core.end_phase()


_INS = ["x", "ffn1_norm", "ffn1_w_gate", "ffn1_w_up", "ffn1_w_down", "mix_norm", "w_in", "conv_qkv",
        "dn_a_log", "dn_dt_bias", "dn_out_norm", "diff_lambda_q1", "diff_lambda_k1", "diff_lambda_q2",
        "diff_lambda_k2", "diff_subln", "w_branch_a", "w_branch_b", "w_out", "ffn2_norm", "ffn2_w_gate",
        "ffn2_w_up", "ffn2_w_down", "final_norm"]


def kernel(**inputs):
    import numpy as np
    import concourse.bacc as bacc
    from concourse.bass_utils import run_bass_kernel_spmd

    nc = bacc.Bacc("TRN2", target_bir_lowering=False, num_devices=1)
    arrays, handles = {}, {}
    for name in _INS:
        arr = np.ascontiguousarray(inputs[name])
        arrays[f"in_{name}"] = arr
        handles[name] = nc.dram_tensor(f"in_{name}", arr.shape, mybir.dt.from_np(arr.dtype),
                                       kind="ExternalInput").ap()
    out = nc.dram_tensor("y_out", (1, T, D_MODEL), F32, kind="ExternalOutput").ap()
    build(nc, handles, out)
    res = run_bass_kernel_spmd(nc, [arrays], core_ids=[0])
    return res.results[0]["y_out"]
```
